# Optimizing a Trainium2 kernel written in Bass

```python
import functools
import jax, jax.numpy as jnp
from jax import lax
import numpy as np

D_MODEL = 2048
BATCH = 1
SEQ = 256
DEPTH = 2
DEC_BATCH = 8
DEC_SEQ = 1
PAST_LEN = 2048
PAGE_SIZE = 128

N_A_LAYERS = DEPTH // 2
N_B_LAYERS = DEPTH - N_A_LAYERS
RMS_EPS = 1e-6
D_POOL = D_MODEL
POOL_WINDOWS = (2, 4, 8, 16)
N_POOL_GROUPS = len(POOL_WINDOWS)
POOL_GROUP_DIM = D_POOL // N_POOL_GROUPS
POOL_STATE = max(POOL_WINDOWS) - 1
HEAD_DIM = 128
DIL_PATTERNS = ((128, 1), (512, 4), (2048, 16))
N_DIL_GROUPS = len(DIL_PATTERNS)
HEADS_PER_GROUP = D_MODEL // 256
N_KV_HEADS = HEADS_PER_GROUP // 2
KV_DIM = N_KV_HEADS * HEAD_DIM
DIL_BLOCK = 128
MAX_WINDOW = max(w for w, _ in DIL_PATTERNS)
N_MEM = 256
MEM_HEADS = 4
MEM_HEAD_DIM = 128
MEM_DIM = MEM_HEADS * MEM_HEAD_DIM
D_FF = -(-8 * D_MODEL // (3 * 256)) * 256

kernel_name = 'yoco_pool_dilated_mem_decoder_step'

def _rmsnorm(x, g):
    xf = x.astype(jnp.float32)
    y = xf * lax.rsqrt(jnp.mean(xf * xf, axis=-1, keepdims=True) + RMS_EPS)
    return (y * g.astype(jnp.float32)).astype(x.dtype)

def _swiglu(h, w_gate, w_up, w_down):
    return (jax.nn.silu(h @ w_gate) * (h @ w_up)) @ w_down

def _pool_mix(u_ext, n_q, w_group, scale):
    n, length, _ = u_ext.shape
    uf = u_ext.astype(jnp.float32)
    cs = jnp.concatenate([jnp.zeros((n, 1, D_POOL), jnp.float32), jnp.cumsum(uf, axis=1)], axis=1)
    e = jnp.arange(length - n_q, length)
    hi = jnp.take(cs, e + 1, axis=1)
    u_q = uf[:, length - n_q:]
    parts = []
    for g, w in enumerate(POOL_WINDOWS):
        sl = slice(g * POOL_GROUP_DIM, (g + 1) * POOL_GROUP_DIM)
        lo = jnp.take(cs[:, :, sl], jnp.maximum(e + 1 - w, 0), axis=1)
        cnt = jnp.minimum(e + 1, w).astype(jnp.float32)[None, :, None]
        parts.append((hi[:, :, sl] - lo) / cnt - u_q[:, :, sl])
    p = jnp.stack(parts, axis=2).astype(u_ext.dtype)
    z = jnp.einsum('nlgc,gcd->nlgd', p, w_group).reshape(n, n_q, D_POOL)
    return z * scale

def _dilated_prompt(q, window, dil, k, v):
    n, s, h, dh = q.shape
    rep = h // N_KV_HEADS
    span = dil * DIL_BLOCK
    s_pad = -(-s // span) * span
    nb = s_pad // span
    padw = ((0, 0), (0, s_pad - s), (0, 0), (0, 0))
    qb = jnp.pad(q, padw).reshape(n, nb, DIL_BLOCK, dil, N_KV_HEADS, rep, dh)
    kb = jnp.pad(k, padw).reshape(n, nb, DIL_BLOCK, dil, N_KV_HEADS, dh)
    vb = jnp.pad(v, padw).reshape(n, nb, DIL_BLOCK, dil, N_KV_HEADS, dh)

    def band(t):
        prev = jnp.concatenate([jnp.zeros_like(t[:, :1]), t[:, :-1]], axis=1)
        return jnp.concatenate([prev, t], axis=2)

    kk, vv = band(kb), band(vb)
    sc = jnp.einsum('nbqrkgd,nbjrkd->nbrkgqj', qb, kk).astype(jnp.float32) * (dh ** -0.5)
    qi = jnp.arange(DIL_BLOCK)[:, None]
    kj = jnp.arange(2 * DIL_BLOCK)[None, :]
    dist = qi + DIL_BLOCK - kj
    blk = jnp.arange(nb)[:, None, None]
    valid = (dist >= 0) & (dist <= window // dil) & ((blk > 0) | (kj >= DIL_BLOCK))
    sc = jnp.where(valid[None, :, None, None, None], sc, -jnp.inf)
    m = jnp.max(sc, axis=-1, keepdims=True)
    pr = jnp.exp(sc - m)
    den = jnp.sum(pr, axis=-1, keepdims=True)
    o = jnp.einsum('nbrkgqj,nbjrkd->nbqrkgd', (pr / den).astype(v.dtype), vv)
    o = o.reshape(n, s_pad, h, dh)[:, :s]
    lse = (m + jnp.log(den))[..., 0].transpose(0, 1, 5, 2, 3, 4).reshape(n, s_pad, h)[:, :s]
    return o, lse

def _dilated_sample(q, window, dil, k_ext, v_ext):
    n, t, h, dh = q.shape
    rep = h // N_KV_HEADS
    lx = k_ext.shape[1]
    nk = window // dil
    idx = (lx - t) + jnp.arange(t)[:, None] - dil * jnp.arange(nk + 1)[None, :]
    valid = idx >= 0
    idc = jnp.maximum(idx, 0)
    kg = jnp.take(k_ext, idc, axis=1)
    vg = jnp.take(v_ext, idc, axis=1)
    qg = q.reshape(n, t, N_KV_HEADS, rep, dh)
    sc = jnp.einsum('ntkgd,ntjkd->ntkgj', qg, kg).astype(jnp.float32) * (dh ** -0.5)
    sc = jnp.where(valid[None, :, None, None, :], sc, -jnp.inf)
    m = jnp.max(sc, axis=-1, keepdims=True)
    pr = jnp.exp(sc - m)
    den = jnp.sum(pr, axis=-1, keepdims=True)
    o = jnp.einsum('ntkgj,ntjkd->ntkgd', (pr / den).astype(v_ext.dtype), vg).reshape(n, t, h, dh)
    lse = (m + jnp.log(den))[..., 0].reshape(n, t, h)
    return o, lse

def _dilated_mix(h, w_q, w_o, attend):
    n, length, _ = h.shape
    q = (h @ w_q).reshape(n, length, N_DIL_GROUPS, HEADS_PER_GROUP, HEAD_DIM)
    outs, lses = [], []
    for g, (w, d) in enumerate(DIL_PATTERNS):
        o, lse = attend(q[:, :, g], w, d)
        outs.append(o.astype(jnp.float32))
        lses.append(lse)
    wts = jax.nn.softmax(jnp.stack(lses), axis=0)[..., None]
    o = jnp.sum(wts * jnp.stack(outs), axis=0).astype(h.dtype)
    return o.reshape(n, length, HEADS_PER_GROUP * HEAD_DIM) @ w_o

def _mem_kv(mem, g, w_k, w_v):
    n, m, _ = mem.shape
    hm = _rmsnorm(mem, g)
    return ((hm @ w_k).reshape(n, m, MEM_HEADS, MEM_HEAD_DIM),
            (hm @ w_v).reshape(n, m, MEM_HEADS, MEM_HEAD_DIM))

def _mem_attend(h, mk, mv, w_q, w_o):
    n, length, _ = h.shape
    q = (h @ w_q).reshape(n, length, MEM_HEADS, MEM_HEAD_DIM)
    sc = jnp.einsum('nlhd,nmhd->nhlm', q, mk).astype(jnp.float32) * (MEM_HEAD_DIM ** -0.5)
    p = jax.nn.softmax(sc, axis=-1).astype(mv.dtype)
    o = jnp.einsum('nhlm,nmhd->nlhd', p, mv).reshape(n, length, MEM_DIM)
    return o @ w_o

def setup_inputs(seed: int = 0) -> dict:
    key = jax.random.key(seed)
    ks = jax.random.split(key, 32)
    f32 = jnp.float32
    w_buf = min(MAX_WINDOW, PAST_LEN)

    def normal(k, shape):
        return jax.random.normal(k, shape, f32)

    def dense(k, shape, fan_in):
        return jax.random.normal(k, shape, f32) * (fan_in ** -0.5)

    def gain(k, shape):
        return 1.0 + 0.02 * jax.random.normal(k, shape, f32)

    return {
        'x_prompt': normal(ks[0], (BATCH, SEQ, D_MODEL)),
        'x_sample': normal(ks[1], (DEC_BATCH, DEC_SEQ, D_MODEL)),
        'mem_prompt': normal(ks[2], (BATCH, N_MEM, D_MODEL)),
        'state_pool': normal(ks[3], (N_A_LAYERS, DEC_BATCH, POOL_STATE, D_POOL)),
        'cache_win_k': normal(ks[4], (DEC_BATCH, w_buf, N_KV_HEADS, HEAD_DIM)),
        'cache_win_v': normal(ks[5], (DEC_BATCH, w_buf, N_KV_HEADS, HEAD_DIM)),
        'cache_mem_k': normal(ks[6], (DEPTH, DEC_BATCH, N_MEM, MEM_HEADS, MEM_HEAD_DIM)),
        'cache_mem_v': normal(ks[7], (DEPTH, DEC_BATCH, N_MEM, MEM_HEADS, MEM_HEAD_DIM)),
        'norm_mix': gain(ks[8], (DEPTH, D_MODEL)),
        'norm_mem_q': gain(ks[9], (DEPTH, D_MODEL)),
        'norm_mem_kv': gain(ks[10], (DEPTH, D_MODEL)),
        'norm_ffn': gain(ks[11], (DEPTH, D_MODEL)),
        'pool_w_in': dense(ks[12], (N_A_LAYERS, D_MODEL, D_POOL), D_MODEL),
        'pool_w_group': dense(ks[13], (N_A_LAYERS, N_POOL_GROUPS, POOL_GROUP_DIM, POOL_GROUP_DIM), POOL_GROUP_DIM),
        'pool_scale': 1.0 + 0.1 * normal(ks[14], (N_A_LAYERS, D_POOL)),
        'pool_w_out': dense(ks[15], (N_A_LAYERS, D_POOL, D_MODEL), D_POOL),
        'norm_kv': gain(ks[16], (D_MODEL,)),
        'w_k_shared': dense(ks[17], (D_MODEL, KV_DIM), D_MODEL),
        'w_v_shared': dense(ks[18], (D_MODEL, KV_DIM), D_MODEL),
        'dil_w_q': dense(ks[19], (N_B_LAYERS, D_MODEL, N_DIL_GROUPS * HEADS_PER_GROUP * HEAD_DIM), D_MODEL),
        'dil_w_o': dense(ks[20], (N_B_LAYERS, HEADS_PER_GROUP * HEAD_DIM, D_MODEL), HEADS_PER_GROUP * HEAD_DIM),
        'mem_w_q': dense(ks[21], (DEPTH, D_MODEL, MEM_DIM), D_MODEL),
        'mem_w_k': dense(ks[22], (DEPTH, D_MODEL, MEM_DIM), D_MODEL),
        'mem_w_v': dense(ks[23], (DEPTH, D_MODEL, MEM_DIM), D_MODEL),
        'mem_w_o': dense(ks[24], (DEPTH, MEM_DIM, D_MODEL), MEM_DIM),
        'ffn_w_gate': dense(ks[25], (DEPTH, D_MODEL, D_FF), D_MODEL),
        'ffn_w_up': dense(ks[26], (DEPTH, D_MODEL, D_FF), D_MODEL),
        'ffn_w_down': dense(ks[27], (DEPTH, D_FF, D_MODEL), D_FF),
        'norm_final': gain(ks[28], (D_MODEL,)),
    }

def reference(x_prompt, x_sample, mem_prompt, state_pool, cache_win_k, cache_win_v, cache_mem_k, cache_mem_v,
              norm_mix, norm_mem_q, norm_mem_kv, norm_ffn, pool_w_in, pool_w_group, pool_scale, pool_w_out,
              norm_kv, w_k_shared, w_v_shared, dil_w_q, dil_w_o, mem_w_q, mem_w_k, mem_w_v, mem_w_o,
              ffn_w_gate, ffn_w_up, ffn_w_down, norm_final):

    def trunk(x, mem_k, mem_v, pool_buf, win_k, win_v):
        n, t, _ = x.shape
        new_pool = []
        k_new = v_new = None
        attend = None
        for l in range(DEPTH):
            if l == N_A_LAYERS:
                hkv = _rmsnorm(x, norm_kv)
                k_new = (hkv @ w_k_shared).reshape(n, t, N_KV_HEADS, HEAD_DIM)
                v_new = (hkv @ w_v_shared).reshape(n, t, N_KV_HEADS, HEAD_DIM)
                if win_k is None:
                    attend = functools.partial(_dilated_prompt, k=k_new, v=v_new)
                else:
                    attend = functools.partial(_dilated_sample,
                                               k_ext=jnp.concatenate([win_k, k_new], axis=1),
                                               v_ext=jnp.concatenate([win_v, v_new], axis=1))
            h = _rmsnorm(x, norm_mix[l])
            if l < N_A_LAYERS:
                u = h @ pool_w_in[l]
                u_ext = u if pool_buf is None else jnp.concatenate([pool_buf[l], u], axis=1)
                new_pool.append(u_ext[:, -POOL_STATE:])
                x = x + _pool_mix(u_ext, t, pool_w_group[l], pool_scale[l]) @ pool_w_out[l]
            else:
                j = l - N_A_LAYERS
                x = x + _dilated_mix(h, dil_w_q[j], dil_w_o[j], attend)
            x = x + _mem_attend(_rmsnorm(x, norm_mem_q[l]), mem_k[l], mem_v[l], mem_w_q[l], mem_w_o[l])
            x = x + _swiglu(_rmsnorm(x, norm_ffn[l]), ffn_w_gate[l], ffn_w_up[l], ffn_w_down[l])
        return _rmsnorm(x, norm_final), jnp.stack(new_pool), k_new, v_new

    mkv = [_mem_kv(mem_prompt, norm_mem_kv[l], mem_w_k[l], mem_w_v[l]) for l in range(DEPTH)]
    mem_k_p = jnp.stack([a for a, _ in mkv])
    mem_v_p = jnp.stack([b for _, b in mkv])

    y_prompt, pool_p, k_p, v_p = trunk(x_prompt, mem_k_p, mem_v_p, None, None, None)
    y_sample, pool_s, k_s, v_s = trunk(x_sample, cache_mem_k, cache_mem_v, state_pool, cache_win_k, cache_win_v)

    keep_from = max(0, k_p.shape[1] - MAX_WINDOW)
    win_k_p = k_p[:, keep_from:]
    win_v_p = v_p[:, keep_from:]
    return (y_prompt, y_sample, pool_p, pool_s, win_k_p, win_v_p, k_s, v_s, mem_k_p, mem_v_p)


_drawn_inputs = setup_inputs


def setup_inputs(seed=0):
    import zlib

    import numpy as np

    out = dict(_drawn_inputs(seed))
    spreads = {}
    factors = {'norm_mix': 2.853,
     'norm_mem_q': 8.0,
     'norm_mem_kv': 2.842,
     'norm_ffn': 3.447,
     'norm_kv': 2.879,
     'norm_final': 2.711}
    for name, (base, spread) in spreads.items():
        noise = np.random.default_rng([zlib.crc32(name.encode()), seed]).standard_normal(out[name].shape)
        drawn = base * np.exp(spread * noise) if base else spread * noise
        out[name] = __import__('jax').numpy.asarray(drawn.astype(out[name].dtype))
    for name, factor in factors.items():
        out[name] = (out[name] * factor).astype(out[name].dtype)
    return out
```

```python
from contextlib import ExitStack

import numpy as np

import concourse.bass as bass
from concourse import mybir

F32 = mybir.dt.float32
F32R = mybir.dt.float32r
ALU = mybir.AluOpType
ACT = mybir.ActivationFunctionType
AX = mybir.AxisListType

P = 128
D = 2048
DC = D // P
TP = 256
TS = 8
T = TP + TS
FF = 5632
FC = FF // P
MEMD = 512
NH_MEM = 4
KVH = 4
NG = 3
NH = 8
DILS = (1, 4, 16)
PAST = 2048
WIN_KEYS = 128
NST = 15
EPS = 1e-6
SCALE = float(P) ** -0.5
MASKED = -1e30
BLK = 2048
NSPLIT = 4
PARTS = (16, 16, 12)
GAIN = {"memkv": (0, 16), "mix": (32, 48), "memq": (64, 80), "ffn": (96, 112), "kv": (128,), "final": (144,),
        "scale": (160,)}

PHASES = [
    ("xload", 0, 1),
    ("memload", 0, 4),
    ("memk0", 4, 2), ("memv0", 4, 1), ("memkt0", 0, 1),
    ("memk1", 4, 2), ("xt", 0, 5), ("st", 0, 2), ("memv1", 4, 1), ("memkt1", 0, 1),
    ("win", 16, 8), ("ut", 0, 2), ("grp", 4, 8), ("wout", 16, 8),
    ("mq0", 4, 2), ("mk0", 0, 8), ("mo0", 4, 8),
    ("f0g0", 32, 16), ("f0d0", 16, 8), ("f0g1", 32, 16), ("f0d1", 16, 8), ("f0g2", 24, 12), ("f0d2", 12, 8),
    ("ksh", 4, 2), ("vsh", 4, 2), ("kt", 0, 2),
    ("dq", 24, 12), ("dk", 0, 16), ("do", 8, 8),
    ("mq1", 4, 2), ("mk1", 0, 8), ("mo1", 4, 8),
    ("f1g0", 32, 16), ("f1d0", 16, 8), ("f1g1", 32, 16), ("f1d1", 16, 8), ("f1g2", 24, 12), ("f1d2", 12, 8),
    ("y", 0, 6),
]
N0, G0 = {}, {}
_n = _g = 0
for _name, _nb, _ni in PHASES:
    N0[_name], G0[_name] = _n, _g
    _n += _nb
    _g += _ni
NBLOCKS = _n

RAW = [("s", "mem", 0), ("s", "mem", 1)]
RAW += [("w", n) for n in range(N0["memk0"], N0["memk1"] + 4)]
RAW += [("s", "x", i) for i in range(3)] + [("s", "state", 0)]
RAW += [("w", n) for n in range(N0["memv1"], N0["mo0"] + 4)]
RAW += [("s", "mk0", i) for i in range(4)] + [("s", "mv0", i) for i in range(4)]
RAW += [("w", n) for n in range(N0["mo0"] + 4, N0["do"] + 4)]
RAW += [("s", "dk", i) for i in range(8)] + [("s", "dv", i) for i in range(8)]
RAW += [("w", n) for n in range(N0["do"] + 4, N0["mo1"] + 4)]
RAW += [("s", "mk1", i) for i in range(4)] + [("s", "mv1", i) for i in range(4)]
RAW += [("w", n) for n in range(N0["mo1"] + 4, NBLOCKS)]
RAW_OF = {k: r for r, k in enumerate(RAW)}

TURN0, _t = {}, 0
for _name, _nb, _ni in PHASES:
    if _nb == 0:
        TURN0[_name] = _t
        _t += _ni
ROWS_DONE, _v = {}, 0
for _k in RAW:
    if _k[0] == "s":
        kind, i = _k[1], _k[2]
        if kind == "mem":
            ROWS_DONE[_k] = ("t", TURN0["memload"] + 2 * (i + 1))
        elif kind == "x":
            ROWS_DONE[_k] = ("t", TURN0["xt"] + (2, 4, 5)[i])
        elif kind == "state":
            ROWS_DONE[_k] = ("t", TURN0["st"] + 2)
        elif kind in ("mk0", "mk1", "dk"):
            ROWS_DONE[_k] = ("t", TURN0[kind] + (2 if kind == "dk" else 2) * (i + 1))
        else:
            _v += 1
            ROWS_DONE[_k] = ("v", _v)
LAND, _c = {}, [0, 0]
for _r, _k in enumerate(RAW):
    _c[_r % 2] += 48 if _k[1] in ("dk", "dv") else 16
    LAND[_k] = _c[_r % 2]

H0 = {"p": 0, "z": 8, "m0": 16, "f0": 21, "dil": 43, "m1": 52, "f1": 57}
GEN = {"memkv0": 0, "memkv1": 1, "mix0": 2, "memq0": 3, "ffn0": 4, "kv": 5, "mix1": 6, "memq1": 7, "ffn1": 8}
E0 = {"m0": 0, "dil": NH_MEM + 1, "m1": NH_MEM + 1 + NH + 1}
SC0 = {"m0": 0, "dil": TS, "m1": 2 * TS}
VU0 = {"m0": 0, "dil": TS // 2, "m1": TS // 2 + TS}
STORED = [16, 16, 48, 48, 64, 64]
CONSTS = 16 * 9
STAT = {"mem": 1, "mix0": 2, "memq0": 3, "ffn0": 4, "kv": 5, "memq1": 6, "ffn1": 7, "final": 8}


def trunk(nc, a, o):
    (y_p, y_s, pool_p, pool_s, wk_p, wv_p, k_s, v_s, mem_k_p, mem_v_p) = o
    ctx = ExitStack()
    with ctx:
        def sb(name, shape, dt=F32):
            return ctx.enter_context(nc.sbuf_tensor(name, shape, dt))

        def sem(name):
            return ctx.enter_context(nc.semaphore(name))

        raw = sb("raw", [P, 2, BLK])
        whi = sb("whi", [P, NSPLIT, BLK], F32R)
        wlo = sb("wlo", [P, NSPLIT, BLK], F32R)
        x = sb("x", [P, DC, T])
        xs = sb("xs", [P, DC, 2, T], F32R)
        hA = sb("hA", [P, 8, 2, T], F32R)
        with nc.sbuf_tensor("hB", [P, 8, 2, T], F32R) as hB:
            pass
        att = sb("att", [P, 16 * T])
        mKT = sb("mKT", [P, 2, NH_MEM, TP])
        mV = sb("mV", [P, 2, 2, MEMD])
        KT = sb("KT", [P, KVH, T])
        V = sb("V", [P, 2, MEMD])
        mask = sb("mask", [P, NG, 2 * P])
        ident = sb("ident", [P, P])
        ones = sb("ones", [P, P])
        gains = sb("gains", [P, 176])
        R = sb("R", [P, T])
        Rc = sb("Rc", [P, 3])
        ssq = sb("ssq", [P, 2, T])
        eps = sb("eps", [P, 1])
        small = sb("small", [P, 32])
        tmp = sb("tmp", [P, 2360])
        qd = att[:, 0:12 * T].rearrange("p (a g h t) -> p a g h t", a=2, g=NG, h=2)
        qm = att[:, 0:4 * T].rearrange("p (h t) -> p h t", h=NH_MEM)
        KTb = att[:, 0:2 * 12 * 129].rearrange("p (a k j) -> p a k j", a=2, k=12)
        KTm = att[:, 4 * T:4 * T + 2048].rearrange("p (a h j) -> p a h j", a=2, h=NH_MEM)
        QzD = att[:, 3168:3936].rearrange("p (g b k h) -> p g b k h", g=NG, b=TS, k=KVH)
        QzM = att[:, 3936:4064].rearrange("p (b h c) -> p b h c", b=TS, h=NH_MEM)
        gateF = tmp[:, 0:2 * T].rearrange("p (m t) -> p m t", m=2)
        siluF = tmp[:, 2 * T:4 * T].rearrange("p (m t) -> p m t", m=2)
        upF = tmp[:, 4 * T:6 * T].rearrange("p (m t) -> p m t", m=2)
        UP = TP + 16
        U, Ta, Tb = (tmp[:, i * 2 * UP:(i + 1) * 2 * UP].rearrange("p (m t) -> p m t", m=2) for i in range(3))
        wsum = tmp[:, 6 * UP:6 * UP + 128].rearrange("p (m b) -> p m b", m=DC)
        ut = tmp[:, 6 * UP + 128:6 * UP + 128 + DC * 23].rearrange("p (m t) -> p m t", m=DC)
        usm = tmp[:, 2200:2216].rearrange("p (m b) -> p m b", m=2)
        us2 = tmp[:, 2216:2232].rearrange("p (m b) -> p m b", m=2)
        invc = tmp[:, 2232:2296].rearrange("p (g t) -> p g t", g=4)
        stage = att[:, 0:1024]
        stage2 = att[:, 1024:2048]
        stage_u = tmp[:, 0:1024]
        gain_rows = att[:, 2048:2304]
        Vsm = att[0:TS, 2304:2816]
        S = tmp[:, 0:1152]
        Pn = tmp[:, 1152:1536]
        PT = tmp[:, 1536:1920]
        Pm = tmp[:, 0:1024].rearrange("p (a q j) -> p a q j", a=2, q=2)
        PTm = tmp[:, 1024:1536].rearrange("p (k t) -> p k t", k=2)
        PsD = tmp[:, 0:774].rearrange("p (b g j) -> p b g j", b=2, g=NG)
        PsDf = tmp[:, 0:774].rearrange("p (b j) -> p b j", b=2)
        PsM = tmp[:, 0:512].rearrange("p (b j) -> p b j", b=2)
        PTzD = tmp[:, 776:1544].rearrange("p (g b k h) -> p g b k h", g=NG, b=TS, k=KVH)
        PTzM = tmp[:, 1808:2064].rearrange("p (k b h c) -> p k b h c", k=2, b=TS, h=NH_MEM)
        Os = tmp[:, 1552:1808].rearrange("p (b d) -> p b d", b=2)
        Vrep = tmp[:, 2064:2320].rearrange("p (b d) -> p b d", b=2)
        std = sb("std", [P, T])
        stdc = sb("stdc", [P, 3])
        sq = sb("sq", [P, 2, T])

        acc = ctx.enter_context(nc.psum_tensor("acc", [P, 4, 512], F32))
        ab = ctx.enter_context(nc.psum_tensor("ab", [P, 4, 512], F32))

        consts_in, mask_in = sem("consts_in"), sem("mask_in")
        raw_in = [sem("raw_in0"), sem("raw_in1")]
        hi_ready, lo_ready = sem("hi_ready"), sem("lo_ready")
        half_used = sem("half_used")
        turned = sem("turned")
        acc_free = sem("acc_free")
        xs_ready = sem("xs_ready")
        h_ready = sem("h_ready")
        ssq_ready, stat_ready, std_ready = sem("ssq_ready"), sem("stat_ready"), sem("std_ready")
        silu_ready = sem("silu_ready")
        zeros_ready = sem("zeros_ready")
        s_ready, s_free = sem("s_ready"), sem("s_free")
        nb_ready, e_ready, p_ready = sem("nb_ready"), sem("e_ready"), sem("p_ready")
        t_ready, pt_ready = sem("t_ready"), sem("pt_ready")
        o_ready, os_ready = sem("o_ready"), sem("os_ready")
        scored = sem("scored")
        v_used = sem("v_used")
        y_ready = sem("y_ready")
        stored = [sem("stored0"), sem("stored1")]
        out_done = sem("out_done")
        vs_done = sem("vs_done")
        vrep_in = sem("vrep_in")

        def counter():
            seen = {}

            def following(eng, which):
                seen[which.name] = seen.get(which.name, 0) + 1
                eng.wait_ge(which, seen[which.name])
            return following

        def kcols(w, k0, nk, c0, nco):
            return w[k0 * P:(k0 + nk) * P, c0:c0 + nco].rearrange("(k p) c -> p k c", p=P)

        def pair_block(w, j, i):
            return kcols(w, 8 * i, 8, 256 * j, 256)

        def quad_block(w, i, k0=0):
            return kcols(w, k0, 4, 512 * i, 512)

        def weight_source(n):
            name = [p for p, nb, _ in PHASES if nb and N0[p] <= n][-1]
            i = n - N0[name]
            if name[:4] == "memk":
                return pair_block(a["mem_w_k"][int(name[4])], i // 2, i % 2)
            if name[:4] == "memv":
                return kcols(a["mem_w_v"][int(name[4])], 4 * i, 4, 0, 512)
            if name == "win":
                return pair_block(a["pool_w_in"][0], i // 2, i % 2)
            if name == "grp":
                return a["pool_w_group"][0, i].rearrange("(k p) c -> p k c", p=P)
            if name == "wout":
                return pair_block(a["pool_w_out"][0], i // 2, i % 2)
            if name[:2] == "mq":
                return pair_block(a["mem_w_q"][int(name[2])], i // 2, i % 2)
            if name[:2] == "mo":
                return quad_block(a["mem_w_o"][int(name[2])], i)
            if name == "ksh":
                return pair_block(a["w_k_shared"], i // 2, i % 2)
            if name == "vsh":
                return kcols(a["w_v_shared"], 4 * i, 4, 0, 512)
            if name == "dq":
                hp, g = divmod(i // 2, NG)
                return kcols(a["dil_w_q"][0], 8 * (i % 2), 8, (g * NH + 2 * hp) * P, 256)
            if name == "do":
                return kcols(a["dil_w_o"][0], 0, 8, 256 * i, 256)
            layer, kind, part = int(name[1]), name[2], int(name[3])
            f0 = sum(PARTS[:part])
            if kind == "g":
                w = a["ffn_w_gate"] if i % 4 < 2 else a["ffn_w_up"]
                return kcols(w[layer], 8 * (i % 2), 8, (f0 + 2 * (i // 4)) * P, 256)
            if part < 2:
                return kcols(a["ffn_w_down"][layer], f0 + 8 * (i % 2), 8, 256 * (i // 2), 256)
            return kcols(a["ffn_w_down"][layer], f0 + 4 * (i % 3), 4, 512 * (i // 3), 512)

        def raw_as(slot, nk):
            return raw[:, slot, :].rearrange("p (k c) -> p k c", k=nk)

        def load_rows(eng, key):
            r = RAW_OF[key]
            _, kind, i = key
            s, done = r % 2, raw_in[r % 2]
            if kind == "mem":
                eng.dma_start(raw[:, s, :], a["mem_prompt"][0, i * P:(i + 1) * P, :]).then_inc(done, 16)
            elif kind == "x":
                if i < 2:
                    eng.dma_start(raw[:, s, :], a["x_prompt"][0, i * P:(i + 1) * P, :]).then_inc(done, 16)
                else:
                    eng.dma_start(raw[0:TS, s, :], a["x_sample"][:, 0, :]).then_inc(done, 16)
            elif kind == "state":
                eng.dma_start(raw[0:TS * NST, s, :], a["state_pool"][0].rearrange("b t c -> (b t) c")).then_inc(done, 16)
            elif kind[:2] in ("mk", "mv"):
                src = a["cache_mem_k" if kind[1] == "k" else "cache_mem_v"][int(kind[2]), 2 * i:2 * i + 2]
                eng.dma_start(raw[:, s, :].rearrange("p (b k c) -> p b k c", b=2, k=2),
                              src.rearrange("b (k p) h d -> p b k (h d)", p=P)).then_inc(done, 16)
            else:
                src = a["cache_win_k" if kind == "dk" else "cache_win_v"][i].rearrange("t h d -> t (h d)")
                for g, d in enumerate(DILS):
                    rows = src[PAST - WIN_KEYS * d:PAST, :].rearrange("(p q) c -> p q c", q=d)[:, 0, :]
                    eng.dma_start(raw[:, s, g * MEMD:(g + 1) * MEMD], rows).then_inc(done, 16)

        def landed(eng, key):
            eng.wait_ge(raw_in[RAW_OF[key] % 2], LAND[key])

        def slot(key):
            return raw[:, RAW_OF[key] % 2, :]

        block = ctx.enter_context(nc.Block())

        @block.sync
        def _(eng):
            def slot_free(r):
                if r >= 2:
                    old = RAW[r - 2]
                    if old[0] == "w":
                        eng.wait_ge(hi_ready, old[1] + 1)
                        eng.wait_ge(lo_ready, old[1] + 1)
                    else:
                        by, count = ROWS_DONE[old]
                        eng.wait_ge(turned if by == "t" else v_used, count)

            def load_block(n):
                r = RAW_OF[("w", n)]
                src = weight_source(n)
                slot_free(r)
                eng.dma_start(raw_as(r % 2, src.shape[1]), src).then_inc(raw_in[r % 2], 16)

            def loop_blocks(name, skip, turns, per, source):
                with eng.Fori(skip, turns) as i:
                    for j in range(per):
                        r = RAW_OF[("w", N0[name] + j)]
                        n = N0[name] + j - 2
                        eng.wait_ge(hi_ready, per * i + (n + 1))
                        eng.wait_ge(lo_ready, per * i + (n + 1))
                        src = source(i, j)
                        eng.dma_start(raw_as(r % 2, src.shape[1]), src).then_inc(raw_in[r % 2], 16)

            def cols(w, k0, nk, c):
                return w[k0 * P:(k0 + nk) * P, bass.ds(c, 256)].rearrange("(k p) c -> p k c", p=P)

            for j, name in enumerate(("norm_mem_kv", "norm_mix", "norm_mem_q", "norm_ffn")):
                eng.dma_start(gain_rows[32 * j:32 * (j + 1), 0:P], a[name].rearrange("l (m p) -> (l m) p", p=P)).then_inc(consts_in, 16)
            for j, name in enumerate(("norm_kv", "norm_final")):
                eng.dma_start(gain_rows[16 * j:16 * (j + 1), P:2 * P], a[name].rearrange("(m p) -> m p", p=P)).then_inc(consts_in, 16)
            eng.dma_start(gain_rows[32:48, P:2 * P], a["pool_scale"].rearrange("l (m p) -> (l m) p", p=P)).then_inc(consts_in, 16)
            eng.dma_start(ident[:, :], a["c_ident"]).then_inc(consts_in, 16)
            eng.dma_start(invc, a["c_inv"]).then_inc(consts_in, 16)

            in_loop = {}
            for l in range(2):
                for part in range(3):
                    in_loop[f"f{l}g{part}"] = (PARTS[part] // 2, 4)
                    if part < 2:
                        in_loop[f"f{l}d{part}"] = (4, 4)
            r = 0
            while r < len(RAW):
                key = RAW[r]
                if key[0] == "s":
                    slot_free(r)
                    load_rows(eng, key)
                    r += 1
                    continue
                n = key[1]
                name = [p for p, nb, _ in PHASES if nb and N0[p] <= n][-1]
                if name in in_loop and n == N0[name]:
                    turns, per = in_loop[name]
                    l, part = int(name[1]), int(name[3])
                    f0 = sum(PARTS[:part])
                    skip = 0
                    if name[2:4] == "g0":
                        for j in range(per):
                            load_block(n + j)
                        skip = 1
                    if name[2] == "g":
                        loop_blocks(name, skip, turns, per, lambda i, j: cols(
                            a["ffn_w_gate" if j < 2 else "ffn_w_up"][l], 8 * (j % 2), 8, i * 256 + f0 * P))
                    else:
                        loop_blocks(name, skip, turns, per, lambda i, j: cols(
                            a["ffn_w_down"][l], f0 + 8 * (j % 2), 8, i * 512 + 256 * (j // 2)))
                    r += turns * per
                    continue
                load_block(n)
                r += 1

        @block.scalar
        def _(eng):
            at = [0]
            following = counter()

            def hi(n, more=0):
                r = RAW_OF[("w", n)]
                eng.wait_ge(raw_in[r % 2], more * 8 + LAND[("w", n)])
                if n >= NSPLIT:
                    eng.wait_ge(half_used, more * 2 + 2 * (n - NSPLIT + 1))
                nc.scalar.activation(whi[:, n % NSPLIT, :], raw[:, r % 2, :], ACT.Copy).then_inc(hi_ready, 1)

            def upto(n):
                while at[0] <= min(n, NBLOCKS - 1):
                    hi(at[0])
                    at[0] += 1

            def root(k, width=T, cols=0):
                eng.wait_ge(stat_ready, k)
                last = nc.scalar.activation(std[:, 0:width], ab[:, 3, 0:width], ACT.Sqrt, bias=eps[:, :], scale=1.0 / D)
                if cols:
                    last = nc.scalar.activation(stdc[:, 0:2], ab[:, 3, 300:302], ACT.Sqrt, bias=eps[:, :], scale=1.0 / D)
                if cols == 3:
                    last = nc.scalar.activation(stdc[0:TS, 2:3], ab[0:TS, 3, 302:303], ACT.Sqrt, bias=eps[0:TS, :],
                                                scale=1.0 / D)
                last.then_inc(std_ready, 1)

            def softmax_exp(parts):
                following(eng, nb_ready)
                for out, in_, b, d in parts:
                    last = nc.scalar.activation(out, in_, ACT.Exp, bias=small[:, b:b + 1], scale=SCALE,
                                                accum_out=small[:, d:d + 1])
                last.then_inc(e_ready, 1)

            def mem_attention(l):
                upto(N0[f"mo{l}"] + 3)
                for h in range(NH_MEM):
                    s = h % 2
                    softmax_exp([(Pm[:, s, q, :], ab[:, s, q * TP:(q + 1) * TP], 2 * s + q, 4 + 2 * s + q)
                                 for q in range(2)])
                softmax_exp([(PsM[:, b, :], ab[:, 0, b * TP:(b + 1) * TP], 16 + b, 20 + b) for b in range(2)])

            def ffn(l):
                for part in range(3):
                    n, g, turns = N0[f"f{l}g{part}"], G0[f"f{l}g{part}"], PARTS[part] // 2

                    def turn(i):
                        hi(n + 2, 4 * i)
                        if part == 0 and isinstance(i, int):
                            root(STAT[f"ffn{l}"])
                            nc.scalar.preload_act_table(ACT.Silu)
                        hi(n + 3, 4 * i)
                        eng.wait_ge(acc_free, 2 * i + (g + 1))
                        nc.scalar.activation(siluF, gateF, ACT.Silu).then_inc(silu_ready, 1)
                        hi(n + 4, 4 * i)
                        hi(n + 5, 4 * i)

                    upto(n + 1)
                    if part == 0:
                        turn(0)
                    with eng.Fori(1 if part == 0 else 0, turns) as i:
                        turn(i)
                    if part < 2:
                        nd = N0[f"f{l}d{part}"]
                        with eng.Fori(0, 4) as i:
                            for j in range(4):
                                hi(nd + 2 + j, 4 * i)
                        at[0] = nd + 18
                    else:
                        at[0] = n + 4 * turns + 2

            eng.dma_start(mask[:, :, :], a["c_mask"]).then_inc(mask_in, 16)
            eng.wait_ge(zeros_ready, 1)
            upto(N0["memk0"] + 2)
            root(STAT["mem"], TP, 2)
            upto(N0["win"] + 2)
            root(STAT["mix0"])
            upto(N0["mq0"] + 2)
            root(STAT["memq0"])
            mem_attention(0)
            ffn(0)
            upto(N0["ksh"] + 2)
            root(STAT["kv"], T, 3)
            dil = [(S[:, 0:768], S[:, 0:768], 0, 4), (S[:, 768:1152], S[:, 768:1152], 1, 5)]
            for hp in range(4):
                for j in range(6):
                    upto(N0["dq"] + 6 * hp + j + 2)
                    if hp and j in (0, 2):
                        softmax_exp(dil)
            upto(N0["do"] + 3)
            softmax_exp(dil)
            softmax_exp(dil)
            softmax_exp([(PsDf[:, b, :], ab[:, b, 0:387], 16 + b, 20 + b) for b in range(2)])
            upto(N0["mq1"] + 2)
            root(STAT["memq1"])
            mem_attention(1)
            ffn(1)
            upto(NBLOCKS - 1)
            root(STAT["final"])

        @block.tensor
        def _(eng):
            mm = nc.tensor.matmul
            following = counter()

            def block_ready(n, more=0):
                eng.wait_ge(hi_ready, more + (n + 1))
                eng.wait_ge(lo_ready, more + (n + 1))

            def item_free(g, more=0):
                if g >= 2:
                    eng.wait_ge(acc_free, more + (g - 1))

            def products(out, s, col, tile, first, last):
                hi_, lo_ = tile
                w_hi, w_lo = whi[:, s, col:col + P], wlo[:, s, col:col + P]
                mm(out, w_hi, hi_, start=first, stop=False)
                mm(out, w_hi, lo_, start=False, stop=False)
                return mm(out, w_lo, hi_, start=False, stop=last)

            def xtile(k, width=T):
                return xs[:, k, 0, 0:width], xs[:, k, 1, 0:width]

            def htile(k, width=T):
                h, k = (hA, k) if k < 8 else (hB, k - 8)
                return h[:, k, 0, 0:width], h[:, k, 1, 0:width]

            def xs_wait(gen):
                return lambda k: eng.wait_ge(xs_ready, 16 * GEN[gen] + k + 1)

            def h_wait(base):
                return lambda k: eng.wait_ge(h_ready, base + k // 2 + 1) if k % 2 == 0 else None

            def pair_item(n, g, nb, tile, ready=None, nmore=0, gmore=0, width=T, after_first=None):
                item_free(g, gmore)
                for i in range(nb):
                    block_ready(n + i, nmore)
                    for k in range(8):
                        if ready is not None:
                            ready(8 * i + k)
                        for m in range(2):
                            last = products(acc[:, 2 * (g % 2) + m, 0:width], (n + i) % NSPLIT, k * 256 + m * P,
                                            tile(8 * i + k, width), i == k == 0, i == nb - 1 and k == 7)
                        if k % 4 == 3:
                            last.then_inc(half_used, 1)
                    if i == 0 and after_first is not None:
                        after_first()

            def pair_phase(name, items, nb, tile, ready=None, width=T, after_first=None):
                for j in range(items):
                    pair_item(N0[name] + nb * j, G0[name] + j, nb, tile, ready if j == 0 else None, width=width,
                              after_first=after_first if j == 0 else None)

            def pair_loop(name, turns, items, tile, ready=None):
                with eng.Fori(0, turns) as i:
                    for j in range(items):
                        pair_item(N0[name] + 2 * j, G0[name] + j, 2, tile, ready if j == 0 else None,
                                  nmore=2 * items * i, gmore=items * i)

            def quad_item(n, g, nb, tile, ready, after_first=None):
                for i in range(nb):
                    block_ready(n + i)
                    for m in range(4):
                        if i == 0 and m % 2 == 0:
                            item_free(g + m // 2)
                        for k in range(4):
                            if m == 0 and ready is not None:
                                ready(4 * i + k)
                            last = products(acc[:, 2 * ((g + m // 2) % 2) + m % 2, 0:T], (n + i) % NSPLIT,
                                            k * 512 + m * P, tile(4 * i + k), i == k == 0, i == nb - 1 and k == 3)
                        if m % 2 == 1:
                            last.then_inc(half_used, 1)

            def value_phase(name, samples):
                n, g = N0[name], G0[name]
                item_free(g)
                if samples:
                    item_free(g + 1)
                for i in range(4):
                    block_ready(n + i)
                    s = (n + i) % NSPLIT
                    for c in range(3 if samples else 2):
                        out, t0, tn = (acc[:, 2 * (g % 2) + c, :], c * P, P) if c < 2 else (acc[0:TS, 2 * ((g + 1) % 2), :], TP, TS)
                        for k in range(4):
                            x_hi, x_lo = (xs[:, 4 * i + k, part, t0:t0 + tn] for part in range(2))
                            w_hi, w_lo = whi[:, s, k * 512:(k + 1) * 512], wlo[:, s, k * 512:(k + 1) * 512]
                            mm(out, x_hi, w_hi, start=i == k == 0, stop=False)
                            mm(out, x_hi, w_lo, start=False, stop=False)
                            last = mm(out, x_lo, w_hi, start=False, stop=i == 3 and k == 3)
                        if c == 0 or c == (2 if samples else 1):
                            last.then_inc(half_used, 1)

            def turn_item(g, parts):
                item_free(g)
                for rows, j, n, src in parts:
                    last = nc.tensor.transpose(acc[0:rows, 2 * (g % 2) + j // 4, (j % 4) * P:(j % 4) * P + n],
                                               src, ident[0:src.shape[0], 0:src.shape[0]])
                last.then_inc(turned, 1)

            def statistics(k, width=T, cols=0):
                eng.wait_ge(ssq_ready, k)
                for m in range(2):
                    last = mm(ab[:, 3, 0:width], ones[:, :], ssq[:, m, 0:width], start=m == 0, stop=m == 1)
                for c in range(cols):
                    tn = P if c < 2 else TS
                    for m in range(2):
                        last = mm(ab[0:tn, 3, 300 + c:301 + c], ssq[:, m, c * P:c * P + tn], ones[:, 0:1],
                                  start=m == 0, stop=m == 1)
                last.then_inc(stat_ready, 1)

            def mem_attention(l):
                g = G0[f"mq{l}"]
                h0 = H0[f"m{l}"]

                def scores(h):
                    eng.wait_ge(acc_free, g + h // 2 + 1)
                    if h >= 2:
                        eng.wait_ge(e_ready, E0[f"m{l}"] + h - 1)
                    for q in range(2):
                        last = mm(ab[:, h % 2, q * TP:(q + 1) * TP], qm[:, h, q * P:(q + 1) * P], mKT[:, l, h, :],
                                  start=True, stop=True)
                    last.then_inc(s_ready, 1)

                def weigh(h):
                    following(eng, p_ready)
                    for k in range(2):
                        for q in range(2):
                            last = nc.tensor.transpose(ab[:, 2, k * TP + q * P:k * TP + (q + 1) * P],
                                                       Pm[:, h % 2, q, k * P:(k + 1) * P], ident[:, :])
                    last.then_inc(t_ready, 1)
                    following(eng, pt_ready)
                    if h:
                        eng.wait_ge(h_ready, h0 + h)
                    for k in range(2):
                        last = mm(ab[:, 3, 0:TP], mV[:, l, k, h * P:(h + 1) * P], PTm[:, k, :], start=k == 0, stop=k == 1)
                    last.then_inc(o_ready, 1)

                scores(0)
                scores(1)
                weigh(0)
                scores(2)
                weigh(1)
                scores(3)
                weigh(2)
                weigh(3)
                gk = G0[f"mk{l}"]

                def turn_keys(b):
                    landed(eng, ("s", f"mk{l}", b // 2))
                    rows = slot(("s", f"mk{l}", b // 2)).rearrange("p (b k c) -> p b k c", b=2, k=2)
                    turn_item(gk + b, [(P, 2 * h + k, P, rows[:, b % 2, k, h * P:(h + 1) * P])
                                       for h in range(NH_MEM) for k in range(2)])

                def sample_scores(b):
                    eng.wait_ge(acc_free, gk + b + 1)
                    if b == 0:
                        eng.wait_ge(e_ready, E0[f"m{l}"] + NH_MEM)
                    r = 32 * (b % 4)
                    for h in range(NH_MEM):
                        last = mm(ab[r:r + NH_MEM, 0, (b // 4) * TP:(b // 4 + 1) * TP], QzM[:, b, h, :],
                                  KTm[:, b % 2, h, :], start=h == 0, stop=h == NH_MEM - 1)
                    last.then_inc(scored, 1)

                turn_keys(0)
                for b in range(TS):
                    if b + 1 < TS:
                        turn_keys(b + 1)
                    sample_scores(b)
                following(eng, p_ready)
                for k in range(2):
                    for q in range(2):
                        last = nc.tensor.transpose(ab[:, 2, k * TP + q * P:k * TP + (q + 1) * P],
                                                   PsM[:, q, k * P:(k + 1) * P], ident[:, :])
                last.then_inc(t_ready, 1)
                following(eng, pt_ready)
                for b in range(TS):
                    key = ("s", f"mv{l}", b // 2)
                    landed(eng, key)
                    rows = slot(key).rearrange("p (b k c) -> p b k c", b=2, k=2)
                    r = 32 * (b % 4)
                    for k in range(2):
                        for h in range(NH_MEM):
                            last = mm(ab[r:r + NH_MEM, 1, (b // 4) * P:(b // 4 + 1) * P], PTzM[:, k, b, h, :],
                                      rows[:, b % 2, k, h * P:(h + 1) * P], start=k == h == 0, stop=k == 1 and h == NH_MEM - 1)
                    if b % 2:
                        last.then_inc(v_used, 1)
                following(eng, os_ready)
                eng.wait_ge(h_ready, h0 + NH_MEM)
                for q in range(2):
                    last = nc.tensor.transpose(ab[:, 3, q * P:(q + 1) * P], Os[:, q, :], ident[:, :])
                last.then_inc(t_ready, 1)

            hd = H0["dil"]

            def dil_scores(h):
                a_, hh, kv = (h // 2) % 2, h % 2, h // 2
                eng.wait_ge(acc_free, G0["dq"] + 3 * (h // 2) + 3)
                if h:
                    eng.wait_ge(s_free, h)
                for g in range(NG):
                    mm(ab[:, g // 2, (g % 2) * TP:(g % 2 + 1) * TP], qd[:, a_, g, hh, P:TP], KT[:, kv, 0:TP],
                       start=True, stop=True)
                for g in range(NG):
                    last = mm(ab[:, 2, g * P:(g + 1) * P], qd[:, a_, g, hh, 0:P], KT[:, kv, 0:P], start=True, stop=True)
                last.then_inc(s_ready, 1)

            def dil_turn(h):
                following(eng, p_ready)
                if h:
                    eng.wait_ge(h_ready, hd + h)
                for j, c in enumerate((TP, 0, P)):
                    last = nc.tensor.transpose(ab[:, 3, j * P:(j + 1) * P], Pn[:, c:c + P], ident[:, :])
                last.then_inc(t_ready, 1)

            def dil_out(h):
                following(eng, pt_ready)
                v = slice((h // 2) * P, (h // 2 + 1) * P)
                mm(ab[:, 3, 0:TP], V[:, 0, v], PT[:, 0:TP], start=True, stop=False)
                mm(ab[:, 3, P:TP], V[:, 1, v], PT[:, TP:TP + P], start=False, stop=True).then_inc(o_ready, 1)

            def dil_samples():
                gk = G0["dk"]

                def turn_keys(b):
                    key = ("s", "dk", b)
                    landed(eng, key)
                    for part in range(2):
                        turn_item(gk + 2 * b + part, [(P, j, P, slot(key)[:, (6 * part + j) * P:(6 * part + j + 1) * P])
                                                      for j in range(6)])

                def sample_scores(b):
                    eng.wait_ge(acc_free, gk + 2 * b + 2)
                    if b == 0:
                        eng.wait_ge(s_free, NH)
                        eng.wait_ge(h_ready, hd + NH)
                    r = 32 * (b % 4)
                    for g in range(NG):
                        for kv in range(KVH):
                            last = mm(ab[r:r + NH, b // 4, g * 129:(g + 1) * 129], QzD[:, g, b, kv, :],
                                      KTb[:, b % 2, KVH * g + kv, :], start=g == kv == 0,
                                      stop=kv == KVH - 1, skip_group_check=True)
                    last.then_inc(scored, 1)

                turn_keys(0)
                for b in range(TS):
                    if b + 1 < TS:
                        turn_keys(b + 1)
                    sample_scores(b)
                following(eng, p_ready)
                for g in range(NG):
                    for q in range(2):
                        j = 2 * g + q
                        last = nc.tensor.transpose(ab[:, 2 + j // 4, (j % 4) * P:(j % 4 + 1) * P], PsD[:, q, g, 0:P], ident[:, :])
                last.then_inc(t_ready, 1)
                following(eng, pt_ready)
                for b in range(TS):
                    key = ("s", "dv", b)
                    landed(eng, key)
                    r = 32 * (b % 4)
                    for g in range(NG):
                        for kv in range(KVH):
                            j = KVH * g + kv
                            last = mm(ab[r:r + NH, 0, (b // 4) * P:(b // 4 + 1) * P], PTzD[:, g, b, kv, :],
                                      slot(key)[:, j * P:(j + 1) * P], start=j == 0, stop=j == 11)
                    last.then_inc(v_used, 1)
                following(eng, os_ready)
                for q in range(2):
                    last = nc.tensor.transpose(ab[:, 1, q * P:(q + 1) * P], Os[:, q, :], ident[:, :])
                last.then_inc(t_ready, 1)

            eng.wait_ge(consts_in, CONSTS)
            eng.wait_ge(zeros_ready, 1)
            turn_item(G0["xload"], [(P, 0, P, gain_rows[:, 0:P]), (P, 1, 48, gain_rows[0:48, P:2 * P])])
            for c in range(2):
                landed(eng, ("s", "mem", c))
                for j in range(2):
                    turn_item(G0["memload"] + 2 * c + j, [(P, m, P, slot(("s", "mem", c))[:, (8 * j + m) * P:(8 * j + m + 1) * P])
                                                          for m in range(8)])
            for l in range(2):
                pair_phase(f"memk{l}", 2, 2, xtile, xs_wait(f"memkv{l}"), TP,
                           (lambda: statistics(STAT["mem"], TP, 2)) if l == 0 else None)
                if l == 1:
                    for c in range(3):
                        landed(eng, ("s", "x", c))
                        rows = slot(("s", "x", c))
                        if c < 2:
                            for j in range(2):
                                turn_item(G0["xt"] + 2 * c + j, [(P, m, P, rows[:, (8 * j + m) * P:(8 * j + m + 1) * P])
                                                                 for m in range(8)])
                        else:
                            item_free(G0["xt"] + 4)
                            for m in range(DC):
                                last = nc.tensor.transpose(acc[:, 2 * ((G0["xt"] + 4) % 2), TS * m:TS * (m + 1)],
                                                           rows[0:TS, m * P:(m + 1) * P], ident[0:TS, 0:TS])
                            last.then_inc(turned, 1)
                    landed(eng, ("s", "state", 0))
                    for j in range(2):
                        turn_item(G0["st"] + j, [(P, m, TS * NST, slot(("s", "state", 0))[0:TS * NST, (8 * j + m) * P:(8 * j + m + 1) * P])
                                                 for m in range(8)])
                value_phase(f"memv{l}", False)
                eng.wait_ge(acc_free, G0[f"memk{l}"] + 2)
                turn_item(G0[f"memkt{l}"], [(P, 4 * c + h, P, mKT[:, l, h, c * P:(c + 1) * P])
                                            for c in range(2) for h in range(NH_MEM)])
            pair_phase("win", 8, 2, xtile, xs_wait("mix0"), after_first=lambda: statistics(STAT["mix0"]))
            eng.wait_ge(h_ready, 8)
            for j in range(2):
                turn_item(G0["ut"] + j, [(23, m, P, ut[:, 8 * j + m, :]) for m in range(8)])
            for gi in range(4):
                quad_item(N0["grp"] + gi, G0["grp"] + 2 * gi, 1, lambda k, gi=gi: htile(4 * gi + k), None)
            pair_phase("wout", 8, 2, htile, h_wait(H0["z"]))

            def ffn(l):
                for part in range(3):
                    g_, d_ = f"f{l}g{part}", f"f{l}d{part}"
                    turns = PARTS[part] // 2
                    if part == 0:
                        pair_item(N0[g_], G0[g_], 2, xtile, xs_wait(f"ffn{l}"), after_first=lambda: statistics(STAT[f"ffn{l}"]))
                        pair_item(N0[g_] + 2, G0[g_] + 1, 2, xtile)
                        with eng.Fori(1, turns) as i:
                            for j in range(2):
                                pair_item(N0[g_] + 2 * j, G0[g_] + j, 2, xtile, nmore=4 * i, gmore=2 * i)
                    else:
                        pair_loop(g_, turns, 2, xtile)
                    base = H0[f"f{l}"] + sum(PARTS[:part]) // 2
                    if part < 2:
                        pair_loop(d_, 4, 2, htile, h_wait(base))
                    else:
                        for q in range(4):
                            quad_item(N0[d_] + 3 * q, G0[d_] + 2 * q, 3, htile, h_wait(base) if q == 0 else None)

            def mem_layer(l):
                pair_phase(f"mq{l}", 2, 2, xtile, xs_wait(f"memq{l}"), after_first=lambda: statistics(STAT[f"memq{l}"]))
                mem_attention(l)
                eng.wait_ge(h_ready, H0[f"m{l}"] + 5)
                for i in range(4):
                    quad_item(N0[f"mo{l}"] + i, G0[f"mo{l}"] + 2 * i, 1, htile, None)
                ffn(l)

            mem_layer(0)
            pair_phase("ksh", 2, 2, xtile, xs_wait("kv"), after_first=lambda: statistics(STAT["kv"], T, 3))
            value_phase("vsh", True)
            eng.wait_ge(acc_free, G0["ksh"] + 2)
            turn_item(G0["kt"], [(P, 4 * c + h, P, KT[:, h, c * P:(c + 1) * P]) for c in range(2) for h in range(KVH)])
            turn_item(G0["kt"] + 1, [(TS, h, P, KT[:, h, TP:T]) for h in range(KVH)])

            steps = [lambda h: dil_scores(h), lambda h: dil_turn(h), lambda h: (dil_out(h), dil_scores(h + 1)),
                     lambda h: dil_turn(h + 1), lambda h: dil_out(h + 1)]
            for hp in range(4):
                for g in range(NG):
                    n, gi = N0["dq"] + 6 * hp + 2 * g, G0["dq"] + 3 * hp + g
                    first = (lambda hp=hp, g=g: steps[2 * g](2 * hp - 2)) if hp else None
                    pair_item(n, gi, 2, xtile, xs_wait("mix1") if hp == g == 0 else None, after_first=first)
                    if hp and g < 2:
                        steps[2 * g + 1](2 * hp - 2)
            for st in steps:
                st(6)
            dil_samples()
            eng.wait_ge(h_ready, hd + NH + 1)
            pair_phase("do", 8, 1, htile)
            mem_layer(1)
            statistics(STAT["final"])
            for c in range(3):
                for j in range(2 if c < 2 else 1):
                    g = G0["y"] + 2 * c + j
                    eng.wait_ge(y_ready, 1)
                    if c < 2:
                        turn_item(g, [(P, m, P, x[:, 8 * j + m, c * P:(c + 1) * P]) for m in range(8)])
                    else:
                        for half in range(2):
                            turn_item(g + half, [(TS, m, P, x[:, 8 * half + m, TP:T]) for m in range(8)])

        @block.vector
        def _(eng):
            v = nc.vector
            at = [0]
            following = counter()

            def lo(n, more=0):
                r = RAW_OF[("w", n)]
                eng.wait_ge(raw_in[r % 2], more * 8 + LAND[("w", n)])
                eng.wait_ge(hi_ready, more + (n + 1))
                if n >= NSPLIT:
                    eng.wait_ge(half_used, more * 2 + 2 * (n - NSPLIT + 1))
                v.tensor_tensor(wlo[:, n % NSPLIT, :], raw[:, r % 2, :], whi[:, n % NSPLIT, :].bitcast(F32),
                                ALU.subtract).then_inc(lo_ready, 1)

            def upto(n):
                while at[0] <= min(n, NBLOCKS - 1):
                    lo(at[0])
                    at[0] += 1

            def block_used(n, more=0, half=2):
                eng.wait_ge(half_used, more * 2 + (2 * n + half))

            def banks(g, width=T):
                return acc[:, 2 * (g % 2):2 * (g % 2) + 2, 0:width]

            def columns(g):
                return acc[:, 2 * (g % 2):2 * (g % 2) + 2, :].rearrange("p b (s c) -> p (b s) c", c=P)

            def twice(ap):
                return ap.rearrange("p (o t) -> p o t", o=1).to_broadcast([P, 2, ap.shape[1]])

            def rms(k, width=T, cols=0):
                eng.wait_ge(std_ready, k)
                last = v.reciprocal(R[:, 0:width], std[:, 0:width])
                if cols:
                    v.reciprocal(Rc[:, 0:2], stdc[:, 0:2])
                if cols == 3:
                    v.reciprocal(Rc[0:TS, 2:3], stdc[0:TS, 2:3])
                eng.drain()

            def split_x(gain, m0, width=T):
                for m in (m0, m0 + 1):
                    v.tensor_scalar(xs[:, m, 0, 0:width], x[:, m, 0:width], gains[:, gain + m:gain + m + 1], None, ALU.mult)
                eng.drain()
                for m in (m0, m0 + 1):
                    v.scalar_tensor_tensor(out=xs[:, m, 1, 0:width], in0=x[:, m, 0:width], scalar=gains[:, gain + m:gain + m + 1],
                                           in1=xs[:, m, 0, 0:width].bitcast(F32), op0=ALU.mult, op1=ALU.subtract).then_inc(xs_ready, 1)

            def add_x(g, m0, gain=None):
                dst = x[:, m0:m0 + 2, :]
                v.tensor_tensor(dst, banks(g), dst, ALU.add).then_inc(acc_free, 1)
                eng.drain()
                if gain is not None:
                    split_x(gain, m0)

            def split_h(h, t, src, tn=2):
                v.tensor_copy(h[:, t, 0, :], src)
                eng.drain()
                v.tensor_tensor(h[:, t, 1, :], src, h[:, t, 0, :].bitcast(F32), ALU.subtract).then_inc(h_ready, 1)

            def stage_item(g, k, rows, width=2 * 512):
                if k in (2, 3):
                    eng.wait_ge(stored[k % 2 ^ 1], STORED[k - 1])
                    eng.drain()
                dst = stage_u if k in (2, 3) else (stage, stage2)[k % 2]
                flat = acc[0:rows, 2 * (g % 2):2 * (g % 2) + 2, :].rearrange("p b c -> p (b c)")
                v.tensor_copy(dst[0:rows, 0:width], flat[:, 0:width]).then_inc(acc_free, 1)

            v.memset(ones[:, :], 1.0)
            v.memset(eps[:, :], EPS)
            v.memset(ab[:, :, :], 0.0).then_inc(zeros_ready, 1)
            eng.wait_ge(turned, 1)
            v.tensor_copy(gains[:, :], acc[:, 0, 0:176]).then_inc(acc_free, 1)
            for c in range(2):
                for j in range(2):
                    eng.wait_ge(turned, TURN0["memload"] + 2 * c + j + 1)
                    v.tensor_copy(x[:, 8 * j:8 * j + 8, c * P:(c + 1) * P], columns(G0["memload"] + 2 * c + j)).then_inc(acc_free, 1)
            eng.drain()
            for l in range(2):
                upto(N0[f"memk{l}"] + 1)
                if l == 1:
                    block_used(N0["memv0"] + 3)
                for m in range(0, DC, 2):
                    split_x(GAIN["memkv"][l], m, TP)
                upto(N0[f"memk{l}"] + 2)
                if l == 0:
                    rms(STAT["mem"], TP, 2)
                upto(N0[f"memk{l}"] + 3)
                for j in range(2):
                    block_used(N0[f"memk{l}"] + 2 * j + 1)
                    g = G0[f"memk{l}"] + j
                    v.tensor_tensor(mKT[:, l, 2 * j:2 * j + 2, :], banks(g, TP), twice(R[:, 0:TP]), ALU.mult).then_inc(acc_free, 1)
                    if l == 0:
                        upto(N0["memv0"] + 2 * j + 1)
                if l == 1:
                    eng.drain()
                    for c in range(3):
                        for j in range(2 if c < 2 else 1):
                            g = G0["xt"] + 2 * c + j
                            eng.wait_ge(turned, TURN0["xt"] + 2 * c + j + 1)
                            if c < 2:
                                v.tensor_copy(x[:, 8 * j:8 * j + 8, c * P:(c + 1) * P], columns(g)).then_inc(acc_free, 1)
                            else:
                                v.tensor_copy(x[:, :, TP:T], acc[:, 2 * (g % 2), 0:P].rearrange("p (m b) -> p m b", b=TS)).then_inc(acc_free, 1)
                    for j in range(2):
                        g = G0["st"] + j
                        eng.wait_ge(turned, TURN0["st"] + j + 1)
                        for q in range(2):
                            w = 2 << (2 * j + q)
                            rows = columns(g)[:, 4 * q:4 * q + 4, 0:TS * NST].rearrange("p s (b t) -> p s b t", t=NST)
                            last = v.tensor_reduce(wsum[:, 8 * j + 4 * q:8 * j + 4 * q + 4, :], rows[:, :, :, NST - (w - 1):NST],
                                                   AX.X, ALU.add)
                        last.then_inc(acc_free, 1)
                g = G0[f"memv{l}"]
                upto(N0[f"memv{l}"] + 3)
                block_used(N0[f"memv{l}"] + 3)
                for c in range(2):
                    last = v.tensor_scalar(mV[:, l, c, :], acc[:, 2 * (g % 2) + c, :], Rc[:, c:c + 1], None, ALU.mult)
                last.then_inc(acc_free, 1)
                eng.wait_ge(turned, TURN0[f"memkt{l}"] + 1)
                stage_item(G0[f"memkt{l}"], l, P)

            upto(N0["win"] + 1)
            v.memset(tmp[:, 0:6 * UP], 0.0)
            eng.drain()
            for m in range(0, DC, 2):
                split_x(GAIN["mix"][0], m)
            for k in range(2):
                eng.wait_ge(stored[k], STORED[k])
            for j in range(8):
                n, g = N0["win"] + 2 * j, G0["win"] + j
                upto(n + 2)
                if j == 0:
                    eng.wait_ge(consts_in, CONSTS)
                    rms(STAT["mix0"])
                upto(n + 3)
                block_used(n + 1)
                gi = j // 2
                w = 2 << gi
                b = banks(g)
                v.tensor_tensor(U[:, :, 16:UP], b[:, :, 0:TP], twice(R[:, 0:TP]), ALU.mult)
                v.tensor_tensor(usm, b[:, :, TP:T], twice(R[:, TP:T]), ALU.mult).then_inc(acc_free, 1)
                eng.drain()
                v.tensor_copy(ut[:, 2 * j:2 * j + 2, 0:NST], U[:, :, UP - NST:UP])
                v.tensor_copy(ut[:, 2 * j:2 * j + 2, NST:NST + TS], usm)
                src, step = U, 1
                for i in range(gi + 1):
                    dst, first = (Ta, Tb)[i % 2], 2 * step - 1
                    v.tensor_tensor(dst[:, :, first:UP], src[:, :, first:UP], src[:, :, first - step:UP - step], ALU.add)
                    eng.drain()
                    src, step = dst, 2 * step
                for m in range(2):
                    v.tensor_tensor(src[:, m, 16:32], src[:, m, 16:32], invc[:, gi, :], ALU.mult)
                v.tensor_tensor(us2, usm, wsum[:, 2 * j:2 * j + 2, :], ALU.add)
                eng.drain()
                pooled = (Tb if src is Ta else Ta)[:, :, 0:T]
                v.scalar_tensor_tensor(out=pooled[:, :, 0:TP], in0=src[:, :, 16:UP], scalar=1.0 / w, in1=U[:, :, 16:UP],
                                       op0=ALU.mult, op1=ALU.subtract)
                v.scalar_tensor_tensor(out=pooled[:, :, TP:T], in0=us2, scalar=1.0 / w, in1=usm, op0=ALU.mult, op1=ALU.subtract)
                eng.drain()
                split_h(hA if j < 4 else hB, slice(2 * j % 8, 2 * j % 8 + 2), pooled)
                eng.drain()
            upto(N0["grp"] + 2)
            for j in range(2):
                eng.wait_ge(turned, TURN0["ut"] + j + 1)
                stage_item(G0["ut"] + j, 2 + j, 23)
            for gi in range(4):
                upto(N0["grp"] + gi + 2)
                for j in range(2):
                    g = G0["grp"] + 2 * gi + j
                    block_used(N0["grp"] + gi)
                    h, t = (hA, 4 * gi + 2 * j) if gi < 2 else (hB, 4 * gi + 2 * j - 8)
                    for part in range(2):
                        for m in range(2):
                            s = gains[:, GAIN["scale"][0] + 4 * gi + 2 * j + m:GAIN["scale"][0] + 4 * gi + 2 * j + m + 1]
                            src = acc[:, 2 * (g % 2) + m, 0:T]
                            if part == 0:
                                v.tensor_scalar(h[:, t + m, 0, :], src, s, None, ALU.mult)
                            else:
                                last = v.scalar_tensor_tensor(out=h[:, t + m, 1, :], in0=src, scalar=s,
                                                              in1=h[:, t + m, 0, :].bitcast(F32), op0=ALU.mult, op1=ALU.subtract)
                        eng.drain()
                        if part == 0:
                            continue
                    v.tensor_copy(small[:, 31:32], eps[:, :]).then_inc(h_ready, 1)
                    v.tensor_copy(small[:, 30:31], eps[:, :]).then_inc(acc_free, 1)
            for j in range(8):
                n = N0["wout"] + 2 * j
                upto(n + 3)
                block_used(n + 1)
                add_x(G0["wout"] + j, 2 * j, GAIN["memq"][0])

            def maxima(parts):
                for in_, c, ax in parts:
                    v.tensor_reduce(small[:, c + 8:c + 9], in_, ax, ALU.max)
                eng.drain()
                for i, (_, c, _) in enumerate(parts):
                    last = v.tensor_scalar(small[:, c:c + 1], small[:, c + 8:c + 9], -SCALE, None, ALU.mult)
                    if i == len(parts) - 1:
                        last.then_inc(nb_ready, 1)

            def inverses(c, n=2):
                following(eng, e_ready)
                v.reciprocal(small[:, c + 12:c + 12 + n], small[:, c + 4:c + 4 + n])
                eng.drain()

            def head_out(h, ready):
                v.tensor_copy(hA[:, h, 0, 0:TP], ab[:, 3, 0:TP])
                eng.drain()
                v.tensor_tensor(hA[:, h, 1, 0:TP], ab[:, 3, 0:TP], hA[:, h, 0, 0:TP].bitcast(F32), ALU.subtract).then_inc(h_ready, 1)

            def samples_out(bank, heads):
                cols = ab[:, bank, 0:2 * P].rearrange("p (q m r) -> p r q m", q=2, r=32)
                dst = [hA[:, 0:heads, part, TP:T].rearrange("p h (q m) -> p h q m", q=2) for part in range(2)]
                for h in range(heads):
                    v.tensor_copy(dst[0][:, h], cols[:, h])
                eng.drain()
                for h in range(heads):
                    last = v.tensor_tensor(dst[1][:, h], cols[:, h], dst[0][:, h].bitcast(F32), ALU.subtract)
                last.then_inc(h_ready, 1)

            def mem_attention(l):
                g = G0[f"mq{l}"]
                n = N0[f"mq{l}"]
                eng.wait_ge(stored[0], STORED[2 if l == 0 else 4])
                eng.wait_ge(stored[1], STORED[3 if l == 0 else 5])
                for j in range(2):
                    upto(n + 2 * j + 2)
                    if j == 0:
                        rms(STAT[f"memq{l}"])
                    upto(n + 2 * j + 3)
                    block_used(n + 2 * j + 1)
                    v.tensor_tensor(qm[:, 2 * j:2 * j + 2, :], banks(g + j), twice(R[:, :]), ALU.mult).then_inc(acc_free, 1)
                upto(N0[f"mo{l}"] + 3)
                v.memset(QzM, 0.0)
                v.memset(PTzM, 0.0)
                eng.drain()
                for h in range(NH_MEM):
                    v.tensor_copy(QzM[:, :, h, h], qm[:, h, TP:T])
                eng.drain()

                def head_max(h):
                    following(eng, s_ready)
                    maxima([(ab[:, h % 2, q * TP:(q + 1) * TP], 2 * (h % 2) + q, AX.X) for q in range(2)])

                def head_probabilities(h):
                    s = h % 2
                    inverses(2 * s)
                    for q in range(2):
                        last = v.tensor_scalar(Pm[:, s, q, :], Pm[:, s, q, :], small[:, 12 + 2 * s + q:13 + 2 * s + q], None, ALU.mult)
                    last.then_inc(p_ready, 1)

                def head_rest(h):
                    following(eng, t_ready)
                    v.tensor_copy(PTm[:, :, :].rearrange("p k t -> p (k t)"), ab[:, 2, :]).then_inc(pt_ready, 1)
                    following(eng, o_ready)
                    head_out(h, None)

                head_max(0)
                head_max(1)
                for h in range(NH_MEM):
                    head_probabilities(h)
                    head_rest(h)
                    if h + 2 < NH_MEM:
                        head_max(h + 2)
                gk = G0[f"mk{l}"]
                for b in range(TS):
                    eng.wait_ge(turned, TURN0[f"mk{l}"] + b + 1)
                    if b >= 2:
                        eng.wait_ge(scored, SC0[f"m{l}"] + b - 1)
                    v.tensor_copy(KTm[:, b % 2].rearrange("p h j -> p (h j)"),
                                  acc[:, 2 * ((gk + b) % 2):2 * ((gk + b) % 2) + 2, :].rearrange("p b c -> p (b c)")).then_inc(acc_free, 1)
                eng.wait_ge(scored, SC0[f"m{l}"] + TS)
                eng.drain()
                maxima([(ab[:, 0, b * TP:(b + 1) * TP], 16 + b, AX.X) for b in range(2)])
                inverses(16)
                for b in range(2):
                    last = v.tensor_scalar(PsM[:, b, :], PsM[:, b, :], small[:, 28 + b:29 + b], None, ALU.mult)
                last.then_inc(p_ready, 1)
                following(eng, t_ready)
                cols = ab[:, 2, :].rearrange("p (k q m r) -> p k q m r", k=2, q=2, r=32)
                dst = PTzM.rearrange("p k (q m) h c -> p k q m h c", q=2)
                for k in range(2):
                    for h in range(NH_MEM):
                        last = v.tensor_copy(dst[:, k, :, :, h, h], cols[:, k, :, :, h])
                last.then_inc(pt_ready, 1)
                eng.wait_ge(v_used, VU0[f"m{l}"] + 4)
                v.tensor_copy(Os.rearrange("p b d -> p (b d)"), ab[:, 1, 0:2 * P]).then_inc(os_ready, 1)
                following(eng, t_ready)
                samples_out(3, NH_MEM)
                eng.drain()

            def mem_layer(l):
                mem_attention(l)
                for i in range(4):
                    upto(N0[f"mo{l}"] + i + 2)
                    for j in range(2):
                        block_used(N0[f"mo{l}"] + i, half=1 + j)
                        add_x(G0[f"mo{l}"] + 2 * i + j, 4 * i + 2 * j, GAIN["ffn"][l])

            def ffn(l, gain):
                for part in range(3):
                    n, g, turns = N0[f"f{l}g{part}"], G0[f"f{l}g{part}"], PARTS[part] // 2
                    e0 = 22 * l + sum(PARTS[:part]) // 2

                    def turn(i, h, t):
                        first = part == 0 and isinstance(i, int)
                        lo(n + 2, 4 * i)
                        if first:
                            rms(STAT[f"ffn{l}"])
                        lo(n + 3, 4 * i)
                        block_used(n + 1, 4 * i)
                        v.tensor_tensor(gateF, banks(g), twice(R[:, :]), ALU.mult).then_inc(acc_free, 1)
                        lo(n + 4, 4 * i)
                        lo(n + 5, 4 * i)
                        eng.wait_ge(silu_ready, 1 * i + (e0 + 1))
                        v.tensor_tensor(siluF, siluF, twice(R[:, :]), ALU.mult)
                        eng.drain()
                        block_used(n + 3, 4 * i)
                        v.tensor_tensor(upF, banks(g + 1), siluF, ALU.mult).then_inc(acc_free, 1)
                        eng.drain()
                        split_h(h, t, upF)
                        eng.drain()

                    upto(n + 1)
                    first = 0
                    if part == 0:
                        turn(0, hA, slice(0, 2))
                        first = 1
                    with eng.Fori(first, 4) as i:
                        turn(i, hA, bass.ds(2 * i, 2))
                    with eng.Fori(4, turns) as i:
                        turn(i, hB, bass.ds(2 * i - 8, 2))
                    if part < 2:
                        nd, gd = N0[f"f{l}d{part}"], G0[f"f{l}d{part}"]
                        with eng.Fori(0, 4) as i:
                            for j in range(2):
                                lo(nd + 2 * j + 2, 4 * i)
                                lo(nd + 2 * j + 3, 4 * i)
                                block_used(nd + 2 * j + 1, 4 * i)
                                dst = x[:, bass.ds(4 * i + 2 * j, 2), :]
                                v.tensor_tensor(dst, banks(gd + j), dst, ALU.add).then_inc(acc_free, 1)
                        eng.drain()
                        at[0] = nd + 18
                    else:
                        at[0] = n + 4 * turns + 2
                        nd = N0[f"f{l}d2"]
                        for q in range(4):
                            upto(nd + 3 * q + 4)
                            for j in range(2):
                                block_used(nd + 3 * q + 2, half=1 + j)
                                add_x(G0[f"f{l}d2"] + 2 * q + j, 4 * q + 2 * j, gain)

            mem_layer(0)
            ffn(0, GAIN["kv"][0])

            n = N0["ksh"]
            for j in range(2):
                upto(n + 2 * j + 2)
                if j == 0:
                    rms(STAT["kv"], T, 3)
                upto(n + 2 * j + 3)
                block_used(n + 2 * j + 1)
                v.tensor_tensor(KT[:, 2 * j:2 * j + 2, :], banks(G0["ksh"] + j), twice(R[:, :]), ALU.mult).then_inc(acc_free, 1)
            v.memset(Vrep, 0.0)
            upto(N0["dq"] + 1)
            block_used(N0["vsh"] + 3)
            g = G0["vsh"]
            for c in range(2):
                last = v.tensor_scalar(V[:, c, :], acc[:, 2 * (g % 2) + c, :], Rc[:, c:c + 1], None, ALU.mult)
            last.then_inc(acc_free, 1)
            v.tensor_scalar(Vsm, acc[0:TS, 2 * ((g + 1) % 2), :], Rc[0:TS, 2:3], None, ALU.mult).then_inc(acc_free, 1)
            for j in range(2):
                eng.wait_ge(turned, TURN0["kt"] + j + 1)
                stage_item(G0["kt"] + j, 4 + j, (P, TS)[j], (1024, 512)[j])

            for m in range(0, DC, 2):
                split_x(GAIN["mix"][1], m)
            eng.wait_ge(stored[0], STORED[4])
            eng.wait_ge(stored[1], STORED[5])
            eng.wait_ge(vs_done, 16)
            eng.wait_ge(mask_in, 16)
            v.memset(QzD, 0.0)
            eng.drain()

            def dil_max(h):
                following(eng, s_ready)
                S1 = S[:, 0:768].rearrange("p (g j) -> p g j", g=NG)
                S0 = S[:, 768:1152].rearrange("p (g j) -> p g j", g=NG)
                v.tensor_tensor(S1, ab[:, 0:2, :].rearrange("p b (g j) -> p (b g) j", j=TP)[:, 0:NG, :], mask[:, :, :], ALU.add)
                v.tensor_tensor(S0, ab[:, 2, 0:384].rearrange("p (g j) -> p g j", g=NG), mask[:, :, P:2 * P], ALU.add).then_inc(s_free, 1)
                eng.drain()
                maxima([(S[:, 0:768], 0, AX.X), (S[:, 768:1152], 1, AX.X)])

            def dil_probabilities():
                inverses(0)
                for (c, w, o_) in ((0, TP, 0), (768, P, TP)):
                    v.tensor_tensor(Pn[:, o_:o_ + w], S[:, c:c + w], S[:, c + w:c + 2 * w], ALU.add)
                eng.drain()
                for (c, w, o_) in ((0, TP, 0), (768, P, TP)):
                    v.tensor_tensor(Pn[:, o_:o_ + w], Pn[:, o_:o_ + w], S[:, c + 2 * w:c + 3 * w], ALU.add)
                eng.drain()
                for i, (w, o_) in enumerate(((TP, 0), (P, TP))):
                    last = v.tensor_scalar(Pn[:, o_:o_ + w], Pn[:, o_:o_ + w], small[:, 12 + i:13 + i], None, ALU.mult)
                last.then_inc(p_ready, 1)

            def dil_turned():
                following(eng, t_ready)
                v.tensor_copy(PT[:, :], ab[:, 3, 0:384]).then_inc(pt_ready, 1)

            def dil_finish(h):
                following(eng, o_ready)
                head_out(h, None)

            steps = [lambda h: (dil_max(h), dil_probabilities()), lambda h: dil_turned(),
                     lambda h: (dil_finish(h), dil_max(h + 1), dil_probabilities()), lambda h: dil_turned(),
                     lambda h: dil_finish(h + 1)]
            for hp in range(4):
                for j in range(6):
                    n, g = N0["dq"] + 6 * hp + j, G0["dq"] + 3 * hp + j // 2
                    upto(n + 2)
                    if j % 2:
                        block_used(n)
                        dst = qd[:, hp % 2, j // 2]
                        v.tensor_tensor(dst, banks(g), twice(R[:, :]), ALU.mult).then_inc(acc_free, 1)
                        eng.drain()
                        v.tensor_copy(QzD[:, j // 2, :, hp, 2 * hp:2 * hp + 2], dst[:, :, TP:T].rearrange("p h b -> p b h"))
                    if hp and j < 5:
                        steps[j](2 * hp - 2)
            upto(N0["do"] + 3)
            for st in steps:
                st(6)
            v.memset(PTzD, 0.0)
            eng.drain()
            gk = G0["dk"]
            for b in range(TS):
                for part in range(2):
                    eng.wait_ge(turned, TURN0["dk"] + 2 * b + part + 1)
                    if part == 0:
                        if b >= 2:
                            eng.wait_ge(scored, SC0["dil"] + b - 1)
                        v.tensor_copy(KTb[:, b % 2, :, P].rearrange("p (g k) -> p g k", g=NG),
                                      KT[:, :, TP + b].rearrange("p (o k) -> p o k", o=1).to_broadcast([P, NG, KVH]))
                    v.tensor_copy(KTb[:, b % 2, 6 * part:6 * part + 6, 0:P], columns(gk + 2 * b + part)[:, 0:6, :]).then_inc(acc_free, 1)
            eng.wait_ge(scored, SC0["dil"] + TS)
            maxima([(ab[:, b, 0:387], 16 + b, AX.X) for b in range(2)])
            inverses(16)
            for b in range(2):
                last = v.tensor_scalar(PsDf[:, b, :], PsDf[:, b, :], small[:, 28 + b:29 + b], None, ALU.mult)
            last.then_inc(p_ready, 1)
            eng.drain()
            v.tensor_reduce(small[:, 8:10], PsD[:, :, :, P], AX.X, ALU.add)
            following(eng, t_ready)
            cols = ab[:, 2:4, :].rearrange("p k (q m r) -> p (k q) m r", m=4, r=32)[:, 0:6].rearrange("p (g q) m r -> p g q m r", g=NG)
            dst = PTzD.rearrange("p g (q m) k h -> p g q m k h", q=2)
            for g in range(NG):
                for h in range(NH):
                    last = v.tensor_copy(dst[:, g, :, :, h // 2, h], cols[:, g, :, :, h])
            last.then_inc(pt_ready, 1)
            eng.wait_ge(v_used, VU0["dil"] + TS)
            eng.wait_ge(vrep_in, 16 * TS)
            for q in range(2):
                last = v.scalar_tensor_tensor(out=Os[:, q, :], in0=Vrep[:, q, :], scalar=small[:, 8 + q:9 + q],
                                              in1=ab[:, 0, q * P:(q + 1) * P], op0=ALU.mult, op1=ALU.add)
            last.then_inc(os_ready, 1)
            following(eng, t_ready)
            samples_out(1, NH)
            eng.drain()
            for j in range(8):
                n = N0["do"] + j
                upto(n + 2)
                block_used(n)
                add_x(G0["do"] + j, 2 * j, GAIN["memq"][1])
            mem_layer(1)
            ffn(1, None)

            rms(STAT["final"])
            for m in range(DC):
                last = v.scalar_tensor_tensor(out=x[:, m, :], in0=x[:, m, :], scalar=gains[:, GAIN["final"][0] + m:GAIN["final"][0] + m + 1],
                                              in1=R[:, :], op0=ALU.mult, op1=ALU.mult)
            last.then_inc(y_ready, 1)
            for c in range(3):
                rows, dst = (P, raw[:, c, :]) if c < 2 else (TS, att[0:TS, 0:D])
                for j in range(2):
                    g = G0["y"] + 2 * c + j
                    eng.wait_ge(turned, TURN0["y"] + 2 * c + j + 1)
                    v.tensor_copy(dst[:, 1024 * j:1024 * (j + 1)],
                                  acc[0:rows, 2 * (g % 2):2 * (g % 2) + 2, :].rearrange("p b c -> p (b c)")).then_inc(acc_free, 1)

        @block.gpsimd
        def _(eng):
            gp = nc.gpsimd

            def squares(done, width=T):
                for j in range(8):
                    done(j)
                    src = x[:, 2 * j:2 * j + 2, 0:width]
                    gp.tensor_tensor((sq if j else ssq)[:, :, 0:width], src, src, ALU.mult)
                    eng.drain()
                    if j:
                        last = gp.tensor_tensor(ssq[:, :, 0:width], ssq[:, :, 0:width], sq[:, :, 0:width], ALU.add)
                        if j == 7:
                            last.then_inc(ssq_ready, 1)
                        eng.drain()

            def taken(g):
                eng.wait_ge(acc_free, g + 1)

            def by_item(g):
                return lambda j: taken(g + j)

            eng.dma_start(pool_s[0, :, 0:NST - 1, :], a["state_pool"][0, :, 1:NST, :]).then_inc(out_done, 16)
            squares(lambda j: taken(G0["memload"] + 3), TP)
            taken(G0["memkt0"])
            eng.dma_start(mem_v_p[0, 0].rearrange("(c p) h d -> p c (h d)", p=P), mV[:, 0, :, :]).then_inc(out_done, 16)
            eng.dma_start(mem_k_p[0, 0].rearrange("(c p) h d -> p c (h d)", p=P),
                          stage.rearrange("p (c k) -> p c k", c=2)).then_inc(stored[0], 16)
            squares(lambda j: taken(G0["xt"] + 4))
            taken(G0["memkt1"])
            eng.dma_start(mem_v_p[1, 0].rearrange("(c p) h d -> p c (h d)", p=P), mV[:, 1, :, :]).then_inc(out_done, 16)
            eng.dma_start(mem_k_p[1, 0].rearrange("(c p) h d -> p c (h d)", p=P),
                          stage2.rearrange("p (c k) -> p c k", c=2)).then_inc(stored[1], 16)
            for j in range(2):
                taken(G0["ut"] + j)
                src, cols = stage_u, slice(1024 * j, 1024 * (j + 1))
                eng.dma_start(pool_p[0, 0, :, cols], src[0:NST, :]).then_inc(stored[j], 16)
                eng.dma_start(pool_s[0, :, NST - 1, cols], src[NST:NST + TS, :]).then_inc(stored[j], 16)
            squares(by_item(G0["wout"]))
            squares(by_item(G0["mo0"]))
            squares(by_item(G0["f0d2"]))
            taken(G0["vsh"] + 1)
            eng.dma_start(v_s.rearrange("b t h d -> (b t) (h d)"), Vsm).then_inc(vs_done, 16)
            eng.dma_start(wv_p[0].rearrange("(c p) h d -> p c (h d)", p=P), V[:, :, :]).then_inc(out_done, 16)
            taken(G0["kt"])
            eng.dma_start(wk_p[0].rearrange("(c p) h d -> p c (h d)", p=P),
                          stage.rearrange("p (c k) -> p c k", c=2)).then_inc(stored[0], 16)
            taken(G0["kt"] + 1)
            eng.dma_start(k_s.rearrange("b t h d -> (b t) (h d)"), stage2[0:TS, 0:MEMD]).then_inc(stored[1], 16)
            eng.wait_ge(vs_done, 16)
            for b in range(TS):
                r = 32 * (b % 4)
                dst = Vrep[r:r + NH, b // 4, :]
                src = v_s[b, 0].rearrange("k (o d) -> k o d", o=1).to_broadcast([KVH, 2, P])
                eng.dma_start(dst, src).then_inc(vrep_in, 16)
            squares(by_item(G0["do"]))
            squares(by_item(G0["mo1"]))
            squares(by_item(G0["f1d2"]))
            for c in range(3):
                taken(G0["y"] + 2 * c + 1)
                if c < 2:
                    eng.dma_start(y_p[0, c * P:(c + 1) * P, :], raw[:, c, :]).then_inc(out_done, 16)
                else:
                    eng.dma_start(y_s[:, 0, :], att[0:TS, 0:D]).then_inc(out_done, 16)
            eng.wait_ge(out_done, 16 * 7)
            eng.wait_ge(stored[0], STORED[4])
            eng.wait_ge(stored[1], STORED[5])
            eng.wait_ge(vs_done, 16)


_INS = ["x_prompt", "x_sample", "mem_prompt", "state_pool", "cache_win_k", "cache_win_v", "cache_mem_k", "cache_mem_v",
        "norm_mix", "norm_mem_q", "norm_mem_kv", "norm_ffn", "pool_w_in", "pool_w_group", "pool_scale", "pool_w_out",
        "norm_kv", "w_k_shared", "w_v_shared", "dil_w_q", "dil_w_o", "mem_w_q", "mem_w_k", "mem_w_v", "mem_w_o",
        "ffn_w_gate", "ffn_w_up", "ffn_w_down", "norm_final"]
_OUTS = [(1, TP, D), (TS, 1, D), (1, 1, NST, D), (1, TS, NST, D), (1, TP, KVH, P), (1, TP, KVH, P), (TS, 1, KVH, P),
         (TS, 1, KVH, P), (2, 1, TP, NH_MEM, P), (2, 1, TP, NH_MEM, P)]


def _shape_constants():
    q = np.arange(P)[:, None] + P
    j = np.arange(2 * P)[None, :]
    mask = np.stack([np.where((q - j >= 0) & ((q - j) % d == 0) & ((q - j) // d <= WIN_KEYS), 0.0, MASKED) for d in DILS], 1)
    t = np.arange(16)
    inv = np.stack([w / np.minimum(t + 1, w) for w in (2, 4, 8, 16)])
    return {"c_ident": np.eye(P, dtype=np.float32), "c_mask": mask.astype(np.float32),
            "c_inv": np.broadcast_to(inv[None], (P, 4, 16)).astype(np.float32)}


def kernel(**inputs):
    import concourse.bacc as bacc
    from concourse.bass_utils import run_bass_kernel_spmd

    nc = bacc.Bacc("TRN2", target_bir_lowering=False, num_devices=1)
    arrays, aps = {}, {}
    given = {n: np.ascontiguousarray(inputs[n]) for n in _INS}
    given.update(_shape_constants())
    for name, v in given.items():
        arrays[f"in_{name}"] = v
        aps[name] = nc.dram_tensor(f"in_{name}", v.shape, F32, kind="ExternalInput").ap()
    outs = [nc.dram_tensor(f"out_{i}", s, F32, kind="ExternalOutput").ap() for i, s in enumerate(_OUTS)]
    trunk(nc, aps, outs)
    r = run_bass_kernel_spmd(nc, [arrays], core_ids=[0])
    return tuple(r.results[0][f"out_{i}"] for i in range(len(_OUTS)))
```

```python
from contextlib import ExitStack

import numpy as np

import concourse.bass as bass
from concourse import mybir

F32 = mybir.dt.float32
F32R = mybir.dt.float32r
ALU = mybir.AluOpType
ACT = mybir.ActivationFunctionType
AX = mybir.AxisListType

P = 128
D = 2048
DC = D // P
TP = 256
TS = 8
T = TP + TS
FF = 5632
FC = FF // P
MEMD = 512
NH_MEM = 4
KVH = 4
NG = 3
NH = 8
DILS = (1, 4, 16)
PAST = 2048
WIN_KEYS = 128
NST = 15
EPS = 1e-6
SCALE = float(P) ** -0.5
MASKED = -1e30
BLK = 2048
NSPLIT = 4
PARTS = (16, 16, 12)
GAIN = {"memkv": (0, 16), "mix": (32, 48), "memq": (64, 80), "ffn": (96, 112), "kv": (128,), "final": (144,),
        "scale": (160,)}

PHASES = [
    ("xload", 0, 1),
    ("memload", 0, 4),
    ("memk0", 4, 2), ("memv0", 4, 1), ("memkt0", 0, 1),
    ("memk1", 4, 2), ("xt", 0, 5), ("st", 0, 2), ("memv1", 4, 1), ("memkt1", 0, 1),
    ("win", 16, 8), ("ut", 0, 2), ("grp", 4, 8), ("wout", 16, 8),
    ("mq0", 4, 2), ("mk0", 0, 8), ("mo0", 4, 8),
    ("f0g0", 32, 16), ("f0d0", 16, 8), ("f0g1", 32, 16), ("f0d1", 16, 8), ("f0g2", 24, 12), ("f0d2", 12, 8),
    ("ksh", 4, 2), ("vsh", 4, 2), ("kt", 0, 2),
    ("dq", 24, 12), ("dk", 0, 16), ("do", 8, 8),
    ("mq1", 4, 2), ("mk1", 0, 8), ("mo1", 4, 8),
    ("f1g0", 32, 16), ("f1d0", 16, 8), ("f1g1", 32, 16), ("f1d1", 16, 8), ("f1g2", 24, 12), ("f1d2", 12, 8),
    ("y", 0, 6),
]
N0, G0 = {}, {}
_n = _g = 0
for _name, _nb, _ni in PHASES:
    N0[_name], G0[_name] = _n, _g
    _n += _nb
    _g += _ni
NBLOCKS = _n

RAW = [("s", "mem", 0), ("s", "mem", 1)]
RAW += [("w", n) for n in range(N0["memk0"], N0["memk1"] + 4)]
RAW += [("s", "x", i) for i in range(3)] + [("s", "state", 0)]
RAW += [("w", n) for n in range(N0["memv1"], NBLOCKS)]
RAW_OF = {k: r for r, k in enumerate(RAW)}

TURN0, _t = {}, 0
for _name, _nb, _ni in PHASES:
    if _nb == 0:
        TURN0[_name] = _t
        _t += _ni
ROWS_DONE = {("s", "mem", 0): TURN0["memload"] + 2, ("s", "mem", 1): TURN0["memload"] + 4,
             ("s", "x", 0): TURN0["xt"] + 2, ("s", "x", 1): TURN0["xt"] + 4, ("s", "x", 2): TURN0["xt"] + 5,
             ("s", "state", 0): TURN0["st"] + 2}
LAND, _c = {}, [0, 0]
for _r, _k in enumerate(RAW):
    _c[_r % 2] += 16
    LAND[_k] = _c[_r % 2]

CACHED = []
for _l in range(2):
    CACHED += [((f"mk{_l}", i), s) for i, s in enumerate((5, 0, 1, 2))]
    CACHED += [((f"mv{_l}", i), s) for i, s in enumerate((3, 5, 0, 1))]
    if _l == 0:
        CACHED += [(("dk", b), (b - 1) % 5 if b else 6) for b in range(TS)]
        CACHED += [(("dv", b), (b + 7) % 5) for b in range(TS)]
CACHED_SLOT = dict(CACHED)
CACHED_LAND, _c = {}, [0] * 7
for _k, _s in CACHED:
    _c[_s] += 48 if _k[0][0] == "d" else 16
    CACHED_LAND[_k] = _c[_s]

H0 = {"p": 0, "z": 8, "m0": 16, "f0": 21, "dil": 43, "m1": 52, "f1": 57}
GEN = {"memkv0": 0, "memkv1": 1, "mix0": 2, "memq0": 3, "ffn0": 4, "kv": 5, "mix1": 6, "memq1": 7, "ffn1": 8}
E0 = {"m0": 0, "dil": NH_MEM + 2, "m1": NH_MEM + 2 + NH + 2}
SC0 = {"m0": 0, "dil": TS, "m1": 2 * TS}
VU0 = {"m0": 0, "dil": TS, "m1": 2 * TS}
STORED = [16, 16, 48, 48, 64, 64]
CONSTS = 16 * 9
STAT = {"mem": 1, "mix0": 2, "memq0": 3, "ffn0": 4, "kv": 5, "memq1": 6, "ffn1": 7, "final": 8}


def trunk(nc, a, o):
    (y_p, y_s, pool_p, pool_s, wk_p, wv_p, k_s, v_s, mem_k_p, mem_v_p) = o
    ctx = ExitStack()
    with ctx:
        def sb(name, shape, dt=F32):
            return ctx.enter_context(nc.sbuf_tensor(name, shape, dt))

        def sem(name):
            return ctx.enter_context(nc.semaphore(name))

        raw = sb("raw", [P, 2, BLK])
        whi = sb("whi", [P, NSPLIT, BLK], F32R)
        wlo = sb("wlo", [P, NSPLIT, BLK], F32R)
        x = sb("x", [P, DC, T])
        with nc.sbuf_tensor("xs", [P, DC, 2, T], F32R) as xs:
            pass
        xs_flat = sb("xs_flat", [P, DC * 2 * T])
        with nc.sbuf_tensor("hA", [P, 8, 2, T], F32R) as hA:
            pass
        hA_flat = sb("hA_flat", [P, 8 * 2 * T])
        with nc.sbuf_tensor("hB", [P, 8, 2, T], F32R) as hB:
            pass
        att = sb("att", [P, 16 * T])
        mKT = sb("mKT", [P, 2, NH_MEM, TP])
        mV = sb("mV", [P, 2, 2, MEMD])
        KT = sb("KT", [P, KVH, T])
        V = sb("V", [P, 2, MEMD])
        mask = sb("mask", [P, NG, 2 * P])
        ident = sb("ident", [P, P])
        ones = sb("ones", [P, P])
        gains = sb("gains", [P, 176])
        R = sb("R", [P, T])
        Rc = sb("Rc", [P, 3])
        ssq = sb("ssq", [P, 2, T])
        eps = sb("eps", [P, 1])
        small = sb("small", [P, 32])
        tmp = sb("tmp", [P, 2360])
        qd = att[:, 0:12 * T].rearrange("p (a g h t) -> p a g h t", a=2, g=NG, h=2)
        qm = att[:, 0:4 * T].rearrange("p (h t) -> p h t", h=NH_MEM)
        KTb = att[:, 0:2 * 12 * 129].rearrange("p (a k j) -> p a k j", a=2, k=12)
        KTm = att[:, 4 * T:4 * T + 2048].rearrange("p (a h j) -> p a h j", a=2, h=NH_MEM)
        QzD = att[:, 3168:3936].rearrange("p (g b k h) -> p g b k h", g=NG, b=TS, k=KVH)
        QzM = att[:, 3936:4064].rearrange("p (b h c) -> p b h c", b=TS, h=NH_MEM)
        gateF = tmp[:, 0:2 * T].rearrange("p (m t) -> p m t", m=2)
        siluF = tmp[:, 2 * T:4 * T].rearrange("p (m t) -> p m t", m=2)
        upF = tmp[:, 4 * T:6 * T].rearrange("p (m t) -> p m t", m=2)
        UP = TP + 16
        U, Ta, Tb = (tmp[:, i * 2 * UP:(i + 1) * 2 * UP].rearrange("p (m t) -> p m t", m=2) for i in range(3))
        wsum = tmp[:, 6 * UP:6 * UP + 128].rearrange("p (m b) -> p m b", m=DC)
        ut = tmp[:, 6 * UP + 128:6 * UP + 128 + DC * 23].rearrange("p (m t) -> p m t", m=DC)
        usm = tmp[:, 2200:2216].rearrange("p (m b) -> p m b", m=2)
        us2 = tmp[:, 2216:2232].rearrange("p (m b) -> p m b", m=2)
        invc = tmp[:, 2232:2296].rearrange("p (g t) -> p g t", g=4)
        stage = att[:, 0:1024]
        stage2 = att[:, 1024:2048]
        stage_u = tmp[:, 0:1024]
        gain_rows = att[:, 2048:2304]
        Vsm = att[0:TS, 2304:2816]
        S = tmp[:, 0:1152]
        Pn = tmp[:, 1152:1536]
        PT = tmp[:, 1536:1920]
        Pm = tmp[:, 0:1024].rearrange("p (a q j) -> p a q j", a=2, q=2)
        PTm = tmp[:, 1024:1536].rearrange("p (k t) -> p k t", k=2)
        PsD = tmp[:, 0:774].rearrange("p (b g j) -> p b g j", b=2, g=NG)
        PsDf = tmp[:, 0:774].rearrange("p (b j) -> p b j", b=2)
        PsM = tmp[:, 0:512].rearrange("p (b j) -> p b j", b=2)
        PTzD = tmp[:, 776:1544].rearrange("p (g b k h) -> p g b k h", g=NG, b=TS, k=KVH)
        PTzM = tmp[:, 1808:2064].rearrange("p (k b h c) -> p k b h c", k=2, b=TS, h=NH_MEM)
        Os = tmp[:, 1552:1808].rearrange("p (b d) -> p b d", b=2)
        Vrep = tmp[:, 2064:2320].rearrange("p (b d) -> p b d", b=2)
        std = sb("std", [P, T])
        stdc = sb("stdc", [P, 3])
        sq = sb("sq", [P, 2, T])

        acc = ctx.enter_context(nc.psum_tensor("acc", [P, 4, 512], F32))
        ab = ctx.enter_context(nc.psum_tensor("ab", [P, 4, 512], F32))

        consts_in, mask_in = sem("consts_in"), sem("mask_in")
        raw_in = [sem("raw_in0"), sem("raw_in1")]
        hi_ready, lo_ready = sem("hi_ready"), sem("lo_ready")
        half_used = sem("half_used")
        turned = sem("turned")
        acc_free = sem("acc_free")
        xs_ready = sem("xs_ready")
        h_ready = sem("h_ready")
        ssq_ready, stat_ready, std_ready = sem("ssq_ready"), sem("stat_ready"), sem("std_ready")
        silu_ready = sem("silu_ready")
        zeros_ready = sem("zeros_ready")
        s_ready, s_free = sem("s_ready"), sem("s_free")
        nb_ready, e_ready, p_ready = sem("nb_ready"), sem("e_ready"), sem("p_ready")
        t_ready, pt_ready = sem("t_ready"), sem("pt_ready")
        o_ready, os_ready = sem("o_ready"), sem("os_ready")
        scored = sem("scored")
        v_used = sem("v_used")
        cached_in = [sem(f"cached_in{i}") for i in range(7)]
        y_ready = sem("y_ready")
        stored = [sem("stored0"), sem("stored1")]
        out_done = sem("out_done")
        vs_done = sem("vs_done")
        vrep_in = sem("vrep_in")

        def counter():
            seen = {}

            def following(eng, which):
                seen[which.name] = seen.get(which.name, 0) + 1
                eng.wait_ge(which, seen[which.name])
            return following

        def kcols(w, k0, nk, c0, nco):
            return w[k0 * P:(k0 + nk) * P, c0:c0 + nco].rearrange("(k p) c -> p k c", p=P)

        def pair_block(w, j, i):
            return kcols(w, 8 * i, 8, 256 * j, 256)

        def quad_block(w, i, k0=0):
            return kcols(w, k0, 4, 512 * i, 512)

        def weight_source(n):
            name = [p for p, nb, _ in PHASES if nb and N0[p] <= n][-1]
            i = n - N0[name]
            if name[:4] == "memk":
                return pair_block(a["mem_w_k"][int(name[4])], i // 2, i % 2)
            if name[:4] == "memv":
                return kcols(a["mem_w_v"][int(name[4])], 4 * i, 4, 0, 512)
            if name == "win":
                return pair_block(a["pool_w_in"][0], i // 2, i % 2)
            if name == "grp":
                return a["pool_w_group"][0, i].rearrange("(k p) c -> p k c", p=P)
            if name == "wout":
                return pair_block(a["pool_w_out"][0], i // 2, i % 2)
            if name[:2] == "mq":
                return pair_block(a["mem_w_q"][int(name[2])], i // 2, i % 2)
            if name[:2] == "mo":
                return quad_block(a["mem_w_o"][int(name[2])], i)
            if name == "ksh":
                return pair_block(a["w_k_shared"], i // 2, i % 2)
            if name == "vsh":
                return kcols(a["w_v_shared"], 4 * i, 4, 0, 512)
            if name == "dq":
                hp, g = divmod(i // 2, NG)
                return kcols(a["dil_w_q"][0], 8 * (i % 2), 8, (g * NH + 2 * hp) * P, 256)
            if name == "do":
                return kcols(a["dil_w_o"][0], 0, 8, 256 * i, 256)
            layer, kind, part = int(name[1]), name[2], int(name[3])
            f0 = sum(PARTS[:part])
            if kind == "g":
                w = a["ffn_w_gate"] if i % 4 < 2 else a["ffn_w_up"]
                return kcols(w[layer], 8 * (i % 2), 8, (f0 + 2 * (i // 4)) * P, 256)
            if part < 2:
                return kcols(a["ffn_w_down"][layer], f0 + 8 * (i % 2), 8, 256 * (i // 2), 256)
            return kcols(a["ffn_w_down"][layer], f0 + 4 * (i % 3), 4, 512 * (i // 3), 512)

        def raw_as(slot, nk):
            return raw[:, slot, :].rearrange("p (k c) -> p k c", k=nk)

        def load_rows(eng, key):
            r = RAW_OF[key]
            _, kind, i = key
            s, done = r % 2, raw_in[r % 2]
            if kind == "mem":
                eng.dma_start(raw[:, s, :], a["mem_prompt"][0, i * P:(i + 1) * P, :]).then_inc(done, 16)
            elif kind == "x":
                if i < 2:
                    eng.dma_start(raw[:, s, :], a["x_prompt"][0, i * P:(i + 1) * P, :]).then_inc(done, 16)
                else:
                    eng.dma_start(raw[0:TS, s, :], a["x_sample"][:, 0, :]).then_inc(done, 16)
            else:
                eng.dma_start(raw[0:TS * NST, s, :], a["state_pool"][0].rearrange("b t c -> (b t) c")).then_inc(done, 16)

        def cached(key, j=0):
            s = CACHED_SLOT[key]
            if key[0][0] == "m":
                return hA_flat[:, 8 * T:8 * T + BLK] if s == 5 else xs_flat[:, s * BLK:(s + 1) * BLK]
            if s == 6:
                return (mKT[:, 0, 0:2, :], mKT[:, 0, 2:4, :])[j].rearrange("p h t -> p (h t)") if j < 2 else mV[:, 0, 0, :]
            return xs_flat[:, (3 * s + j) * MEMD:(3 * s + j + 1) * MEMD]

        def load_cached(eng, key):
            kind, i = key
            done = cached_in[CACHED_SLOT[key]]
            if kind[0] == "m":
                src = a["cache_mem_k" if kind[1] == "k" else "cache_mem_v"][int(kind[2]), 2 * i:2 * i + 2]
                eng.dma_start(cached(key).rearrange("p (b k c) -> p b k c", b=2, k=2),
                              src.rearrange("b (k p) h d -> p b k (h d)", p=P)).then_inc(done, 16)
            else:
                src = a["cache_win_k" if kind == "dk" else "cache_win_v"][i].rearrange("t h d -> t (h d)")
                for g, d in enumerate(DILS):
                    rows = src[PAST - WIN_KEYS * d:PAST, :].rearrange("(p q) c -> p q c", q=d)[:, 0, :]
                    eng.dma_start(cached(key, g), rows).then_inc(done, 16)

        def cached_landed(eng, key):
            eng.wait_ge(cached_in[CACHED_SLOT[key]], CACHED_LAND[key])

        def landed(eng, key):
            eng.wait_ge(raw_in[RAW_OF[key] % 2], LAND[key])

        def slot(key):
            return raw[:, RAW_OF[key] % 2, :]

        block = ctx.enter_context(nc.Block())

        @block.sync
        def _(eng):
            def slot_free(r):
                if r >= 2:
                    old = RAW[r - 2]
                    if old[0] == "w":
                        eng.wait_ge(hi_ready, old[1] + 1)
                        eng.wait_ge(lo_ready, old[1] + 1)
                    else:
                        eng.wait_ge(turned, ROWS_DONE[old])

            def load_block(n):
                r = RAW_OF[("w", n)]
                src = weight_source(n)
                slot_free(r)
                eng.dma_start(raw_as(r % 2, src.shape[1]), src).then_inc(raw_in[r % 2], 16)

            def loop_blocks(name, turns, per, source):
                with eng.Fori(0, turns) as i:
                    for j in range(per):
                        r = RAW_OF[("w", N0[name] + j)]
                        n = N0[name] + j - 2
                        eng.wait_ge(hi_ready, per * i + (n + 1))
                        eng.wait_ge(lo_ready, per * i + (n + 1))
                        src = source(i, j)
                        eng.dma_start(raw_as(r % 2, src.shape[1]), src).then_inc(raw_in[r % 2], 16)

            def cols(w, k0, nk, c):
                return w[k0 * P:(k0 + nk) * P, bass.ds(c, 256)].rearrange("(k p) c -> p k c", p=P)

            for j, name in enumerate(("norm_mem_kv", "norm_mix", "norm_mem_q", "norm_ffn")):
                eng.dma_start(gain_rows[32 * j:32 * (j + 1), 0:P], a[name].rearrange("l (m p) -> (l m) p", p=P)).then_inc(consts_in, 16)
            for j, name in enumerate(("norm_kv", "norm_final")):
                eng.dma_start(gain_rows[16 * j:16 * (j + 1), P:2 * P], a[name].rearrange("(m p) -> m p", p=P)).then_inc(consts_in, 16)
            eng.dma_start(gain_rows[32:48, P:2 * P], a["pool_scale"].rearrange("l (m p) -> (l m) p", p=P)).then_inc(consts_in, 16)
            eng.dma_start(ident[:, :], a["c_ident"]).then_inc(consts_in, 16)
            eng.dma_start(invc, a["c_inv"]).then_inc(consts_in, 16)

            in_loop = {}
            for l in range(2):
                for part in range(3):
                    in_loop[f"f{l}g{part}"] = (PARTS[part] // 2, 4)
                    if part < 2:
                        in_loop[f"f{l}d{part}"] = (4, 4)
            r = 0
            while r < len(RAW):
                key = RAW[r]
                if key[0] == "s":
                    slot_free(r)
                    load_rows(eng, key)
                    r += 1
                    continue
                n = key[1]
                name = [p for p, nb, _ in PHASES if nb and N0[p] <= n][-1]
                if name in in_loop and n == N0[name]:
                    turns, per = in_loop[name]
                    l, part = int(name[1]), int(name[3])
                    f0 = sum(PARTS[:part])
                    if name[2] == "g":
                        loop_blocks(name, turns, per, lambda i, j: cols(
                            a["ffn_w_gate" if j < 2 else "ffn_w_up"][l], 8 * (j % 2), 8, i * 256 + f0 * P))
                    else:
                        loop_blocks(name, turns, per, lambda i, j: cols(
                            a["ffn_w_down"][l], f0 + 8 * (j % 2), 8, i * 512 + 256 * (j // 2)))
                    r += turns * per
                    continue
                load_block(n)
                r += 1

        @block.scalar
        def _(eng):
            at = [0]
            following = counter()

            def hi(n, more=0):
                r = RAW_OF[("w", n)]
                eng.wait_ge(raw_in[r % 2], more * 8 + LAND[("w", n)])
                if n >= NSPLIT:
                    eng.wait_ge(half_used, more * 2 + 2 * (n - NSPLIT + 1))
                nc.scalar.activation(whi[:, n % NSPLIT, :], raw[:, r % 2, :], ACT.Copy).then_inc(hi_ready, 1)

            def upto(n):
                while at[0] <= min(n, NBLOCKS - 1):
                    hi(at[0])
                    at[0] += 1

            def root(k, width=T, cols=0):
                eng.wait_ge(stat_ready, k)
                last = nc.scalar.activation(std[:, 0:width], ab[:, 3, 0:width], ACT.Sqrt, bias=eps[:, :], scale=1.0 / D)
                if cols:
                    last = nc.scalar.activation(stdc[:, 0:2], ab[:, 3, 300:302], ACT.Sqrt, bias=eps[:, :], scale=1.0 / D)
                if cols == 3:
                    last = nc.scalar.activation(stdc[0:TS, 2:3], ab[0:TS, 3, 302:303], ACT.Sqrt, bias=eps[0:TS, :],
                                                scale=1.0 / D)
                last.then_inc(std_ready, 1)

            def softmax_exp(parts):
                following(eng, nb_ready)
                for out, in_, b, d in parts:
                    last = nc.scalar.activation(out, in_, ACT.Exp, bias=small[:, b:b + 1], scale=SCALE,
                                                accum_out=small[:, d:d + 1])
                last.then_inc(e_ready, 1)

            def copy_item(g, out, in_):
                eng.wait_ge(acc_free, g)
                nc.scalar.copy(out, in_).then_inc(acc_free, 1)

            def mem_attention(l):
                gk = G0[f"mk{l}"]

                def head_exp(h):
                    s = h % 2
                    softmax_exp([(Pm[:, s, q, :], ab[:, s, q * TP:(q + 1) * TP], 2 * s + q, 4 + 2 * s + q)
                                 for q in range(2)])

                def samples_exp(q):
                    softmax_exp([(PsM[:, q, :], ab[:, q, 0:TP], 16 + q, 20 + q)])

                def keys(b):
                    eng.wait_ge(turned, TURN0[f"mk{l}"] + b + 1)
                    if b >= 2:
                        eng.wait_ge(scored, SC0[f"m{l}"] + b - 1)
                    copy_item(gk + b, KTm[:, b % 2].rearrange("p h j -> p (h j)"),
                              acc[:, 2 * ((gk + b) % 2):2 * ((gk + b) % 2) + 2, :].rearrange("p b c -> p (b c)"))

                upto(N0[f"mo{l}"] + 2)
                head_exp(0)
                head_exp(1)
                keys(0)
                head_exp(2)
                keys(1)
                head_exp(3)
                keys(2)
                upto(N0[f"mo{l}"] + 3)
                keys(3)
                keys(4)
                samples_exp(0)
                for b in range(5, TS):
                    keys(b)
                samples_exp(1)

            def ffn(l):
                for part in range(3):
                    n, g, turns = N0[f"f{l}g{part}"], G0[f"f{l}g{part}"], PARTS[part] // 2

                    def turn(i):
                        hi(n + 2, 4 * i)
                        if part == 0 and isinstance(i, int):
                            root(STAT[f"ffn{l}"])
                            nc.scalar.preload_act_table(ACT.Silu)
                        hi(n + 3, 4 * i)
                        eng.wait_ge(acc_free, 2 * i + (g + 1))
                        nc.scalar.activation(siluF, gateF, ACT.Silu).then_inc(silu_ready, 1)
                        hi(n + 4, 4 * i)
                        hi(n + 5, 4 * i)

                    upto(n + 1)
                    if part == 0:
                        turn(0)
                    with eng.Fori(1 if part == 0 else 0, turns) as i:
                        turn(i)
                    if part < 2:
                        nd = N0[f"f{l}d{part}"]
                        with eng.Fori(0, 4) as i:
                            for j in range(4):
                                hi(nd + 2 + j, 4 * i)
                        at[0] = nd + 18
                    else:
                        at[0] = n + 4 * turns + 2

            eng.dma_start(mask[:, :, :], a["c_mask"]).then_inc(mask_in, 16)
            eng.wait_ge(zeros_ready, 1)
            upto(N0["memk0"] + 2)
            root(STAT["mem"], TP, 2)
            upto(N0["win"] + 2)
            root(STAT["mix0"])
            upto(N0["mq0"] + 2)
            root(STAT["memq0"])
            mem_attention(0)
            ffn(0)
            upto(N0["ksh"] + 2)
            root(STAT["kv"], T, 3)
            dil = [(S[:, 0:768], S[:, 0:768], 0, 4), (S[:, 768:1152], S[:, 768:1152], 1, 5)]
            for hp in range(4):
                for j in range(6):
                    upto(N0["dq"] + 6 * hp + j + 2)
                    if hp and j in (0, 2):
                        softmax_exp(dil)
            gk = G0["dk"]

            def dil_keys(b):
                if b == 1:
                    eng.wait_ge(s_ready, NH_MEM + NH)
                if b >= 2:
                    eng.wait_ge(scored, SC0["dil"] + b - 1)
                nc.scalar.copy(KTb[:, b % 2, :, P].rearrange("p (g k) -> p g k", g=NG),
                               KT[:, :, TP + b].rearrange("p (o k) -> p o k", o=1).to_broadcast([P, NG, KVH]))
                for part in range(2):
                    g = gk + 2 * b + part
                    eng.wait_ge(turned, TURN0["dk"] + 2 * b + part + 1)
                    copy_item(g, KTb[:, b % 2, 6 * part:6 * part + 6, 0:P],
                              acc[:, 2 * (g % 2):2 * (g % 2) + 2, :].rearrange("p b (s c) -> p (b s) c", c=P)[:, 0:6, :])

            def dil_samples_exp(q):
                softmax_exp([(PsDf[:, q, :], ab[:, q, 0:387], 16 + q, 20 + q)])

            upto(N0["do"] + 2)
            dil_keys(0)
            softmax_exp(dil)
            upto(N0["do"] + 3)
            dil_keys(1)
            softmax_exp(dil)
            for b in range(2, 5):
                dil_keys(b)
            dil_samples_exp(0)
            for b in range(5, TS):
                dil_keys(b)
            dil_samples_exp(1)
            upto(N0["mq1"] + 2)
            root(STAT["memq1"])
            mem_attention(1)
            ffn(1)
            upto(NBLOCKS - 1)
            root(STAT["final"])

        @block.tensor
        def _(eng):
            mm = nc.tensor.matmul
            following = counter()

            def block_ready(n, more=0):
                eng.wait_ge(hi_ready, more + (n + 1))
                eng.wait_ge(lo_ready, more + (n + 1))

            def item_free(g, more=0):
                if g >= 2:
                    eng.wait_ge(acc_free, more + (g - 1))

            def products(out, s, col, tile, first, last):
                hi_, lo_ = tile
                w_hi, w_lo = whi[:, s, col:col + P], wlo[:, s, col:col + P]
                mm(out, w_hi, hi_, start=first, stop=False)
                mm(out, w_hi, lo_, start=False, stop=False)
                return mm(out, w_lo, hi_, start=False, stop=last)

            def xtile(k, width=T):
                return xs[:, k, 0, 0:width], xs[:, k, 1, 0:width]

            def htile(k, width=T):
                h, k = (hA, k) if k < 8 else (hB, k - 8)
                return h[:, k, 0, 0:width], h[:, k, 1, 0:width]

            def xs_wait(gen):
                return lambda k: eng.wait_ge(xs_ready, 16 * GEN[gen] + k + 1)

            def h_wait(base):
                return lambda k: eng.wait_ge(h_ready, base + k // 2 + 1) if k % 2 == 0 else None

            def pair_item(n, g, nb, tile, ready=None, nmore=0, gmore=0, width=T, after_first=None):
                item_free(g, gmore)
                for i in range(nb):
                    block_ready(n + i, nmore)
                    for k in range(8):
                        if ready is not None:
                            ready(8 * i + k)
                        for m in range(2):
                            last = products(acc[:, 2 * (g % 2) + m, 0:width], (n + i) % NSPLIT, k * 256 + m * P,
                                            tile(8 * i + k, width), i == k == 0, i == nb - 1 and k == 7)
                        if k % 4 == 3:
                            last.then_inc(half_used, 1)
                    if i == 0 and after_first is not None:
                        after_first()

            def pair_phase(name, items, nb, tile, ready=None, width=T, after_first=None):
                for j in range(items):
                    pair_item(N0[name] + nb * j, G0[name] + j, nb, tile, ready if j == 0 else None, width=width,
                              after_first=after_first if j == 0 else None)

            def pair_loop(name, turns, items, tile, ready=None):
                with eng.Fori(0, turns) as i:
                    for j in range(items):
                        pair_item(N0[name] + 2 * j, G0[name] + j, 2, tile, ready if j == 0 else None,
                                  nmore=2 * items * i, gmore=items * i)

            def quad_item(n, g, nb, tile, ready, after_first=None):
                for i in range(nb):
                    block_ready(n + i)
                    for m in range(4):
                        if i == 0 and m % 2 == 0:
                            item_free(g + m // 2)
                        for k in range(4):
                            if m == 0 and ready is not None:
                                ready(4 * i + k)
                            last = products(acc[:, 2 * ((g + m // 2) % 2) + m % 2, 0:T], (n + i) % NSPLIT,
                                            k * 512 + m * P, tile(4 * i + k), i == k == 0, i == nb - 1 and k == 3)
                        if m % 2 == 1:
                            last.then_inc(half_used, 1)

            def value_phase(name, samples):
                n, g = N0[name], G0[name]
                item_free(g)
                if samples:
                    item_free(g + 1)
                for i in range(4):
                    block_ready(n + i)
                    s = (n + i) % NSPLIT
                    for c in range(3 if samples else 2):
                        out, t0, tn = (acc[:, 2 * (g % 2) + c, :], c * P, P) if c < 2 else (acc[0:TS, 2 * ((g + 1) % 2), :], TP, TS)
                        for k in range(4):
                            x_hi, x_lo = (xs[:, 4 * i + k, part, t0:t0 + tn] for part in range(2))
                            w_hi, w_lo = whi[:, s, k * 512:(k + 1) * 512], wlo[:, s, k * 512:(k + 1) * 512]
                            mm(out, x_hi, w_hi, start=i == k == 0, stop=False)
                            mm(out, x_hi, w_lo, start=False, stop=False)
                            last = mm(out, x_lo, w_hi, start=False, stop=i == 3 and k == 3)
                        if c == 0 or c == (2 if samples else 1):
                            last.then_inc(half_used, 1)

            def turn_item(g, parts):
                item_free(g)
                for rows, j, n, src in parts:
                    last = nc.tensor.transpose(acc[0:rows, 2 * (g % 2) + j // 4, (j % 4) * P:(j % 4) * P + n],
                                               src, ident[0:src.shape[0], 0:src.shape[0]])
                last.then_inc(turned, 1)

            def statistics(k, width=T, cols=0):
                eng.wait_ge(ssq_ready, k)
                for m in range(2):
                    last = mm(ab[:, 3, 0:width], ones[:, :], ssq[:, m, 0:width], start=m == 0, stop=m == 1)
                for c in range(cols):
                    tn = P if c < 2 else TS
                    for m in range(2):
                        last = mm(ab[0:tn, 3, 300 + c:301 + c], ssq[:, m, c * P:c * P + tn], ones[:, 0:1],
                                  start=m == 0, stop=m == 1)
                last.then_inc(stat_ready, 1)

            def mem_attention(l):
                g = G0[f"mq{l}"]
                h0 = H0[f"m{l}"]
                gk = G0[f"mk{l}"]

                def scores(h):
                    eng.wait_ge(acc_free, g + h // 2 + 1)
                    if h >= 2:
                        eng.wait_ge(e_ready, E0[f"m{l}"] + h - 1)
                    for q in range(2):
                        last = mm(ab[:, h % 2, q * TP:(q + 1) * TP], qm[:, h, q * P:(q + 1) * P], mKT[:, l, h, :],
                                  start=True, stop=True)
                    last.then_inc(s_ready, 1)

                def turn_probabilities(h):
                    following(eng, p_ready)
                    for k in range(2):
                        for q in range(2):
                            last = nc.tensor.transpose(ab[:, 2, k * TP + q * P:k * TP + (q + 1) * P],
                                                       Pm[:, h % 2, q, k * P:(k + 1) * P], ident[:, :])
                    last.then_inc(t_ready, 1)

                def weigh(h):
                    following(eng, pt_ready)
                    if h:
                        eng.wait_ge(h_ready, h0 + h)
                    for k in range(2):
                        last = mm(ab[:, 3, 0:TP], mV[:, l, k, h * P:(h + 1) * P], PTm[:, k, :], start=k == 0, stop=k == 1)
                    last.then_inc(o_ready, 1)

                def turn_keys(b):
                    key = (f"mk{l}", b // 2)
                    cached_landed(eng, key)
                    rows = cached(key).rearrange("p (b k c) -> p b k c", b=2, k=2)
                    turn_item(gk + b, [(P, 2 * h + k, P, rows[:, b % 2, k, h * P:(h + 1) * P])
                                       for h in range(NH_MEM) for k in range(2)])

                def sample_scores(b):
                    eng.wait_ge(acc_free, gk + b + 1)
                    if b % 4 == 0:
                        eng.wait_ge(e_ready, E0[f"m{l}"] + 3 + b // 4)
                    r = 32 * (b % 4)
                    for h in range(NH_MEM):
                        last = mm(ab[r:r + NH_MEM, b // 4, 0:TP], QzM[:, b, h, :],
                                  KTm[:, b % 2, h, :], start=h == 0, stop=h == NH_MEM - 1)
                    last.then_inc(scored, 1)

                def turn_samples(q):
                    following(eng, p_ready)
                    for k in range(2):
                        last = nc.tensor.transpose(ab[:, 2, k * P:(k + 1) * P], PsM[:, q, k * P:(k + 1) * P], ident[:, :])
                    last.then_inc(t_ready, 1)

                def sample_values(b):
                    if b % 4 == 0:
                        following(eng, pt_ready)
                    if b == 0:
                        eng.wait_ge(h_ready, h0 + NH_MEM)
                    key = (f"mv{l}", b // 2)
                    cached_landed(eng, key)
                    rows = cached(key).rearrange("p (b k c) -> p b k c", b=2, k=2)
                    r = 32 * (b % 4)
                    for k in range(2):
                        for h in range(NH_MEM):
                            last = mm(ab[r:r + NH_MEM, (3, 0)[b // 4], 0:P], PTzM[:, k, b, h, :],
                                      rows[:, b % 2, k, h * P:(h + 1) * P], start=k == h == 0, stop=k == 1 and h == NH_MEM - 1)
                    last.then_inc(v_used, 1)

                def turn_outputs(q):
                    following(eng, os_ready)
                    nc.tensor.transpose(ab[:, 1 + q, 0:P], Os[:, q, :], ident[:, :]).then_inc(t_ready, 1)

                pair_item(N0[f"mq{l}"], g, 2, xtile, xs_wait(f"memq{l}"), after_first=lambda: statistics(STAT[f"memq{l}"]))
                pair_item(N0[f"mq{l}"] + 2, g + 1, 2, xtile, after_first=lambda: (scores(0), scores(1)))
                turn_keys(0)
                turn_probabilities(0)
                scores(2)
                turn_keys(1)
                weigh(0)
                turn_probabilities(1)
                scores(3)
                turn_keys(2)
                weigh(1)
                sample_scores(0)
                turn_probabilities(2)
                turn_keys(3)
                sample_scores(1)
                weigh(2)
                turn_probabilities(3)
                sample_scores(2)
                weigh(3)
                turn_keys(4)
                sample_scores(3)
                turn_keys(5)
                sample_scores(4)
                turn_keys(6)
                turn_samples(0)
                sample_scores(5)
                turn_keys(7)
                sample_scores(6)
                sample_values(0)
                sample_values(1)
                sample_scores(7)
                sample_values(2)
                sample_values(3)
                turn_samples(1)
                sample_values(4)
                sample_values(5)
                turn_outputs(0)
                sample_values(6)
                sample_values(7)
                turn_outputs(1)

            hd = H0["dil"]

            def dil_scores(h):
                a_, hh, kv = (h // 2) % 2, h % 2, h // 2
                eng.wait_ge(acc_free, G0["dq"] + 3 * (h // 2) + 3)
                if h:
                    eng.wait_ge(s_free, h)
                for g in range(NG):
                    mm(ab[:, g // 2, (g % 2) * TP:(g % 2 + 1) * TP], qd[:, a_, g, hh, P:TP], KT[:, kv, 0:TP],
                       start=True, stop=True)
                for g in range(NG):
                    last = mm(ab[:, 2, g * P:(g + 1) * P], qd[:, a_, g, hh, 0:P], KT[:, kv, 0:P], start=True, stop=True)
                last.then_inc(s_ready, 1)

            def dil_turn(h):
                following(eng, p_ready)
                if h:
                    eng.wait_ge(h_ready, hd + h)
                for j, c in enumerate((TP, 0, P)):
                    last = nc.tensor.transpose(ab[:, 3, j * P:(j + 1) * P], Pn[:, c:c + P], ident[:, :])
                last.then_inc(t_ready, 1)

            def dil_out(h):
                following(eng, pt_ready)
                v = slice((h // 2) * P, (h // 2 + 1) * P)
                mm(ab[:, 3, 0:TP], V[:, 0, v], PT[:, 0:TP], start=True, stop=False)
                mm(ab[:, 3, P:TP], V[:, 1, v], PT[:, TP:TP + P], start=False, stop=True).then_inc(o_ready, 1)

            gk = G0["dk"]

            def dil_turn_keys(b):
                cached_landed(eng, ("dk", b))
                for part in range(2):
                    turn_item(gk + 2 * b + part, [(P, i, P, cached(("dk", b), j // 4)[:, (j % 4) * P:(j % 4 + 1) * P])
                                                  for i, j in enumerate(range(6 * part, 6 * part + 6))])

            def dil_sample_scores(b):
                eng.wait_ge(acc_free, gk + 2 * b + 2)
                if b == 0:
                    eng.wait_ge(s_free, NH)
                r = 32 * (b % 4)
                for g in range(NG):
                    for kv in range(KVH):
                        last = mm(ab[r:r + NH, b // 4, g * 129:(g + 1) * 129], QzD[:, g, b, kv, :],
                                  KTb[:, b % 2, KVH * g + kv, :], start=g == kv == 0,
                                  stop=kv == KVH - 1, skip_group_check=True)
                last.then_inc(scored, 1)

            def dil_turn_samples(q):
                following(eng, p_ready)
                for g in range(NG):
                    last = nc.tensor.transpose(ab[:, 2, g * P:(g + 1) * P], PsD[:, q, g, 0:P], ident[:, :])
                last.then_inc(t_ready, 1)

            def dil_sample_values(b):
                if b % 4 == 0:
                    following(eng, pt_ready)
                if b == 0:
                    eng.wait_ge(h_ready, hd + NH)
                cached_landed(eng, ("dv", b))
                r = 32 * (b % 4)
                for g in range(NG):
                    for kv in range(KVH):
                        last = mm(ab[r:r + NH, (3, 0)[b // 4], 0:P], PTzD[:, g, b, kv, :],
                                  cached(("dv", b), g)[:, kv * P:(kv + 1) * P], start=g == kv == 0,
                                  stop=g == NG - 1 and kv == KVH - 1)
                last.then_inc(v_used, 1)

            def dil_turn_outputs(q):
                following(eng, os_ready)
                nc.tensor.transpose(ab[:, 1 + q, 0:P], Os[:, q, :], ident[:, :]).then_inc(t_ready, 1)

            def dil_last():
                dil_scores(6)
                dil_turn_keys(0)
                dil_turn(6)
                dil_out(6)
                dil_scores(7)
                dil_turn_keys(1)
                dil_sample_scores(0)
                dil_turn(7)
                dil_turn_keys(2)
                dil_out(7)
                dil_sample_scores(1)
                for b in range(2, 5):
                    dil_turn_keys(b + 1)
                    dil_sample_scores(b)
                dil_turn_keys(6)
                dil_turn_samples(0)
                dil_sample_scores(5)
                dil_turn_keys(7)
                dil_sample_scores(6)
                dil_sample_values(0)
                dil_sample_values(1)
                dil_sample_scores(7)
                dil_sample_values(2)
                dil_sample_values(3)
                dil_turn_samples(1)
                dil_sample_values(4)
                dil_sample_values(5)
                dil_turn_outputs(0)
                dil_sample_values(6)
                dil_sample_values(7)
                dil_turn_outputs(1)

            eng.wait_ge(consts_in, CONSTS)
            eng.wait_ge(zeros_ready, 1)
            turn_item(G0["xload"], [(P, 0, P, gain_rows[:, 0:P]), (P, 1, 48, gain_rows[0:48, P:2 * P])])
            for c in range(2):
                landed(eng, ("s", "mem", c))
                for j in range(2):
                    turn_item(G0["memload"] + 2 * c + j, [(P, m, P, slot(("s", "mem", c))[:, (8 * j + m) * P:(8 * j + m + 1) * P])
                                                          for m in range(8)])
            for l in range(2):
                pair_phase(f"memk{l}", 2, 2, xtile, xs_wait(f"memkv{l}"), TP,
                           (lambda: statistics(STAT["mem"], TP, 2)) if l == 0 else None)
                if l == 1:
                    for c in range(3):
                        landed(eng, ("s", "x", c))
                        rows = slot(("s", "x", c))
                        if c < 2:
                            for j in range(2):
                                turn_item(G0["xt"] + 2 * c + j, [(P, m, P, rows[:, (8 * j + m) * P:(8 * j + m + 1) * P])
                                                                 for m in range(8)])
                        else:
                            item_free(G0["xt"] + 4)
                            for m in range(DC):
                                last = nc.tensor.transpose(acc[:, 2 * ((G0["xt"] + 4) % 2), TS * m:TS * (m + 1)],
                                                           rows[0:TS, m * P:(m + 1) * P], ident[0:TS, 0:TS])
                            last.then_inc(turned, 1)
                    landed(eng, ("s", "state", 0))
                    for j in range(2):
                        turn_item(G0["st"] + j, [(P, m, TS * NST, slot(("s", "state", 0))[0:TS * NST, (8 * j + m) * P:(8 * j + m + 1) * P])
                                                 for m in range(8)])
                value_phase(f"memv{l}", False)
                eng.wait_ge(acc_free, G0[f"memk{l}"] + 2)
                turn_item(G0[f"memkt{l}"], [(P, 4 * c + h, P, mKT[:, l, h, c * P:(c + 1) * P])
                                            for c in range(2) for h in range(NH_MEM)])
            pair_phase("win", 8, 2, xtile, xs_wait("mix0"), after_first=lambda: statistics(STAT["mix0"]))
            eng.wait_ge(h_ready, 8)
            for j in range(2):
                turn_item(G0["ut"] + j, [(23, m, P, ut[:, 8 * j + m, :]) for m in range(8)])
            for gi in range(4):
                quad_item(N0["grp"] + gi, G0["grp"] + 2 * gi, 1, lambda k, gi=gi: htile(4 * gi + k), None)
            pair_phase("wout", 8, 2, htile, h_wait(H0["z"]))

            def ffn(l):
                for part in range(3):
                    g_, d_ = f"f{l}g{part}", f"f{l}d{part}"
                    turns = PARTS[part] // 2
                    if part == 0:
                        pair_item(N0[g_], G0[g_], 2, xtile, xs_wait(f"ffn{l}"), after_first=lambda: statistics(STAT[f"ffn{l}"]))
                        pair_item(N0[g_] + 2, G0[g_] + 1, 2, xtile)
                        with eng.Fori(1, turns) as i:
                            for j in range(2):
                                pair_item(N0[g_] + 2 * j, G0[g_] + j, 2, xtile, nmore=4 * i, gmore=2 * i)
                    else:
                        pair_loop(g_, turns, 2, xtile)
                    base = H0[f"f{l}"] + sum(PARTS[:part]) // 2
                    if part < 2:
                        pair_loop(d_, 4, 2, htile, h_wait(base))
                    else:
                        for q in range(4):
                            quad_item(N0[d_] + 3 * q, G0[d_] + 2 * q, 3, htile, h_wait(base) if q == 0 else None)

            def mem_layer(l):
                mem_attention(l)
                eng.wait_ge(h_ready, H0[f"m{l}"] + 5)
                for i in range(4):
                    quad_item(N0[f"mo{l}"] + i, G0[f"mo{l}"] + 2 * i, 1, htile, None)
                ffn(l)

            mem_layer(0)
            pair_phase("ksh", 2, 2, xtile, xs_wait("kv"), after_first=lambda: statistics(STAT["kv"], T, 3))
            value_phase("vsh", True)
            eng.wait_ge(acc_free, G0["ksh"] + 2)
            turn_item(G0["kt"], [(P, 4 * c + h, P, KT[:, h, c * P:(c + 1) * P]) for c in range(2) for h in range(KVH)])
            turn_item(G0["kt"] + 1, [(TS, h, P, KT[:, h, TP:T]) for h in range(KVH)])

            steps = [lambda h: dil_scores(h), lambda h: dil_turn(h), lambda h: (dil_out(h), dil_scores(h + 1)),
                     lambda h: dil_turn(h + 1), lambda h: dil_out(h + 1)]
            for hp in range(4):
                for g in range(NG):
                    n, gi = N0["dq"] + 6 * hp + 2 * g, G0["dq"] + 3 * hp + g
                    first = (lambda hp=hp, g=g: steps[2 * g](2 * hp - 2)) if hp else None
                    pair_item(n, gi, 2, xtile, xs_wait("mix1") if hp == g == 0 else None, after_first=first)
                    if hp and g < 2:
                        steps[2 * g + 1](2 * hp - 2)
            dil_last()
            eng.wait_ge(h_ready, hd + NH + 1)
            pair_phase("do", 8, 1, htile)
            mem_layer(1)
            statistics(STAT["final"])
            for c in range(3):
                for j in range(2 if c < 2 else 1):
                    g = G0["y"] + 2 * c + j
                    eng.wait_ge(y_ready, 1)
                    if c < 2:
                        turn_item(g, [(P, m, P, x[:, 8 * j + m, c * P:(c + 1) * P]) for m in range(8)])
                    else:
                        for half in range(2):
                            turn_item(g + half, [(TS, m, P, x[:, 8 * half + m, TP:T]) for m in range(8)])

        @block.vector
        def _(eng):
            v = nc.vector
            at = [0]
            following = counter()

            def lo(n, more=0):
                r = RAW_OF[("w", n)]
                eng.wait_ge(raw_in[r % 2], more * 8 + LAND[("w", n)])
                eng.wait_ge(hi_ready, more + (n + 1))
                if n >= NSPLIT:
                    eng.wait_ge(half_used, more * 2 + 2 * (n - NSPLIT + 1))
                v.tensor_tensor(wlo[:, n % NSPLIT, :], raw[:, r % 2, :], whi[:, n % NSPLIT, :].bitcast(F32),
                                ALU.subtract).then_inc(lo_ready, 1)

            def upto(n):
                while at[0] <= min(n, NBLOCKS - 1):
                    lo(at[0])
                    at[0] += 1

            def block_used(n, more=0, half=2):
                eng.wait_ge(half_used, more * 2 + (2 * n + half))

            def banks(g, width=T):
                return acc[:, 2 * (g % 2):2 * (g % 2) + 2, 0:width]

            def columns(g):
                return acc[:, 2 * (g % 2):2 * (g % 2) + 2, :].rearrange("p b (s c) -> p (b s) c", c=P)

            def twice(ap):
                return ap.rearrange("p (o t) -> p o t", o=1).to_broadcast([P, 2, ap.shape[1]])

            def rms(k, width=T, cols=0):
                eng.wait_ge(std_ready, k)
                last = v.reciprocal(R[:, 0:width], std[:, 0:width])
                if cols:
                    v.reciprocal(Rc[:, 0:2], stdc[:, 0:2])
                if cols == 3:
                    v.reciprocal(Rc[0:TS, 2:3], stdc[0:TS, 2:3])
                eng.drain()

            def split_x(gain, m0, width=T):
                for m in (m0, m0 + 1):
                    v.tensor_scalar(xs[:, m, 0, 0:width], x[:, m, 0:width], gains[:, gain + m:gain + m + 1], None, ALU.mult)
                eng.drain()
                for m in (m0, m0 + 1):
                    v.scalar_tensor_tensor(out=xs[:, m, 1, 0:width], in0=x[:, m, 0:width], scalar=gains[:, gain + m:gain + m + 1],
                                           in1=xs[:, m, 0, 0:width].bitcast(F32), op0=ALU.mult, op1=ALU.subtract).then_inc(xs_ready, 1)

            def add_x(g, m0, gain=None):
                dst = x[:, m0:m0 + 2, :]
                v.tensor_tensor(dst, banks(g), dst, ALU.add).then_inc(acc_free, 1)
                eng.drain()
                if gain is not None:
                    split_x(gain, m0)

            def split_h(h, t, src, tn=2):
                v.tensor_copy(h[:, t, 0, :], src)
                eng.drain()
                v.tensor_tensor(h[:, t, 1, :], src, h[:, t, 0, :].bitcast(F32), ALU.subtract).then_inc(h_ready, 1)

            def stage_item(g, k, rows, width=2 * 512):
                if k in (2, 3):
                    eng.wait_ge(stored[k % 2 ^ 1], STORED[k - 1])
                    eng.drain()
                dst = stage_u if k in (2, 3) else (stage, stage2)[k % 2]
                flat = acc[0:rows, 2 * (g % 2):2 * (g % 2) + 2, :].rearrange("p b c -> p (b c)")
                v.tensor_copy(dst[0:rows, 0:width], flat[:, 0:width]).then_inc(acc_free, 1)

            v.memset(ones[:, :], 1.0)
            v.memset(eps[:, :], EPS)
            v.memset(ab[:, :, :], 0.0).then_inc(zeros_ready, 1)
            eng.wait_ge(turned, 1)
            v.tensor_copy(gains[:, :], acc[:, 0, 0:176]).then_inc(acc_free, 1)
            for c in range(2):
                for j in range(2):
                    eng.wait_ge(turned, TURN0["memload"] + 2 * c + j + 1)
                    v.tensor_copy(x[:, 8 * j:8 * j + 8, c * P:(c + 1) * P], columns(G0["memload"] + 2 * c + j)).then_inc(acc_free, 1)
            eng.drain()
            for l in range(2):
                upto(N0[f"memk{l}"] + 1)
                if l == 1:
                    block_used(N0["memv0"] + 3)
                for m in range(0, DC, 2):
                    split_x(GAIN["memkv"][l], m, TP)
                upto(N0[f"memk{l}"] + 2)
                if l == 0:
                    rms(STAT["mem"], TP, 2)
                upto(N0[f"memk{l}"] + 3)
                for j in range(2):
                    block_used(N0[f"memk{l}"] + 2 * j + 1)
                    g = G0[f"memk{l}"] + j
                    v.tensor_tensor(mKT[:, l, 2 * j:2 * j + 2, :], banks(g, TP), twice(R[:, 0:TP]), ALU.mult).then_inc(acc_free, 1)
                    if l == 0:
                        upto(N0["memv0"] + 2 * j + 1)
                if l == 1:
                    eng.drain()
                    for c in range(3):
                        for j in range(2 if c < 2 else 1):
                            g = G0["xt"] + 2 * c + j
                            eng.wait_ge(turned, TURN0["xt"] + 2 * c + j + 1)
                            if c < 2:
                                v.tensor_copy(x[:, 8 * j:8 * j + 8, c * P:(c + 1) * P], columns(g)).then_inc(acc_free, 1)
                            else:
                                v.tensor_copy(x[:, :, TP:T], acc[:, 2 * (g % 2), 0:P].rearrange("p (m b) -> p m b", b=TS)).then_inc(acc_free, 1)
                    for j in range(2):
                        g = G0["st"] + j
                        eng.wait_ge(turned, TURN0["st"] + j + 1)
                        for q in range(2):
                            w = 2 << (2 * j + q)
                            rows = columns(g)[:, 4 * q:4 * q + 4, 0:TS * NST].rearrange("p s (b t) -> p s b t", t=NST)
                            last = v.tensor_reduce(wsum[:, 8 * j + 4 * q:8 * j + 4 * q + 4, :], rows[:, :, :, NST - (w - 1):NST],
                                                   AX.X, ALU.add)
                        last.then_inc(acc_free, 1)
                g = G0[f"memv{l}"]
                upto(N0[f"memv{l}"] + 3)
                block_used(N0[f"memv{l}"] + 3)
                for c in range(2):
                    last = v.tensor_scalar(mV[:, l, c, :], acc[:, 2 * (g % 2) + c, :], Rc[:, c:c + 1], None, ALU.mult)
                last.then_inc(acc_free, 1)
                eng.wait_ge(turned, TURN0[f"memkt{l}"] + 1)
                stage_item(G0[f"memkt{l}"], l, P)

            upto(N0["win"] + 1)
            v.memset(tmp[:, 0:6 * UP], 0.0)
            eng.drain()
            for m in range(0, DC, 2):
                split_x(GAIN["mix"][0], m)
            for k in range(2):
                eng.wait_ge(stored[k], STORED[k])
            for j in range(8):
                n, g = N0["win"] + 2 * j, G0["win"] + j
                upto(n + 2)
                if j == 0:
                    eng.wait_ge(consts_in, CONSTS)
                    rms(STAT["mix0"])
                upto(n + 3)
                block_used(n + 1)
                gi = j // 2
                w = 2 << gi
                b = banks(g)
                v.tensor_tensor(U[:, :, 16:UP], b[:, :, 0:TP], twice(R[:, 0:TP]), ALU.mult)
                v.tensor_tensor(usm, b[:, :, TP:T], twice(R[:, TP:T]), ALU.mult).then_inc(acc_free, 1)
                eng.drain()
                v.tensor_copy(ut[:, 2 * j:2 * j + 2, 0:NST], U[:, :, UP - NST:UP])
                v.tensor_copy(ut[:, 2 * j:2 * j + 2, NST:NST + TS], usm)
                src, step = U, 1
                for i in range(gi + 1):
                    dst, first = (Ta, Tb)[i % 2], 2 * step - 1
                    v.tensor_tensor(dst[:, :, first:UP], src[:, :, first:UP], src[:, :, first - step:UP - step], ALU.add)
                    eng.drain()
                    src, step = dst, 2 * step
                for m in range(2):
                    v.tensor_tensor(src[:, m, 16:32], src[:, m, 16:32], invc[:, gi, :], ALU.mult)
                v.tensor_tensor(us2, usm, wsum[:, 2 * j:2 * j + 2, :], ALU.add)
                eng.drain()
                pooled = (Tb if src is Ta else Ta)[:, :, 0:T]
                v.scalar_tensor_tensor(out=pooled[:, :, 0:TP], in0=src[:, :, 16:UP], scalar=1.0 / w, in1=U[:, :, 16:UP],
                                       op0=ALU.mult, op1=ALU.subtract)
                v.scalar_tensor_tensor(out=pooled[:, :, TP:T], in0=us2, scalar=1.0 / w, in1=usm, op0=ALU.mult, op1=ALU.subtract)
                eng.drain()
                split_h(hA if j < 4 else hB, slice(2 * j % 8, 2 * j % 8 + 2), pooled)
                eng.drain()
            upto(N0["grp"] + 2)
            for j in range(2):
                eng.wait_ge(turned, TURN0["ut"] + j + 1)
                stage_item(G0["ut"] + j, 2 + j, 23)
            for gi in range(4):
                upto(N0["grp"] + gi + 2)
                for j in range(2):
                    g = G0["grp"] + 2 * gi + j
                    block_used(N0["grp"] + gi)
                    h, t = (hA, 4 * gi + 2 * j) if gi < 2 else (hB, 4 * gi + 2 * j - 8)
                    for part in range(2):
                        for m in range(2):
                            s = gains[:, GAIN["scale"][0] + 4 * gi + 2 * j + m:GAIN["scale"][0] + 4 * gi + 2 * j + m + 1]
                            src = acc[:, 2 * (g % 2) + m, 0:T]
                            if part == 0:
                                v.tensor_scalar(h[:, t + m, 0, :], src, s, None, ALU.mult)
                            else:
                                last = v.scalar_tensor_tensor(out=h[:, t + m, 1, :], in0=src, scalar=s,
                                                              in1=h[:, t + m, 0, :].bitcast(F32), op0=ALU.mult, op1=ALU.subtract)
                        eng.drain()
                        if part == 0:
                            continue
                    v.tensor_copy(small[:, 31:32], eps[:, :]).then_inc(h_ready, 1)
                    v.tensor_copy(small[:, 30:31], eps[:, :]).then_inc(acc_free, 1)
            for j in range(8):
                n = N0["wout"] + 2 * j
                upto(n + 3)
                block_used(n + 1)
                add_x(G0["wout"] + j, 2 * j, GAIN["memq"][0])

            def maxima(parts):
                for in_, c, ax in parts:
                    v.tensor_reduce(small[:, c + 8:c + 9], in_, ax, ALU.max)
                eng.drain()
                for i, (_, c, _) in enumerate(parts):
                    last = v.tensor_scalar(small[:, c:c + 1], small[:, c + 8:c + 9], -SCALE, None, ALU.mult)
                    if i == len(parts) - 1:
                        last.then_inc(nb_ready, 1)

            def inverses(c, n=2):
                following(eng, e_ready)
                v.reciprocal(small[:, c + 12:c + 12 + n], small[:, c + 4:c + 4 + n])
                eng.drain()

            def head_out(h, ready):
                v.tensor_copy(hA[:, h, 0, 0:TP], ab[:, 3, 0:TP])
                eng.drain()
                v.tensor_tensor(hA[:, h, 1, 0:TP], ab[:, 3, 0:TP], hA[:, h, 0, 0:TP].bitcast(F32), ALU.subtract).then_inc(h_ready, 1)

            def samples_out(bank, heads, q):
                src = ab[:, bank, 0:P].rearrange("p (m r) -> p r m", r=32)[:, 0:heads, :]
                dst = [hA[:, 0:heads, part, TP + 4 * q:TP + 4 * q + 4] for part in range(2)]
                v.tensor_copy(dst[0], src)
                eng.drain()
                return v.tensor_tensor(dst[1], src, dst[0].bitcast(F32), ALU.subtract)

            def mem_attention(l):
                g = G0[f"mq{l}"]
                n = N0[f"mq{l}"]
                mo = N0[f"mo{l}"]

                def queries(j):
                    block_used(n + 2 * j + 1)
                    v.tensor_tensor(qm[:, 2 * j:2 * j + 2, :], banks(g + j), twice(R[:, :]), ALU.mult).then_inc(acc_free, 1)

                def head_max(h):
                    following(eng, s_ready)
                    maxima([(ab[:, h % 2, q * TP:(q + 1) * TP], 2 * (h % 2) + q, AX.X) for q in range(2)])

                def head_probabilities(h):
                    s = h % 2
                    inverses(2 * s)
                    for q in range(2):
                        last = v.tensor_scalar(Pm[:, s, q, :], Pm[:, s, q, :], small[:, 12 + 2 * s + q:13 + 2 * s + q], None, ALU.mult)
                    last.then_inc(p_ready, 1)

                def head_turned():
                    following(eng, t_ready)
                    v.tensor_copy(PTm[:, :, :].rearrange("p k t -> p (k t)"), ab[:, 2, :]).then_inc(pt_ready, 1)

                def head_finish(h):
                    following(eng, o_ready)
                    head_out(h, None)

                def samples_max(q):
                    eng.wait_ge(scored, SC0[f"m{l}"] + 4 * q + 4)
                    maxima([(ab[:, q, 0:TP], 16 + q, AX.X)])

                def samples_probabilities(q):
                    inverses(16 + q, 1)
                    v.tensor_scalar(PsM[:, q, :], PsM[:, q, :], small[:, 28 + q:29 + q], None, ALU.mult).then_inc(p_ready, 1)

                def samples_turned(q):
                    following(eng, t_ready)
                    cols = ab[:, 2, 0:2 * P].rearrange("p (k m r) -> p k m r", k=2, r=32)
                    dst = PTzM.rearrange("p k b h c -> p k b (h c)")
                    for k in range(2):
                        last = v.tensor_copy(dst[:, k, 4 * q:4 * q + 4, 0:16:NH_MEM + 1], cols[:, k, :, 0:NH_MEM])
                    last.then_inc(pt_ready, 1)

                def samples_rows(q):
                    eng.wait_ge(v_used, VU0[f"m{l}"] + 4 * q + 4)
                    v.tensor_copy(Os[:, q, :], ab[:, (3, 0)[q], 0:P]).then_inc(os_ready, 1)

                eng.wait_ge(stored[0], STORED[2 if l == 0 else 4])
                eng.wait_ge(stored[1], STORED[3 if l == 0 else 5])
                upto(n + 2)
                rms(STAT[f"memq{l}"])
                upto(n + 3)
                queries(0)
                v.memset(QzM, 0.0)
                v.memset(PTzM, 0.0)
                upto(mo + 1)
                head_max(0)
                head_max(1)
                head_probabilities(0)
                head_probabilities(1)
                upto(mo + 2)
                queries(1)
                eng.drain()
                v.tensor_copy(QzM.rearrange("p b h c -> p (h c) b")[:, 0:16:NH_MEM + 1, :], qm[:, :, TP:T])
                head_turned()
                head_max(2)
                head_finish(0)
                head_turned()
                head_max(3)
                head_probabilities(2)
                head_finish(1)
                head_probabilities(3)
                head_turned()
                head_finish(2)
                head_turned()
                head_finish(3)
                upto(mo + 3)
                samples_max(0)
                samples_probabilities(0)
                samples_turned(0)
                samples_max(1)
                samples_probabilities(1)
                samples_turned(1)
                samples_rows(0)
                following(eng, t_ready)
                samples_out(1, NH_MEM, 0)
                samples_rows(1)
                following(eng, t_ready)
                samples_out(2, NH_MEM, 1).then_inc(h_ready, 1)
                eng.drain()

            def mem_layer(l):
                mem_attention(l)
                for i in range(4):
                    upto(N0[f"mo{l}"] + i + 2)
                    for j in range(2):
                        block_used(N0[f"mo{l}"] + i, half=1 + j)
                        add_x(G0[f"mo{l}"] + 2 * i + j, 4 * i + 2 * j, GAIN["ffn"][l])

            def ffn(l, gain):
                for part in range(3):
                    n, g, turns = N0[f"f{l}g{part}"], G0[f"f{l}g{part}"], PARTS[part] // 2
                    e0 = 22 * l + sum(PARTS[:part]) // 2

                    def turn(i, h, t):
                        first = part == 0 and isinstance(i, int)
                        lo(n + 2, 4 * i)
                        if first:
                            rms(STAT[f"ffn{l}"])
                        lo(n + 3, 4 * i)
                        block_used(n + 1, 4 * i)
                        v.tensor_tensor(gateF, banks(g), twice(R[:, :]), ALU.mult).then_inc(acc_free, 1)
                        lo(n + 4, 4 * i)
                        lo(n + 5, 4 * i)
                        eng.wait_ge(silu_ready, 1 * i + (e0 + 1))
                        v.tensor_tensor(siluF, siluF, twice(R[:, :]), ALU.mult)
                        eng.drain()
                        block_used(n + 3, 4 * i)
                        v.tensor_tensor(upF, banks(g + 1), siluF, ALU.mult).then_inc(acc_free, 1)
                        eng.drain()
                        split_h(h, t, upF)
                        eng.drain()

                    upto(n + 1)
                    first = 0
                    if part == 0:
                        turn(0, hA, slice(0, 2))
                        first = 1
                    with eng.Fori(first, 4) as i:
                        turn(i, hA, bass.ds(2 * i, 2))
                    with eng.Fori(4, turns) as i:
                        turn(i, hB, bass.ds(2 * i - 8, 2))
                    if part < 2:
                        nd, gd = N0[f"f{l}d{part}"], G0[f"f{l}d{part}"]
                        with eng.Fori(0, 4) as i:
                            for j in range(2):
                                lo(nd + 2 * j + 2, 4 * i)
                                lo(nd + 2 * j + 3, 4 * i)
                                block_used(nd + 2 * j + 1, 4 * i)
                                dst = x[:, bass.ds(4 * i + 2 * j, 2), :]
                                v.tensor_tensor(dst, banks(gd + j), dst, ALU.add).then_inc(acc_free, 1)
                        eng.drain()
                        at[0] = nd + 18
                    else:
                        at[0] = n + 4 * turns + 2
                        nd = N0[f"f{l}d2"]
                        for q in range(4):
                            upto(nd + 3 * q + 4)
                            for j in range(2):
                                block_used(nd + 3 * q + 2, half=1 + j)
                                add_x(G0[f"f{l}d2"] + 2 * q + j, 4 * q + 2 * j, gain)

            mem_layer(0)
            ffn(0, GAIN["kv"][0])

            n = N0["ksh"]
            for j in range(2):
                upto(n + 2 * j + 2)
                if j == 0:
                    rms(STAT["kv"], T, 3)
                upto(n + 2 * j + 3)
                block_used(n + 2 * j + 1)
                v.tensor_tensor(KT[:, 2 * j:2 * j + 2, :], banks(G0["ksh"] + j), twice(R[:, :]), ALU.mult).then_inc(acc_free, 1)
            v.memset(Vrep, 0.0)
            upto(N0["dq"] + 1)
            block_used(N0["vsh"] + 3)
            g = G0["vsh"]
            for c in range(2):
                last = v.tensor_scalar(V[:, c, :], acc[:, 2 * (g % 2) + c, :], Rc[:, c:c + 1], None, ALU.mult)
            last.then_inc(acc_free, 1)
            v.tensor_scalar(Vsm, acc[0:TS, 2 * ((g + 1) % 2), :], Rc[0:TS, 2:3], None, ALU.mult).then_inc(acc_free, 1)
            for j in range(2):
                eng.wait_ge(turned, TURN0["kt"] + j + 1)
                stage_item(G0["kt"] + j, 4 + j, (P, TS)[j], (1024, 512)[j])

            for m in range(0, DC, 2):
                split_x(GAIN["mix"][1], m)
            eng.wait_ge(stored[0], STORED[4])
            eng.wait_ge(stored[1], STORED[5])
            eng.wait_ge(vs_done, 16)
            eng.wait_ge(mask_in, 16)
            v.memset(QzD, 0.0)
            eng.drain()

            def dil_max(h):
                following(eng, s_ready)
                S1 = S[:, 0:768].rearrange("p (g j) -> p g j", g=NG)
                S0 = S[:, 768:1152].rearrange("p (g j) -> p g j", g=NG)
                v.tensor_tensor(S1, ab[:, 0:2, :].rearrange("p b (g j) -> p (b g) j", j=TP)[:, 0:NG, :], mask[:, :, :], ALU.add)
                v.tensor_tensor(S0, ab[:, 2, 0:384].rearrange("p (g j) -> p g j", g=NG), mask[:, :, P:2 * P], ALU.add).then_inc(s_free, 1)
                eng.drain()
                maxima([(S[:, 0:768], 0, AX.X), (S[:, 768:1152], 1, AX.X)])

            def dil_probabilities():
                inverses(0)
                for (c, w, o_) in ((0, TP, 0), (768, P, TP)):
                    v.tensor_tensor(Pn[:, o_:o_ + w], S[:, c:c + w], S[:, c + w:c + 2 * w], ALU.add)
                eng.drain()
                for (c, w, o_) in ((0, TP, 0), (768, P, TP)):
                    v.tensor_tensor(Pn[:, o_:o_ + w], Pn[:, o_:o_ + w], S[:, c + 2 * w:c + 3 * w], ALU.add)
                eng.drain()
                for i, (w, o_) in enumerate(((TP, 0), (P, TP))):
                    last = v.tensor_scalar(Pn[:, o_:o_ + w], Pn[:, o_:o_ + w], small[:, 12 + i:13 + i], None, ALU.mult)
                last.then_inc(p_ready, 1)

            def dil_turned():
                following(eng, t_ready)
                v.tensor_copy(PT[:, :], ab[:, 3, 0:384]).then_inc(pt_ready, 1)

            def dil_finish(h):
                following(eng, o_ready)
                head_out(h, None)

            steps = [lambda h: (dil_max(h), dil_probabilities()), lambda h: dil_turned(),
                     lambda h: (dil_finish(h), dil_max(h + 1), dil_probabilities()), lambda h: dil_turned(),
                     lambda h: dil_finish(h + 1)]
            for hp in range(4):
                for j in range(6):
                    n, g = N0["dq"] + 6 * hp + j, G0["dq"] + 3 * hp + j // 2
                    upto(n + 2)
                    if j % 2:
                        block_used(n)
                        dst = qd[:, hp % 2, j // 2]
                        v.tensor_tensor(dst, banks(g), twice(R[:, :]), ALU.mult).then_inc(acc_free, 1)
                        eng.drain()
                        v.tensor_copy(QzD[:, j // 2, :, hp, 2 * hp:2 * hp + 2], dst[:, :, TP:T].rearrange("p h b -> p b h"))
                    if hp and j < 5:
                        steps[j](2 * hp - 2)
            def dil_samples_max(q):
                eng.wait_ge(scored, SC0["dil"] + 4 * q + 4)
                maxima([(ab[:, q, 0:387], 16 + q, AX.X)])

            def dil_samples_probabilities(q):
                inverses(16 + q, 1)
                v.tensor_scalar(PsDf[:, q, :], PsDf[:, q, :], small[:, 28 + q:29 + q], None, ALU.mult).then_inc(p_ready, 1)
                eng.drain()
                v.tensor_reduce(small[:, 8 + q:9 + q], PsD[:, q, :, P], AX.X, ALU.add)

            def dil_samples_turned(q):
                following(eng, t_ready)
                cols = ab[:, 2, 0:3 * P].rearrange("p (g m r) -> p g m r", g=NG, r=32)
                dst = PTzD.rearrange("p g b k h -> p g b (k h)")
                for c in range(2):
                    last = v.tensor_copy(dst[:, :, 4 * q:4 * q + 4, c::NH + 2], cols[:, :, :, c:NH:2])
                last.then_inc(pt_ready, 1)

            def dil_samples_rows(q):
                eng.wait_ge(v_used, VU0["dil"] + 4 * q + 4)
                v.scalar_tensor_tensor(out=Os[:, q, :], in0=Vrep[:, q, :], scalar=small[:, 8 + q:9 + q],
                                       in1=ab[:, (3, 0)[q], 0:P], op0=ALU.mult, op1=ALU.add).then_inc(os_ready, 1)

            upto(N0["do"] + 2)
            dil_max(6)
            dil_probabilities()
            upto(N0["do"] + 3)
            dil_turned()
            dil_finish(6)
            dil_max(7)
            dil_probabilities()
            dil_turned()
            dil_finish(7)
            v.memset(PTzD, 0.0)
            eng.drain()
            dil_samples_max(0)
            dil_samples_probabilities(0)
            dil_samples_turned(0)
            dil_samples_max(1)
            dil_samples_probabilities(1)
            dil_samples_turned(1)
            eng.wait_ge(vrep_in, 16 * TS)
            dil_samples_rows(0)
            following(eng, t_ready)
            samples_out(1, NH, 0)
            dil_samples_rows(1)
            following(eng, t_ready)
            samples_out(2, NH, 1).then_inc(h_ready, 1)
            eng.drain()
            for j in range(8):
                n = N0["do"] + j
                upto(n + 2)
                block_used(n)
                add_x(G0["do"] + j, 2 * j, GAIN["memq"][1])
            mem_layer(1)
            ffn(1, None)

            rms(STAT["final"])
            for m in range(DC):
                last = v.scalar_tensor_tensor(out=x[:, m, :], in0=x[:, m, :], scalar=gains[:, GAIN["final"][0] + m:GAIN["final"][0] + m + 1],
                                              in1=R[:, :], op0=ALU.mult, op1=ALU.mult)
            last.then_inc(y_ready, 1)
            for c in range(3):
                rows, dst = (P, raw[:, c, :]) if c < 2 else (TS, att[0:TS, 0:D])
                for j in range(2):
                    g = G0["y"] + 2 * c + j
                    eng.wait_ge(turned, TURN0["y"] + 2 * c + j + 1)
                    v.tensor_copy(dst[:, 1024 * j:1024 * (j + 1)],
                                  acc[0:rows, 2 * (g % 2):2 * (g % 2) + 2, :].rearrange("p b c -> p (b c)")).then_inc(acc_free, 1)

        @block.gpsimd
        def _(eng):
            gp = nc.gpsimd

            def squares(done, width=T):
                for j in range(8):
                    done(j)
                    src = x[:, 2 * j:2 * j + 2, 0:width]
                    gp.tensor_tensor((sq if j else ssq)[:, :, 0:width], src, src, ALU.mult)
                    eng.drain()
                    if j:
                        last = gp.tensor_tensor(ssq[:, :, 0:width], ssq[:, :, 0:width], sq[:, :, 0:width], ALU.add)
                        if j == 7:
                            last.then_inc(ssq_ready, 1)
                        eng.drain()

            def taken(g):
                eng.wait_ge(acc_free, g + 1)

            def by_item(g):
                return lambda j: taken(g + j)

            def load_memory_rows(l):
                eng.wait_ge(half_used, 2 * N0[f"mq{l}"])
                load_cached(eng, (f"mk{l}", 0))
                eng.wait_ge(half_used, 2 * (N0[f"mq{l}"] + 4))
                for i in range(1, 4):
                    load_cached(eng, (f"mk{l}", i))
                load_cached(eng, (f"mv{l}", 0))
                for i in range(1, 4):
                    eng.wait_ge(turned, TURN0[f"mk{l}"] + 2 * i)
                    load_cached(eng, (f"mv{l}", i))

            later = [(key, s) for key, s in CACHED if key[0][0] == "d" and key != ("dk", 0)]

            eng.dma_start(pool_s[0, :, 0:NST - 1, :], a["state_pool"][0, :, 1:NST, :]).then_inc(out_done, 16)
            squares(lambda j: taken(G0["memload"] + 3), TP)
            taken(G0["memkt0"])
            eng.dma_start(mem_v_p[0, 0].rearrange("(c p) h d -> p c (h d)", p=P), mV[:, 0, :, :]).then_inc(out_done, 16)
            eng.dma_start(mem_k_p[0, 0].rearrange("(c p) h d -> p c (h d)", p=P),
                          stage.rearrange("p (c k) -> p c k", c=2)).then_inc(stored[0], 16)
            squares(lambda j: taken(G0["xt"] + 4))
            taken(G0["memkt1"])
            eng.dma_start(mem_v_p[1, 0].rearrange("(c p) h d -> p c (h d)", p=P), mV[:, 1, :, :]).then_inc(out_done, 16)
            eng.dma_start(mem_k_p[1, 0].rearrange("(c p) h d -> p c (h d)", p=P),
                          stage2.rearrange("p (c k) -> p c k", c=2)).then_inc(stored[1], 16)
            for j in range(2):
                taken(G0["ut"] + j)
                src, cols = stage_u, slice(1024 * j, 1024 * (j + 1))
                eng.dma_start(pool_p[0, 0, :, cols], src[0:NST, :]).then_inc(stored[j], 16)
                eng.dma_start(pool_s[0, :, NST - 1, cols], src[NST:NST + TS, :]).then_inc(stored[j], 16)
            squares(by_item(G0["wout"]))
            load_memory_rows(0)
            squares(by_item(G0["mo0"]))
            squares(by_item(G0["f0d2"]))
            taken(G0["vsh"] + 1)
            eng.dma_start(v_s.rearrange("b t h d -> (b t) (h d)"), Vsm).then_inc(vs_done, 16)
            eng.dma_start(wv_p[0].rearrange("(c p) h d -> p c (h d)", p=P), V[:, :, :]).then_inc(out_done, 16)
            taken(G0["kt"])
            eng.dma_start(wk_p[0].rearrange("(c p) h d -> p c (h d)", p=P),
                          stage.rearrange("p (c k) -> p c k", c=2)).then_inc(stored[0], 16)
            taken(G0["kt"] + 1)
            eng.dma_start(k_s.rearrange("b t h d -> (b t) (h d)"), stage2[0:TS, 0:MEMD]).then_inc(stored[1], 16)
            load_cached(eng, ("dk", 0))
            eng.wait_ge(vs_done, 16)
            for b in range(TS):
                r = 32 * (b % 4)
                dst = Vrep[r:r + NH, b // 4, :]
                src = v_s[b, 0].rearrange("k (o d) -> k o d", o=1).to_broadcast([KVH, 2, P])
                eng.dma_start(dst, src).then_inc(vrep_in, 16)
            eng.wait_ge(half_used, 2 * N0["do"])
            for i, (key, _) in enumerate(later):
                if i >= 5:
                    kind, b = later[i - 5][0]
                    if kind == "dk":
                        eng.wait_ge(turned, TURN0["dk"] + 2 * (b + 1))
                    else:
                        eng.wait_ge(v_used, VU0["dil"] + b + 1)
                load_cached(eng, key)
            squares(by_item(G0["do"]))
            load_memory_rows(1)
            squares(by_item(G0["mo1"]))
            squares(by_item(G0["f1d2"]))
            for c in range(3):
                taken(G0["y"] + 2 * c + 1)
                if c < 2:
                    eng.dma_start(y_p[0, c * P:(c + 1) * P, :], raw[:, c, :]).then_inc(out_done, 16)
                else:
                    eng.dma_start(y_s[:, 0, :], att[0:TS, 0:D]).then_inc(out_done, 16)
            eng.wait_ge(out_done, 16 * 7)
            eng.wait_ge(stored[0], STORED[4])
            eng.wait_ge(stored[1], STORED[5])
            eng.wait_ge(vs_done, 16)


_INS = ["x_prompt", "x_sample", "mem_prompt", "state_pool", "cache_win_k", "cache_win_v", "cache_mem_k", "cache_mem_v",
        "norm_mix", "norm_mem_q", "norm_mem_kv", "norm_ffn", "pool_w_in", "pool_w_group", "pool_scale", "pool_w_out",
        "norm_kv", "w_k_shared", "w_v_shared", "dil_w_q", "dil_w_o", "mem_w_q", "mem_w_k", "mem_w_v", "mem_w_o",
        "ffn_w_gate", "ffn_w_up", "ffn_w_down", "norm_final"]
_OUTS = [(1, TP, D), (TS, 1, D), (1, 1, NST, D), (1, TS, NST, D), (1, TP, KVH, P), (1, TP, KVH, P), (TS, 1, KVH, P),
         (TS, 1, KVH, P), (2, 1, TP, NH_MEM, P), (2, 1, TP, NH_MEM, P)]


def _shape_constants():
    q = np.arange(P)[:, None] + P
    j = np.arange(2 * P)[None, :]
    mask = np.stack([np.where((q - j >= 0) & ((q - j) % d == 0) & ((q - j) // d <= WIN_KEYS), 0.0, MASKED) for d in DILS], 1)
    t = np.arange(16)
    inv = np.stack([w / np.minimum(t + 1, w) for w in (2, 4, 8, 16)])
    return {"c_ident": np.eye(P, dtype=np.float32), "c_mask": mask.astype(np.float32),
            "c_inv": np.broadcast_to(inv[None], (P, 4, 16)).astype(np.float32)}


def kernel(**inputs):
    import concourse.bacc as bacc
    from concourse.bass_utils import run_bass_kernel_spmd

    nc = bacc.Bacc("TRN2", target_bir_lowering=False, num_devices=1)
    arrays, aps = {}, {}
    given = {n: np.ascontiguousarray(inputs[n]) for n in _INS}
    given.update(_shape_constants())
    for name, v in given.items():
        arrays[f"in_{name}"] = v
        aps[name] = nc.dram_tensor(f"in_{name}", v.shape, F32, kind="ExternalInput").ap()
    outs = [nc.dram_tensor(f"out_{i}", s, F32, kind="ExternalOutput").ap() for i, s in enumerate(_OUTS)]
    trunk(nc, aps, outs)
    r = run_bass_kernel_spmd(nc, [arrays], core_ids=[0])
    return tuple(r.results[0][f"out_{i}"] for i in range(len(_OUTS)))
```

```python
from contextlib import ExitStack

import numpy as np

import concourse.bass as bass
from concourse import mybir

F32 = mybir.dt.float32
F32R = mybir.dt.float32r
ALU = mybir.AluOpType
ACT = mybir.ActivationFunctionType
AX = mybir.AxisListType

P = 128
D = 2048
DC = D // P
TP = 256
TS = 8
T = TP + TS
FF = 5632
FC = FF // P
MEMD = 512
NH_MEM = 4
KVH = 4
NG = 3
NH = 8
DILS = (1, 4, 16)
PAST = 2048
WIN_KEYS = 128
NST = 15
EPS = 1e-6
SCALE = float(P) ** -0.5
MASKED = -1e30
BLK = 2048
NSPLIT = 4
PARTS = (16, 16, 12)
GAIN = {"memkv": (0, 16), "mix": (32, 48), "memq": (64, 80), "ffn": (96, 112), "kv": (128,), "final": (144,),
        "scale": (160,)}

PHASES = [
    ("memload", 0, 4),
    ("xload", 0, 1),
    ("memk0", 4, 2), ("memv0", 4, 1), ("memkt0", 0, 1),
    ("memk1", 4, 2), ("xt", 0, 5), ("st", 0, 2), ("memv1", 4, 1), ("memkt1", 0, 1),
    ("win", 16, 8), ("grp", 4, 8), ("ut", 0, 2), ("wout", 16, 8),
    ("mq0", 4, 2), ("mk0", 0, 8), ("mo0", 4, 8),
    ("f0g0", 32, 16), ("f0d0", 16, 8), ("f0g1", 32, 16), ("f0d1", 16, 8), ("f0g2", 24, 12), ("f0d2", 12, 8),
    ("ksh", 4, 2), ("vsh", 4, 2), ("kt", 0, 2),
    ("dq", 24, 12), ("dk", 0, 16), ("do", 8, 8),
    ("mq1", 4, 2), ("mk1", 0, 8), ("mo1", 4, 8),
    ("f1g0", 32, 16), ("f1d0", 16, 8), ("f1g1", 32, 16), ("f1d1", 16, 8), ("f1g2", 24, 12), ("f1d2", 12, 8),
    ("y", 0, 6),
]
N0, G0 = {}, {}
_n = _g = 0
for _name, _nb, _ni in PHASES:
    N0[_name], G0[_name] = _n, _g
    _n += _nb
    _g += _ni
NBLOCKS = _n

TURN0, _t = {}, 0
for _name, _nb, _ni in PHASES:
    if _nb == 0:
        TURN0[_name] = _t
        _t += _ni
CACHED = [(("mem", 0), 7), (("mem", 1), 8), (("x", 0), 4), (("x", 1), 1), (("x", 2), 3), (("state", 0), 2)]
for _l in range(2):
    CACHED += [((f"mk{_l}", i), s) for i, s in enumerate((5, 0, 1, 2))]
    CACHED += [((f"mv{_l}", i), s) for i, s in enumerate((3, 5, 0, 1))]
    if _l == 0:
        CACHED += [(("dk", b), (b - 1) % 5 if b else 6) for b in range(TS)]
        CACHED += [(("dv", b), (b + 7) % 5) for b in range(TS)]
CACHED_SLOT = dict(CACHED)
CACHED_LAND, _c = {}, [0] * 9
for _k, _s in CACHED:
    _c[_s] += 48 if _k[0][0] == "d" else 32 if _k == ("x", 1) else 16
    CACHED_LAND[_k] = _c[_s]

H0 = {"p": 0, "z": 8, "m0": 16, "f0": 21, "dil": 43, "m1": 52, "f1": 57}
GEN = {"memkv0": 0, "mix0": 1, "memq0": 2, "ffn0": 3, "kv": 4, "mix1": 5, "memq1": 6, "ffn1": 7}
E0 = {"m0": 0, "dil": NH_MEM + 2, "m1": NH_MEM + 2 + NH + 2}
SC0 = {"m0": 0, "dil": TS, "m1": 2 * TS}
VU0 = {"m0": 0, "dil": TS, "m1": 2 * TS}
STORED = [16, 16, 48, 48, 64, 64]
GAINS_IN = 16 * 7
STAT = {"mem": 1, "mix0": 2, "memq0": 3, "ffn0": 4, "kv": 5, "memq1": 6, "ffn1": 7, "final": 8}


def trunk(nc, a, o):
    (y_p, y_s, pool_p, pool_s, wk_p, wv_p, k_s, v_s, mem_k_p, mem_v_p) = o
    ctx = ExitStack()
    with ctx:
        def sb(name, shape, dt=F32):
            return ctx.enter_context(nc.sbuf_tensor(name, shape, dt))

        def sem(name):
            return ctx.enter_context(nc.semaphore(name))

        raw = sb("raw", [P, 2, BLK])
        whi = sb("whi", [P, NSPLIT, BLK], F32R)
        wlo = sb("wlo", [P, NSPLIT, BLK], F32R)
        x = sb("x", [P, DC, T])
        with nc.sbuf_tensor("xs", [P, DC, 2, T], F32R) as xs:
            pass
        xs_flat = sb("xs_flat", [P, DC * 2 * T])
        with nc.sbuf_tensor("hA", [P, 8, 2, T], F32R) as hA:
            pass
        hA_flat = sb("hA_flat", [P, 8 * 2 * T])
        with nc.sbuf_tensor("hB", [P, 8, 2, T], F32R) as hB:
            pass
        att = sb("att", [P, 16 * T])
        mKT = sb("mKT", [P, 2, NH_MEM, TP])
        mV = sb("mV", [P, 2, 2, MEMD])
        KT = sb("KT", [P, KVH, T])
        V = sb("V", [P, 2, MEMD])
        mask = sb("mask", [P, NG, 2 * P])
        ident = sb("ident", [P, P])
        ones = sb("ones", [P, P])
        gains = sb("gains", [P, 176])
        R = sb("R", [P, T])
        Rc = sb("Rc", [P, 3])
        ssq = sb("ssq", [P, 2, T])
        eps = sb("eps", [P, 1])
        small = sb("small", [P, 32])
        tmp = sb("tmp", [P, 2360])
        qd = att[:, 0:12 * T].rearrange("p (a g h t) -> p a g h t", a=2, g=NG, h=2)
        qm = att[:, 0:4 * T].rearrange("p (h t) -> p h t", h=NH_MEM)
        KTb = att[:, 0:2 * 12 * 129].rearrange("p (a k j) -> p a k j", a=2, k=12)
        KTm = att[:, 4 * T:4 * T + 2048].rearrange("p (a h j) -> p a h j", a=2, h=NH_MEM)
        QzD = att[:, 3168:3936].rearrange("p (g b k h) -> p g b k h", g=NG, b=TS, k=KVH)
        QzM = att[:, 3936:4064].rearrange("p (b h c) -> p b h c", b=TS, h=NH_MEM)
        gateF = tmp[:, 0:2 * T].rearrange("p (m t) -> p m t", m=2)
        siluF = tmp[:, 2 * T:4 * T].rearrange("p (m t) -> p m t", m=2)
        upF = tmp[:, 4 * T:6 * T].rearrange("p (m t) -> p m t", m=2)
        UP = TP + 16
        U, Ta, Tb = (tmp[:, i * 2 * UP:(i + 1) * 2 * UP].rearrange("p (m t) -> p m t", m=2) for i in range(3))
        wsum = tmp[:, 6 * UP:6 * UP + 128].rearrange("p (m b) -> p m b", m=DC)
        ut = tmp[:, 6 * UP + 128:6 * UP + 128 + DC * 23].rearrange("p (m t) -> p m t", m=DC)
        usm = tmp[:, 2200:2216].rearrange("p (m b) -> p m b", m=2)
        us2 = tmp[:, 2216:2232].rearrange("p (m b) -> p m b", m=2)
        invc = tmp[:, 2232:2296].rearrange("p (g t) -> p g t", g=4)
        stage = att[:, 0:1024]
        stage2 = att[:, 1024:2048]
        stage_m = tmp[:, 0:1024]
        stage_u = KT[:, :, :].rearrange("p h t -> p (h t)")[:, 0:1024]
        zF = tmp[:, 0:4 * T].rearrange("p (j m t) -> p j m t", j=2, m=2)
        gain_rows = att[:, 2048:2304]
        Vsm = att[0:TS, 2304:2816]
        S = tmp[:, 0:1152]
        Pn = tmp[:, 1152:1536]
        PT = tmp[:, 1536:1920]
        Pm = tmp[:, 0:1024].rearrange("p (a q j) -> p a q j", a=2, q=2)
        PTm = tmp[:, 1024:1536].rearrange("p (k t) -> p k t", k=2)
        PsD = tmp[:, 0:774].rearrange("p (b g j) -> p b g j", b=2, g=NG)
        PsDf = tmp[:, 0:774].rearrange("p (b j) -> p b j", b=2)
        PsM = tmp[:, 0:512].rearrange("p (b j) -> p b j", b=2)
        PTzD = tmp[:, 776:1544].rearrange("p (g b k h) -> p g b k h", g=NG, b=TS, k=KVH)
        PTzM = tmp[:, 1808:2064].rearrange("p (k b h c) -> p k b h c", k=2, b=TS, h=NH_MEM)
        Os = tmp[:, 1552:1808].rearrange("p (b d) -> p b d", b=2)
        Vrep = tmp[:, 2064:2320].rearrange("p (b d) -> p b d", b=2)
        std = sb("std", [P, T])
        stdc = sb("stdc", [P, 3])
        sq = sb("sq", [P, 2, T])

        acc = ctx.enter_context(nc.psum_tensor("acc", [P, 4, 512], F32))
        ab = ctx.enter_context(nc.psum_tensor("ab", [P, 4, 512], F32))

        ident_in, gains_in, mask_in = sem("ident_in"), sem("gains_in"), sem("mask_in")
        raw_in = [sem("raw_in0"), sem("raw_in1")]
        hi_ready, lo_ready = sem("hi_ready"), sem("lo_ready")
        half_used = sem("half_used")
        turned = sem("turned")
        acc_free = sem("acc_free")
        high_ready, low_ready = sem("high_ready"), sem("low_ready")
        xs_ready = sem("xs_ready")
        h_ready = sem("h_ready")
        ssq_ready, stat_ready, std_ready = sem("ssq_ready"), sem("stat_ready"), sem("std_ready")
        silu_ready = sem("silu_ready")
        zeros_ready = sem("zeros_ready")
        s_ready, s_free = sem("s_ready"), sem("s_free")
        nb_ready, e_ready, p_ready = sem("nb_ready"), sem("e_ready"), sem("p_ready")
        t_ready, pt_ready = sem("t_ready"), sem("pt_ready")
        o_ready, os_ready = sem("o_ready"), sem("os_ready")
        scored = sem("scored")
        v_used = sem("v_used")
        cached_in = [sem(f"cached_in{i}") for i in range(9)]
        y_ready = sem("y_ready")
        y_out = [sem("y_out0"), sem("y_out1")]
        rms_ready = sem("rms_ready")
        y_stored = sem("y_stored")
        stored = [sem("stored0"), sem("stored1")]
        out_done = sem("out_done")
        vs_done = sem("vs_done")
        vrep_in = sem("vrep_in")

        def counter():
            seen = {}

            def following(eng, which):
                seen[which.name] = seen.get(which.name, 0) + 1
                eng.wait_ge(which, seen[which.name])
            return following

        def kcols(w, k0, nk, c0, nco):
            return w[k0 * P:(k0 + nk) * P, c0:c0 + nco].rearrange("(k p) c -> p k c", p=P)

        def pair_block(w, j, i):
            return kcols(w, 8 * i, 8, 256 * j, 256)

        def quad_block(w, i, k0=0):
            return kcols(w, k0, 4, 512 * i, 512)

        def weight_source(n):
            name = [p for p, nb, _ in PHASES if nb and N0[p] <= n][-1]
            i = n - N0[name]
            if name[:4] == "memk":
                return pair_block(a["mem_w_k"][int(name[4])], i // 2, i % 2)
            if name[:4] == "memv":
                return kcols(a["mem_w_v"][int(name[4])], 4 * i, 4, 0, 512)
            if name == "win":
                return pair_block(a["pool_w_in"][0], i // 2, i % 2)
            if name == "grp":
                return a["pool_w_group"][0, i].rearrange("(k p) c -> p k c", p=P)
            if name == "wout":
                return pair_block(a["pool_w_out"][0], i // 2, i % 2)
            if name[:2] == "mq":
                return pair_block(a["mem_w_q"][int(name[2])], i // 2, i % 2)
            if name[:2] == "mo":
                return quad_block(a["mem_w_o"][int(name[2])], i)
            if name == "ksh":
                return pair_block(a["w_k_shared"], i // 2, i % 2)
            if name == "vsh":
                return kcols(a["w_v_shared"], 4 * i, 4, 0, 512)
            if name == "dq":
                hp, g = divmod(i // 2, NG)
                return kcols(a["dil_w_q"][0], 8 * (i % 2), 8, (g * NH + 2 * hp) * P, 256)
            if name == "do":
                return kcols(a["dil_w_o"][0], 0, 8, 256 * i, 256)
            layer, kind, part = int(name[1]), name[2], int(name[3])
            f0 = sum(PARTS[:part])
            if kind == "g":
                w = a["ffn_w_gate"] if i % 4 < 2 else a["ffn_w_up"]
                return kcols(w[layer], 8 * (i % 2), 8, (f0 + 2 * (i // 4)) * P, 256)
            if part < 2:
                return kcols(a["ffn_w_down"][layer], f0 + 8 * (i % 2), 8, 256 * (i // 2), 256)
            return kcols(a["ffn_w_down"][layer], f0 + 4 * (i % 3), 4, 512 * (i // 3), 512)

        def raw_as(slot, nk):
            return raw[:, slot, :].rearrange("p (k c) -> p k c", k=nk)

        def cached(key, j=0):
            s = CACHED_SLOT[key]
            if key[0] == "mem":
                return hA_flat[:, key[1] * BLK:(key[1] + 1) * BLK]
            if key == ("x", 0):
                return tmp[:, 0:BLK]
            if key == ("x", 1):
                return (V[:, :, :], mV[:, 1, :, :])[j].rearrange("p c k -> p (c k)")
            if key[0] in ("x", "state"):
                return xs_flat[:, s * BLK:(s + 1) * BLK]
            if key[0][0] == "m":
                return hA_flat[:, 8 * T:8 * T + BLK] if s == 5 else xs_flat[:, s * BLK:(s + 1) * BLK]
            if s == 6:
                return (mKT[:, 0, 0:2, :], mKT[:, 0, 2:4, :])[j].rearrange("p h t -> p (h t)") if j < 2 else mV[:, 0, 0, :]
            return xs_flat[:, (3 * s + j) * MEMD:(3 * s + j + 1) * MEMD]

        def load_cached(eng, key):
            kind, i = key
            done = cached_in[CACHED_SLOT[key]]
            if kind == "mem":
                eng.dma_start(cached(key), a["mem_prompt"][0, i * P:(i + 1) * P, :]).then_inc(done, 16)
            elif key == ("x", 0):
                eng.dma_start(cached(key), a["x_prompt"][0, 0:P, :]).then_inc(done, 16)
            elif key == ("x", 1):
                for j in range(2):
                    eng.dma_start(cached(key, j), a["x_prompt"][0, P:2 * P, 1024 * j:1024 * (j + 1)]).then_inc(done, 16)
            elif kind == "x":
                eng.dma_start(cached(key)[0:TS, :], a["x_sample"][:, 0, :]).then_inc(done, 16)
            elif kind == "state":
                eng.dma_start(cached(key)[0:TS * NST, :], a["state_pool"][0].rearrange("b t c -> (b t) c")).then_inc(done, 16)
            elif kind[0] == "m":
                src = a["cache_mem_k" if kind[1] == "k" else "cache_mem_v"][int(kind[2]), 2 * i:2 * i + 2]
                eng.dma_start(cached(key).rearrange("p (b k c) -> p b k c", b=2, k=2),
                              src.rearrange("b (k p) h d -> p b k (h d)", p=P)).then_inc(done, 16)
            else:
                src = a["cache_win_k" if kind == "dk" else "cache_win_v"][i].rearrange("t h d -> t (h d)")
                for g, d in enumerate(DILS):
                    rows = src[PAST - WIN_KEYS * d:PAST, :].rearrange("(p q) c -> p q c", q=d)[:, 0, :]
                    eng.dma_start(cached(key, g), rows).then_inc(done, 16)

        def cached_landed(eng, key):
            eng.wait_ge(cached_in[CACHED_SLOT[key]], CACHED_LAND[key])

        def landed(eng, n, more=0):
            eng.wait_ge(raw_in[n % 2], more * 8 + 16 * (n // 2 + 1))

        xg = xs_flat[:, 0:DC * T].rearrange("p (m t) -> p m t", m=DC)

        def output_item(k):
            c, j = divmod(k, 2)
            rows, dst = (P, raw[:, c, :]) if c < 2 else (TS, att[0:TS, 0:D])
            g = G0["y"] + k
            banks = ab if c == 1 else acc
            src = banks[0:rows, 2 * (g % 2):2 * (g % 2) + 2, :].rearrange("p b c -> p (b c)")
            return rows, dst[:, 1024 * j:1024 * (j + 1)], src, Rc[0:rows, c:c + 1]

        block = ctx.enter_context(nc.Block())

        @block.sync
        def _(eng):
            def load_block(n):
                if n >= 2:
                    eng.wait_ge(hi_ready, n - 1)
                    eng.wait_ge(lo_ready, n - 1)
                src = weight_source(n)
                eng.dma_start(raw_as(n % 2, src.shape[1]), src).then_inc(raw_in[n % 2], 16)

            def loop_blocks(name, turns, per, source):
                with eng.Fori(0, turns) as i:
                    for j in range(per):
                        n = N0[name] + j
                        eng.wait_ge(hi_ready, per * i + (n - 1))
                        eng.wait_ge(lo_ready, per * i + (n - 1))
                        src = source(i, j)
                        eng.dma_start(raw_as(n % 2, src.shape[1]), src).then_inc(raw_in[n % 2], 16)

            def cols(w, k0, nk, c):
                return w[k0 * P:(k0 + nk) * P, bass.ds(c, 256)].rearrange("(k p) c -> p k c", p=P)

            in_loop = {}
            for l in range(2):
                for part in range(3):
                    in_loop[f"f{l}g{part}"] = (PARTS[part] // 2, 4)
                    if part < 2:
                        in_loop[f"f{l}d{part}"] = (4, 4)
            load_cached(eng, ("mem", 0))
            eng.dma_start(ident[:, :], a["c_ident"]).then_inc(ident_in, 16)
            load_cached(eng, ("mem", 1))
            for j, name in enumerate(("norm_mem_kv", "norm_mix", "norm_mem_q", "norm_ffn")):
                eng.dma_start(gain_rows[32 * j:32 * (j + 1), 0:P], a[name].rearrange("l (m p) -> (l m) p", p=P)).then_inc(gains_in, 16)
            for j, name in enumerate(("norm_kv", "norm_final")):
                eng.dma_start(gain_rows[16 * j:16 * (j + 1), P:2 * P], a[name].rearrange("(m p) -> m p", p=P)).then_inc(gains_in, 16)
            eng.dma_start(gain_rows[32:48, P:2 * P], a["pool_scale"].rearrange("l (m p) -> (l m) p", p=P)).then_inc(gains_in, 16)
            n = 0
            while n < NBLOCKS:
                name = [p for p, nb, _ in PHASES if nb and N0[p] <= n][-1]
                if name in in_loop and n == N0[name]:
                    turns, per = in_loop[name]
                    l, part = int(name[1]), int(name[3])
                    f0 = sum(PARTS[:part])
                    if name[2] == "g":
                        loop_blocks(name, turns, per, lambda i, j: cols(
                            a["ffn_w_gate" if j < 2 else "ffn_w_up"][l], 8 * (j % 2), 8, i * 256 + f0 * P))
                    else:
                        loop_blocks(name, turns, per, lambda i, j: cols(
                            a["ffn_w_down"][l], f0 + 8 * (j % 2), 8, i * 512 + 256 * (j // 2)))
                    n += turns * per
                    continue
                load_block(n)
                n += 1
            for c in range(3):
                dst, src = (y_p[0, c * P:(c + 1) * P, :], raw[:, c, :]) if c < 2 else (y_s[:, 0, :], att[0:TS, 0:D])
                for k in range(2):
                    eng.wait_ge(y_out[k], c + 1)
                    cols = slice(k * 1024, (k + 1) * 1024)
                    eng.dma_start(dst[:, cols], src[:, cols]).then_inc(y_stored, 16)
            eng.wait_ge(y_stored, 16 * 6)

        @block.scalar
        def _(eng):
            at = [0]
            following = counter()

            def hi(n, more=0):
                landed(eng, n, more)
                if n >= NSPLIT:
                    eng.wait_ge(half_used, more * 2 + 2 * (n - NSPLIT + 1))
                nc.scalar.activation(whi[:, n % NSPLIT, :], raw[:, n % 2, :], ACT.Copy).then_inc(hi_ready, 1)

            def upto(n):
                while at[0] <= min(n, NBLOCKS - 1):
                    hi(at[0])
                    at[0] += 1

            def root(k, width=T, cols=0):
                eng.wait_ge(stat_ready, k)
                if width:
                    last = nc.scalar.activation(std[:, 0:width], ab[:, 3, 0:width], ACT.Sqrt, bias=eps[:, :], scale=1.0 / D)
                if cols:
                    last = nc.scalar.activation(stdc[:, 0:2], ab[:, 3, 300:302], ACT.Sqrt, bias=eps[:, :], scale=1.0 / D)
                if cols == 3:
                    last = nc.scalar.activation(stdc[0:TS, 2:3], ab[0:TS, 3, 302:303], ACT.Sqrt, bias=eps[0:TS, :],
                                                scale=1.0 / D)
                last.then_inc(std_ready, 1)

            def softmax_exp(parts):
                following(eng, nb_ready)
                for out, in_, b, d in parts:
                    last = nc.scalar.activation(out, in_, ACT.Exp, bias=small[:, b:b + 1], scale=SCALE,
                                                accum_out=small[:, d:d + 1])
                last.then_inc(e_ready, 1)

            def copy_item(g, out, in_):
                eng.wait_ge(acc_free, g)
                nc.scalar.copy(out, in_).then_inc(acc_free, 1)

            def mem_attention(l):
                gk = G0[f"mk{l}"]

                def head_exp(h):
                    s = h % 2
                    softmax_exp([(Pm[:, s, q, :], ab[:, s, q * TP:(q + 1) * TP], 2 * s + q, 4 + 2 * s + q)
                                 for q in range(2)])

                def samples_exp(q):
                    softmax_exp([(PsM[:, q, :], ab[:, q, 0:TP], 16 + q, 20 + q)])

                def keys(b):
                    eng.wait_ge(turned, TURN0[f"mk{l}"] + b + 1)
                    if b >= 2:
                        eng.wait_ge(scored, SC0[f"m{l}"] + b - 1)
                    copy_item(gk + b, KTm[:, b % 2].rearrange("p h j -> p (h j)"),
                              acc[:, 2 * ((gk + b) % 2):2 * ((gk + b) % 2) + 2, :].rearrange("p b c -> p (b c)"))

                upto(N0[f"mo{l}"])
                head_exp(0)
                head_exp(1)
                upto(N0[f"mo{l}"] + 1)
                keys(0)
                head_exp(2)
                head_exp(3)
                keys(1)
                upto(N0[f"mo{l}"] + 2)
                keys(2)
                upto(N0[f"mo{l}"] + 3)
                keys(3)
                keys(4)
                samples_exp(0)
                for b in range(5, TS):
                    keys(b)
                samples_exp(1)

            def ffn(l):
                for part in range(3):
                    n, g, turns = N0[f"f{l}g{part}"], G0[f"f{l}g{part}"], PARTS[part] // 2

                    def turn(i):
                        hi(n + 2, 4 * i)
                        if part == 0 and isinstance(i, int):
                            root(STAT[f"ffn{l}"])
                            nc.scalar.preload_act_table(ACT.Silu)
                        hi(n + 3, 4 * i)
                        eng.wait_ge(acc_free, 2 * i + (g + 1))
                        nc.scalar.activation(siluF, gateF, ACT.Silu).then_inc(silu_ready, 1)
                        hi(n + 4, 4 * i)
                        hi(n + 5, 4 * i)

                    upto(n + 1)
                    if part == 0:
                        turn(0)
                    with eng.Fori(1 if part == 0 else 0, turns) as i:
                        turn(i)
                    if part < 2:
                        nd = N0[f"f{l}d{part}"]
                        with eng.Fori(0, 4) as i:
                            for j in range(4):
                                hi(nd + 2 + j, 4 * i)
                        at[0] = nd + 18
                    else:
                        at[0] = n + 4 * turns + 2

            nc.scalar.preload_act_table(ACT.Copy)
            eng.wait_ge(zeros_ready, 1)
            upto(1)
            eng.wait_ge(acc_free, G0["xload"] + 1)
            eng.dma_start(mask[:, :, :], a["c_mask"]).then_inc(mask_in, 16)
            eng.dma_start(invc, a["c_inv"]).then_inc(mask_in, 16)
            for m in range(DC):
                c = GAIN["memkv"][1] + m
                nc.scalar.activation((hA, hB)[m // 8][:, m % 8, 0, 0:TP], x[:, m, 0:TP], ACT.Copy,
                                     scale=gains[:, c:c + 1]).then_inc(high_ready, 1)
                if m % 8 == 3:
                    upto(2 + m // 8)
            root(STAT["mem"], TP, 2)
            upto(N0["win"] + 2)
            root(STAT["mix0"])
            upto(N0["grp"] + 1)
            for gi in range(4):
                upto(N0["grp"] + gi + 2)
                for j in range(2):
                    g = G0["grp"] + 2 * gi + j
                    eng.wait_ge(half_used, 2 * (N0["grp"] + gi) + 1 + j)
                    eng.wait_ge(h_ready, 8 + (2 * gi - 1 + j if gi else 0))
                    eng.wait_ge(acc_free, g)
                    for m in range(2):
                        c = GAIN["scale"][0] + 4 * gi + 2 * j + m
                        last = nc.scalar.activation(zF[:, j, m, :], acc[:, 2 * (g % 2) + m, 0:T], ACT.Copy, scale=gains[:, c:c + 1])
                    last.then_inc(acc_free, 1)
            upto(N0["mq0"] + 2)
            root(STAT["memq0"])
            mem_attention(0)
            ffn(0)
            upto(N0["ksh"] + 2)
            root(STAT["kv"], T, 3)
            upto(N0["dq"] + 1)
            for j, (rows, width) in enumerate(((P, 1024), (TS, 512))):
                g = G0["kt"] + j
                eng.wait_ge(turned, TURN0["kt"] + j + 1)
                copy_item(g, (stage, stage2)[j][0:rows, 0:width],
                          acc[0:rows, 2 * (g % 2):2 * (g % 2) + 2, :].rearrange("p b c -> p (b c)")[:, 0:width])
            dil = [(S[:, 0:768], S[:, 0:768], 0, 4), (S[:, 768:1152], S[:, 768:1152], 1, 5)]
            for hp in range(4):
                for j in range(6):
                    upto(N0["dq"] + 6 * hp + j + 2)
                    if hp and j in (0, 2):
                        softmax_exp(dil)
            gk = G0["dk"]

            def dil_keys(b):
                if b == 1:
                    eng.wait_ge(s_ready, NH_MEM + NH)
                if b >= 2:
                    eng.wait_ge(scored, SC0["dil"] + b - 1)
                nc.scalar.copy(KTb[:, b % 2, :, P].rearrange("p (g k) -> p g k", g=NG),
                               KT[:, :, TP + b].rearrange("p (o k) -> p o k", o=1).to_broadcast([P, NG, KVH]))
                for part in range(2):
                    g = gk + 2 * b + part
                    eng.wait_ge(turned, TURN0["dk"] + 2 * b + part + 1)
                    copy_item(g, KTb[:, b % 2, 6 * part:6 * part + 6, 0:P],
                              acc[:, 2 * (g % 2):2 * (g % 2) + 2, :].rearrange("p b (s c) -> p (b s) c", c=P)[:, 0:6, :])

            def dil_samples_exp(q):
                softmax_exp([(PsDf[:, q, :], ab[:, q, 0:387], 16 + q, 20 + q)])

            upto(N0["do"] + 2)
            dil_keys(0)
            softmax_exp(dil)
            dil_keys(1)
            softmax_exp(dil)
            upto(N0["do"] + 3)
            for b in range(2, 5):
                dil_keys(b)
            dil_samples_exp(0)
            for b in range(5, TS):
                dil_keys(b)
            dil_samples_exp(1)
            upto(N0["mq1"] + 2)
            root(STAT["memq1"])
            mem_attention(1)
            ffn(1)
            upto(NBLOCKS - 1)
            nc.scalar.preload_act_table(ACT.Sqrt)
            root(STAT["final"], 0, 3)
            for k in range(1, 6, 2):
                eng.wait_ge(turned, TURN0["y"] + k + 1)
                if k == 1:
                    eng.wait_ge(rms_ready, 1)
                rows, dst, src, r = output_item(k)
                nc.scalar.activation(dst, src, ACT.Copy, scale=r).then_inc(y_out[1], 1)

        @block.tensor
        def _(eng):
            mm = nc.tensor.matmul
            following = counter()

            def block_ready(n, more=0):
                eng.wait_ge(hi_ready, more + (n + 1))
                eng.wait_ge(lo_ready, more + (n + 1))

            def item_free(g, more=0):
                if g >= 2:
                    eng.wait_ge(acc_free, more + (g - 1))

            def products(out, s, col, tile, first, last):
                hi_, lo_ = tile
                w_hi, w_lo = whi[:, s, col:col + P], wlo[:, s, col:col + P]
                mm(out, w_hi, hi_, start=first, stop=False)
                mm(out, w_hi, lo_, start=False, stop=False)
                return mm(out, w_lo, hi_, start=False, stop=last)

            def xtile(k, width=T):
                return xs[:, k, 0, 0:width], xs[:, k, 1, 0:width]

            def htile(k, width=T):
                h, k = (hA, k) if k < 8 else (hB, k - 8)
                return h[:, k, 0, 0:width], h[:, k, 1, 0:width]

            def xs_wait(gen):
                return lambda k: eng.wait_ge(xs_ready, 16 * GEN[gen] + k + 1)

            def h_wait(base):
                return lambda k: eng.wait_ge(h_ready, base + k // 2 + 1) if k % 2 == 0 else None

            def pair_item(n, g, nb, tile, ready=None, nmore=0, gmore=0, width=T, after_first=None, halves=None):
                item_free(g, gmore)
                for i in range(nb):
                    block_ready(n + i, nmore)
                    for k in range(8):
                        if ready is not None:
                            ready(8 * i + k)
                        for m in range(2):
                            last = products(acc[:, 2 * (g % 2) + m, 0:width], (n + i) % NSPLIT, k * 256 + m * P,
                                            tile(8 * i + k, width), i == k == 0, i == nb - 1 and k == 7)
                        if k % 4 == 3:
                            last.then_inc(half_used, 1)
                            if halves is not None and 2 * i + k // 4 in halves:
                                halves[2 * i + k // 4]()
                    if i == 0 and after_first is not None:
                        after_first()

            def pair_phase(name, items, nb, tile, ready=None, width=T, after_first=None):
                for j in range(items):
                    pair_item(N0[name] + nb * j, G0[name] + j, nb, tile, ready if j == 0 else None, width=width,
                              after_first=after_first if j == 0 else None)

            def pair_loop(name, turns, items, tile, ready=None):
                with eng.Fori(0, turns) as i:
                    for j in range(items):
                        pair_item(N0[name] + 2 * j, G0[name] + j, 2, tile, ready if j == 0 else None,
                                  nmore=2 * items * i, gmore=items * i)

            def quad_item(n, g, nb, tile, ready, after_first=None):
                for i in range(nb):
                    block_ready(n + i)
                    for m in range(4):
                        if i == 0 and m % 2 == 0:
                            item_free(g + m // 2)
                        for k in range(4):
                            if m == 0 and ready is not None:
                                ready(4 * i + k)
                            last = products(acc[:, 2 * ((g + m // 2) % 2) + m % 2, 0:T], (n + i) % NSPLIT,
                                            k * 512 + m * P, tile(4 * i + k), i == k == 0, i == nb - 1 and k == 3)
                        if m % 2 == 1:
                            last.then_inc(half_used, 1)

            def value_phase(name, samples, tile=None):
                n, g = N0[name], G0[name]
                item_free(g)
                if samples:
                    item_free(g + 1)
                for i in range(4):
                    block_ready(n + i)
                    s = (n + i) % NSPLIT
                    for c in range(3 if samples else 2):
                        out, t0, tn = (acc[:, 2 * (g % 2) + c, :], c * P, P) if c < 2 else (acc[0:TS, 2 * ((g + 1) % 2), :], TP, TS)
                        for k in range(4):
                            x_hi, x_lo = (part[:, t0:t0 + tn] for part in (tile or xtile)(4 * i + k))
                            w_hi, w_lo = whi[:, s, k * 512:(k + 1) * 512], wlo[:, s, k * 512:(k + 1) * 512]
                            mm(out, x_hi, w_hi, start=i == k == 0, stop=False)
                            mm(out, x_hi, w_lo, start=False, stop=False)
                            last = mm(out, x_lo, w_hi, start=False, stop=i == 3 and k == 3)
                        if c == 0 or c == (2 if samples else 1):
                            last.then_inc(half_used, 1)

            def turn_item(g, parts):
                item_free(g)
                for rows, j, n, src in parts:
                    last = nc.tensor.transpose(acc[0:rows, 2 * (g % 2) + j // 4, (j % 4) * P:(j % 4) * P + n],
                                               src, ident[0:src.shape[0], 0:src.shape[0]])
                last.then_inc(turned, 1)

            def statistics(k, width=T, cols=0):
                eng.wait_ge(ssq_ready, k)
                for m in range(2 if width else 0):
                    last = mm(ab[:, 3, 0:width], ones[:, :], ssq[:, m, 0:width], start=m == 0, stop=m == 1)
                for c in range(cols):
                    tn = P if c < 2 else TS
                    for m in range(2):
                        last = mm(ab[0:tn, 3, 300 + c:301 + c], ssq[:, m, c * P:c * P + tn], ones[:, 0:1],
                                  start=m == 0, stop=m == 1)
                last.then_inc(stat_ready, 1)

            def mem_attention(l):
                g = G0[f"mq{l}"]
                h0 = H0[f"m{l}"]
                gk = G0[f"mk{l}"]

                def scores(h):
                    eng.wait_ge(acc_free, g + h // 2 + 1)
                    if h >= 2:
                        eng.wait_ge(e_ready, E0[f"m{l}"] + h - 1)
                    for q in range(2):
                        last = mm(ab[:, h % 2, q * TP:(q + 1) * TP], qm[:, h, q * P:(q + 1) * P], mKT[:, l, h, :],
                                  start=True, stop=True)
                    last.then_inc(s_ready, 1)

                def turn_probabilities(h):
                    following(eng, p_ready)
                    for k in range(2):
                        for q in range(2):
                            last = nc.tensor.transpose(ab[:, 2, k * TP + q * P:k * TP + (q + 1) * P],
                                                       Pm[:, h % 2, q, k * P:(k + 1) * P], ident[:, :])
                    last.then_inc(t_ready, 1)

                def weigh(h):
                    following(eng, pt_ready)
                    if h:
                        eng.wait_ge(h_ready, h0 + h)
                    for k in range(2):
                        last = mm(ab[:, 3, 0:TP], mV[:, l, k, h * P:(h + 1) * P], PTm[:, k, :], start=k == 0, stop=k == 1)
                    last.then_inc(o_ready, 1)

                def turn_keys(b):
                    key = (f"mk{l}", b // 2)
                    cached_landed(eng, key)
                    rows = cached(key).rearrange("p (b k c) -> p b k c", b=2, k=2)
                    turn_item(gk + b, [(P, 2 * h + k, P, rows[:, b % 2, k, h * P:(h + 1) * P])
                                       for h in range(NH_MEM) for k in range(2)])

                def sample_scores(b):
                    eng.wait_ge(acc_free, gk + b + 1)
                    if b % 4 == 0:
                        eng.wait_ge(e_ready, E0[f"m{l}"] + 3 + b // 4)
                    r = 32 * (b % 4)
                    for h in range(NH_MEM):
                        last = mm(ab[r:r + NH_MEM, b // 4, 0:TP], QzM[:, b, h, :],
                                  KTm[:, b % 2, h, :], start=h == 0, stop=h == NH_MEM - 1)
                    last.then_inc(scored, 1)

                def turn_samples(q):
                    following(eng, p_ready)
                    for k in range(2):
                        last = nc.tensor.transpose(ab[:, 2, k * P:(k + 1) * P], PsM[:, q, k * P:(k + 1) * P], ident[:, :])
                    last.then_inc(t_ready, 1)

                def sample_values(b):
                    if b % 4 == 0:
                        following(eng, pt_ready)
                    if b == 0:
                        eng.wait_ge(h_ready, h0 + NH_MEM)
                    key = (f"mv{l}", b // 2)
                    cached_landed(eng, key)
                    rows = cached(key).rearrange("p (b k c) -> p b k c", b=2, k=2)
                    r = 32 * (b % 4)
                    for k in range(2):
                        for h in range(NH_MEM):
                            last = mm(ab[r:r + NH_MEM, (3, 0)[b // 4], 0:P], PTzM[:, k, b, h, :],
                                      rows[:, b % 2, k, h * P:(h + 1) * P], start=k == h == 0, stop=k == 1 and h == NH_MEM - 1)
                    last.then_inc(v_used, 1)

                def turn_outputs(q):
                    following(eng, os_ready)
                    nc.tensor.transpose(ab[:, 1 + q, 0:P], Os[:, q, :], ident[:, :]).then_inc(t_ready, 1)

                pair_item(N0[f"mq{l}"], g, 2, xtile, xs_wait(f"memq{l}"), after_first=lambda: statistics(STAT[f"memq{l}"]))
                pair_item(N0[f"mq{l}"] + 2, g + 1, 2, xtile,
                          halves={0: lambda: (scores(0), scores(1)), 2: lambda: turn_probabilities(0)})
                weigh(0)
                turn_keys(0)
                scores(2)
                turn_probabilities(1)
                turn_keys(1)
                scores(3)
                weigh(1)
                turn_keys(2)
                sample_scores(0)
                turn_probabilities(2)
                turn_keys(3)
                sample_scores(1)
                weigh(2)
                turn_probabilities(3)
                sample_scores(2)
                weigh(3)
                turn_keys(4)
                sample_scores(3)
                turn_keys(5)
                sample_scores(4)
                turn_keys(6)
                turn_samples(0)
                sample_scores(5)
                turn_keys(7)
                sample_scores(6)
                sample_values(0)
                sample_scores(7)
                sample_values(1)
                sample_values(2)
                turn_samples(1)
                sample_values(3)
                sample_values(4)
                sample_values(5)
                turn_outputs(0)
                sample_values(6)
                sample_values(7)
                turn_outputs(1)

            hd = H0["dil"]

            def dil_scores(h):
                a_, hh, kv = (h // 2) % 2, h % 2, h // 2
                eng.wait_ge(acc_free, G0["dq"] + 3 * (h // 2) + 3)
                if h:
                    eng.wait_ge(s_free, h)
                for g in range(NG):
                    mm(ab[:, g // 2, (g % 2) * TP:(g % 2 + 1) * TP], qd[:, a_, g, hh, P:TP], KT[:, kv, 0:TP],
                       start=True, stop=True)
                for g in range(NG):
                    last = mm(ab[:, 2, g * P:(g + 1) * P], qd[:, a_, g, hh, 0:P], KT[:, kv, 0:P], start=True, stop=True)
                last.then_inc(s_ready, 1)

            def dil_turn(h):
                following(eng, p_ready)
                if h:
                    eng.wait_ge(h_ready, hd + h)
                for j, c in enumerate((TP, 0, P)):
                    last = nc.tensor.transpose(ab[:, 3, j * P:(j + 1) * P], Pn[:, c:c + P], ident[:, :])
                last.then_inc(t_ready, 1)

            def dil_out(h):
                following(eng, pt_ready)
                v = slice((h // 2) * P, (h // 2 + 1) * P)
                mm(ab[:, 3, 0:TP], V[:, 0, v], PT[:, 0:TP], start=True, stop=False)
                mm(ab[:, 3, P:TP], V[:, 1, v], PT[:, TP:TP + P], start=False, stop=True).then_inc(o_ready, 1)

            gk = G0["dk"]

            def dil_turn_keys(b):
                cached_landed(eng, ("dk", b))
                for part in range(2):
                    turn_item(gk + 2 * b + part, [(P, i, P, cached(("dk", b), j // 4)[:, (j % 4) * P:(j % 4 + 1) * P])
                                                  for i, j in enumerate(range(6 * part, 6 * part + 6))])

            def dil_sample_scores(b):
                eng.wait_ge(acc_free, gk + 2 * b + 2)
                if b == 0:
                    eng.wait_ge(s_free, NH)
                r = 32 * (b % 4)
                for g in range(NG):
                    for kv in range(KVH):
                        last = mm(ab[r:r + NH, b // 4, g * 129:(g + 1) * 129], QzD[:, g, b, kv, :],
                                  KTb[:, b % 2, KVH * g + kv, :], start=g == kv == 0,
                                  stop=kv == KVH - 1, skip_group_check=True)
                last.then_inc(scored, 1)

            def dil_turn_samples(q):
                following(eng, p_ready)
                for g in range(NG):
                    last = nc.tensor.transpose(ab[:, 2, g * P:(g + 1) * P], PsD[:, q, g, 0:P], ident[:, :])
                last.then_inc(t_ready, 1)

            def dil_sample_values(b):
                if b % 4 == 0:
                    following(eng, pt_ready)
                if b == 0:
                    eng.wait_ge(h_ready, hd + NH)
                cached_landed(eng, ("dv", b))
                r = 32 * (b % 4)
                for g in range(NG):
                    for kv in range(KVH):
                        last = mm(ab[r:r + NH, (3, 0)[b // 4], 0:P], PTzD[:, g, b, kv, :],
                                  cached(("dv", b), g)[:, kv * P:(kv + 1) * P], start=g == kv == 0,
                                  stop=g == NG - 1 and kv == KVH - 1)
                last.then_inc(v_used, 1)

            def dil_turn_outputs(q):
                following(eng, os_ready)
                nc.tensor.transpose(ab[:, 1 + q, 0:P], Os[:, q, :], ident[:, :]).then_inc(t_ready, 1)

            def dil_last():
                dil_scores(6)
                dil_turn_keys(0)
                dil_scores(7)
                dil_turn(6)
                dil_turn_keys(1)
                dil_out(6)
                dil_sample_scores(0)
                dil_turn_keys(2)
                dil_sample_scores(1)
                dil_turn(7)
                dil_turn_keys(3)
                dil_out(7)
                dil_sample_scores(2)
                for b in range(3, 5):
                    dil_turn_keys(b + 1)
                    dil_sample_scores(b)
                dil_turn_keys(6)
                dil_turn_samples(0)
                dil_sample_scores(5)
                dil_turn_keys(7)
                dil_sample_scores(6)
                dil_sample_values(0)
                dil_sample_scores(7)
                dil_sample_values(1)
                dil_sample_values(2)
                dil_turn_samples(1)
                dil_sample_values(3)
                dil_sample_values(4)
                dil_sample_values(5)
                dil_turn_outputs(0)
                dil_sample_values(6)
                dil_sample_values(7)
                dil_turn_outputs(1)

            eng.wait_ge(ident_in, 16)
            eng.wait_ge(zeros_ready, 1)
            for c in range(2):
                cached_landed(eng, ("mem", c))
                for j in range(2):
                    turn_item(G0["memload"] + 2 * c + j, [(P, m, P, cached(("mem", c))[:, (8 * j + m) * P:(8 * j + m + 1) * P])
                                                          for m in range(8)])
            eng.wait_ge(gains_in, GAINS_IN)
            turn_item(G0["xload"], [(P, 0, P, gain_rows[:, 0:P]), (P, 1, 48, gain_rows[0:48, P:2 * P])])
            pair_item(N0["memk0"], G0["memk0"], 2, xtile, xs_wait("memkv0"), width=TP)
            statistics(STAT["mem"], TP, 2)
            pair_item(N0["memk0"] + 2, G0["memk0"] + 1, 2, xtile, width=TP)

            def memory_keys_out(l):
                eng.wait_ge(acc_free, G0[f"memk{l}"] + 2)
                turn_item(G0[f"memkt{l}"], [(P, 4 * c + h, P, mKT[:, l, h, c * P:(c + 1) * P])
                                            for c in range(2) for h in range(NH_MEM)])

            value_phase("memv0", False)
            memory_keys_out(0)
            pair_phase("memk1", 2, 2, htile, lambda k: eng.wait_ge(low_ready, k // 2 + 1), TP)
            for c in range(3):
                cached_landed(eng, ("x", c))
                rows = cached(("x", c))
                if c < 2:
                    for j in range(2):
                        half = cached(("x", 1), j) if c else rows[:, 1024 * j:1024 * (j + 1)]
                        turn_item(G0["xt"] + 2 * c + j, [(P, m, P, half[:, m * P:(m + 1) * P]) for m in range(8)])
                else:
                    item_free(G0["xt"] + 4)
                    for m in range(DC):
                        last = nc.tensor.transpose(acc[:, 2 * ((G0["xt"] + 4) % 2), TS * m:TS * (m + 1)],
                                                   rows[0:TS, m * P:(m + 1) * P], ident[0:TS, 0:TS])
                    last.then_inc(turned, 1)
            cached_landed(eng, ("state", 0))
            for j in range(2):
                turn_item(G0["st"] + j, [(P, m, TS * NST, cached(("state", 0))[0:TS * NST, (8 * j + m) * P:(8 * j + m + 1) * P])
                                         for m in range(8)])
            value_phase("memv1", False, htile)
            memory_keys_out(1)
            pair_phase("win", 8, 2, xtile, xs_wait("mix0"), after_first=lambda: statistics(STAT["mix0"]))
            for gi in range(4):
                quad_item(N0["grp"] + gi, G0["grp"] + 2 * gi, 1, lambda k, gi=gi: htile(4 * gi + k), h_wait(2 * gi))
            for j in range(2):
                turn_item(G0["ut"] + j, [(23, m, P, ut[:, 8 * j + m, :]) for m in range(8)])
            pair_phase("wout", 8, 2, htile, h_wait(H0["z"]))

            def ffn(l):
                for part in range(3):
                    g_, d_ = f"f{l}g{part}", f"f{l}d{part}"
                    turns = PARTS[part] // 2
                    if part == 0:
                        pair_item(N0[g_], G0[g_], 2, xtile, xs_wait(f"ffn{l}"), after_first=lambda: statistics(STAT[f"ffn{l}"]))
                        pair_item(N0[g_] + 2, G0[g_] + 1, 2, xtile)
                        with eng.Fori(1, turns) as i:
                            for j in range(2):
                                pair_item(N0[g_] + 2 * j, G0[g_] + j, 2, xtile, nmore=4 * i, gmore=2 * i)
                    else:
                        pair_loop(g_, turns, 2, xtile)
                    base = H0[f"f{l}"] + sum(PARTS[:part]) // 2
                    if part < 2:
                        pair_loop(d_, 4, 2, htile, h_wait(base))
                    else:
                        for q in range(4):
                            quad_item(N0[d_] + 3 * q, G0[d_] + 2 * q, 3, htile, h_wait(base) if q == 0 else None)

            def mem_layer(l):
                mem_attention(l)
                eng.wait_ge(h_ready, H0[f"m{l}"] + 5)
                for i in range(4):
                    quad_item(N0[f"mo{l}"] + i, G0[f"mo{l}"] + 2 * i, 1, htile, None)
                ffn(l)

            mem_layer(0)
            pair_phase("ksh", 2, 2, xtile, xs_wait("kv"), after_first=lambda: statistics(STAT["kv"], T, 3))
            value_phase("vsh", True)
            eng.wait_ge(acc_free, G0["ksh"] + 2)
            turn_item(G0["kt"], [(P, 4 * c + h, P, KT[:, h, c * P:(c + 1) * P]) for c in range(2) for h in range(KVH)])
            turn_item(G0["kt"] + 1, [(TS, h, P, KT[:, h, TP:T]) for h in range(KVH)])

            steps = [lambda h: dil_scores(h), lambda h: dil_scores(h + 1), lambda h: dil_turn(h), lambda h: dil_out(h),
                     lambda h: dil_turn(h + 1), lambda h: dil_out(h + 1)]
            for hp in range(4):
                for g in range(NG):
                    n, gi = N0["dq"] + 6 * hp + 2 * g, G0["dq"] + 3 * hp + g
                    first = (lambda hp=hp, g=g: steps[2 * g](2 * hp - 2)) if hp else None
                    pair_item(n, gi, 2, xtile, xs_wait("mix1") if hp == g == 0 else None, after_first=first)
                    if hp:
                        steps[2 * g + 1](2 * hp - 2)
            dil_last()
            eng.wait_ge(h_ready, hd + NH + 1)
            pair_phase("do", 8, 1, htile)
            mem_layer(1)
            for k in range(6):
                c, j = divmod(k, 2)
                g = G0["y"] + k
                eng.wait_ge(y_ready, 4 * j + 4)
                if k == 3:
                    statistics(STAT["final"], 0, 3)
                if k < 2:
                    item_free(g)
                elif k == 3:
                    eng.wait_ge(std_ready, STAT["final"])
                elif k > 3:
                    eng.wait_ge(y_out[k % 2], 1)
                rows, t0 = (P, c * P) if c < 2 else (TS, TP)
                for m in range(8):
                    last = nc.tensor.transpose((ab if c == 1 else acc)[0:rows, 2 * (g % 2) + m // 4, (m % 4) * P:(m % 4 + 1) * P],
                                               xg[:, 8 * j + m, t0:t0 + rows], ident[:, :])
                last.then_inc(turned, 1)

        @block.vector
        def _(eng):
            v = nc.vector
            at = [0]
            following = counter()

            def lo(n, more=0):
                landed(eng, n, more)
                eng.wait_ge(hi_ready, more + (n + 1))
                if n >= NSPLIT:
                    eng.wait_ge(half_used, more * 2 + 2 * (n - NSPLIT + 1))
                v.tensor_tensor(wlo[:, n % NSPLIT, :], raw[:, n % 2, :], whi[:, n % NSPLIT, :].bitcast(F32),
                                ALU.subtract).then_inc(lo_ready, 1)

            def upto(n):
                while at[0] <= min(n, NBLOCKS - 1):
                    lo(at[0])
                    at[0] += 1

            def block_used(n, more=0, half=2):
                eng.wait_ge(half_used, more * 2 + (2 * n + half))

            def banks(g, width=T):
                return acc[:, 2 * (g % 2):2 * (g % 2) + 2, 0:width]

            def columns(g):
                return acc[:, 2 * (g % 2):2 * (g % 2) + 2, :].rearrange("p b (s c) -> p (b s) c", c=P)

            def twice(ap):
                return ap.rearrange("p (o t) -> p o t", o=1).to_broadcast([P, 2, ap.shape[1]])

            def rms(k, width=T, cols=0, signal=None):
                eng.wait_ge(std_ready, k)
                if width:
                    v.reciprocal(R[:, 0:width], std[:, 0:width])
                if cols:
                    v.reciprocal(Rc[:, 0:2], stdc[:, 0:2])
                if cols == 3:
                    last = v.reciprocal(Rc[0:TS, 2:3], stdc[0:TS, 2:3])
                    if signal is not None:
                        last.then_inc(signal, 1)
                eng.drain()

            def split_x(gain, m0, width=T):
                def dst(m, part):
                    return xs[:, m, part, 0:width]
                for m in (m0, m0 + 1):
                    v.tensor_scalar(dst(m, 0), x[:, m, 0:width], gains[:, gain + m:gain + m + 1], None, ALU.mult)
                eng.drain()
                for m in (m0, m0 + 1):
                    v.scalar_tensor_tensor(out=dst(m, 1), in0=x[:, m, 0:width], scalar=gains[:, gain + m:gain + m + 1],
                                           in1=dst(m, 0).bitcast(F32), op0=ALU.mult, op1=ALU.subtract).then_inc(xs_ready, 1)

            def add_x(g, m0, gain=None):
                dst = x[:, m0:m0 + 2, :]
                v.tensor_tensor(dst, banks(g), dst, ALU.add).then_inc(acc_free, 1)
                eng.drain()
                if gain is not None:
                    split_x(gain, m0)
                else:
                    for m in (m0, m0 + 1):
                        c = GAIN["final"][0] + m
                        last = v.tensor_scalar(xg[:, m, :], x[:, m, :], gains[:, c:c + 1], None, ALU.mult)
                    last.then_inc(y_ready, 1)

            def split_h(h, t, src, tn=2):
                v.tensor_copy(h[:, t, 0, :], src)
                eng.drain()
                v.tensor_tensor(h[:, t, 1, :], src, h[:, t, 0, :].bitcast(F32), ALU.subtract).then_inc(h_ready, 1)

            def stage_item(g, k, rows, width=2 * 512):
                dst = (stage_u, stage2, stage_m, stage_u)[k]
                flat = acc[0:rows, 2 * (g % 2):2 * (g % 2) + 2, :].rearrange("p b c -> p (b c)")
                v.tensor_copy(dst[0:rows, 0:width], flat[:, 0:width]).then_inc(acc_free, 1)

            v.memset(ones[:, :], 1.0)
            v.memset(eps[:, :], EPS)
            v.memset(ab[:, :, :], 0.0).then_inc(zeros_ready, 1)
            for c in range(2):
                for j in range(2):
                    eng.wait_ge(turned, TURN0["memload"] + 2 * c + j + 1)
                    v.tensor_copy(x[:, 8 * j:8 * j + 8, c * P:(c + 1) * P], columns(G0["memload"] + 2 * c + j)).then_inc(acc_free, 1)
            eng.wait_ge(turned, TURN0["xload"] + 1)
            v.tensor_copy(gains[:, :], acc[:, 2 * (G0["xload"] % 2), 0:176]).then_inc(acc_free, 1)
            eng.drain()
            for m in range(0, DC, 2):
                split_x(GAIN["memkv"][0], m, TP)
                if m in (0, 6):
                    upto(m // 6)
            upto(3)
            rms(STAT["mem"], TP, 2)

            def memory_keys(l, ahead):
                for j in range(2):
                    block_used(N0[f"memk{l}"] + 2 * j + 1)
                    g = G0[f"memk{l}"] + j
                    v.tensor_tensor(mKT[:, l, 2 * j:2 * j + 2, :], banks(g, TP), twice(R[:, 0:TP]), ALU.mult).then_inc(acc_free, 1)
                    upto(ahead + 2 * j if l == 0 else ahead + 1)

            def memory_values(l):
                g = G0[f"memv{l}"]
                block_used(N0[f"memv{l}"] + 3)
                for c in range(2):
                    last = v.tensor_scalar(mV[:, l, c, :], acc[:, 2 * (g % 2) + c, :], Rc[:, c:c + 1], None, ALU.mult)
                last.then_inc(acc_free, 1)
                eng.wait_ge(turned, TURN0[f"memkt{l}"] + 1)
                stage_item(G0[f"memkt{l}"], l, P)

            memory_keys(0, N0["memv0"] + 1)
            upto(N0["memk1"] + 1)
            memory_values(0)
            upto(N0["memk1"] + 3)
            memory_keys(1, N0["memv1"])
            for c in range(3):
                for j in range(2 if c < 2 else 1):
                    g = G0["xt"] + 2 * c + j
                    eng.wait_ge(turned, TURN0["xt"] + 2 * c + j + 1)
                    if c < 2:
                        v.tensor_copy(x[:, 8 * j:8 * j + 8, c * P:(c + 1) * P], columns(g)).then_inc(acc_free, 1)
                    else:
                        v.tensor_copy(x[:, :, TP:T], acc[:, 2 * (g % 2), 0:P].rearrange("p (m b) -> p m b", b=TS)).then_inc(acc_free, 1)
            upto(N0["memv1"] + 2)
            for j in range(2):
                g = G0["st"] + j
                eng.wait_ge(turned, TURN0["st"] + j + 1)
                for q in range(2):
                    w = 2 << (2 * j + q)
                    rows = columns(g)[:, 4 * q:4 * q + 4, 0:TS * NST].rearrange("p s (b t) -> p s b t", t=NST)
                    last = v.tensor_reduce(wsum[:, 8 * j + 4 * q:8 * j + 4 * q + 4, :], rows[:, :, :, NST - (w - 1):NST],
                                           AX.X, ALU.add)
                last.then_inc(acc_free, 1)
            upto(N0["memv1"] + 3)
            for m in range(0, DC, 2):
                split_x(GAIN["mix"][0], m)
                if m in (4, 8):
                    upto(N0["win"] + m // 4 - 1)
            memory_values(1)

            v.memset(tmp[:, 0:6 * UP], 0.0)
            eng.drain()
            for j in range(8):
                n, g = N0["win"] + 2 * j, G0["win"] + j
                upto(n + 2)
                if j == 0:
                    eng.wait_ge(mask_in, 32)
                    rms(STAT["mix0"])
                if j == 4:
                    eng.wait_ge(stored[1], STORED[1])
                upto(n + 3)
                block_used(n + 1)
                gi = j // 2
                w = 2 << gi
                b = banks(g)
                v.tensor_tensor(U[:, :, 16:UP], b[:, :, 0:TP], twice(R[:, 0:TP]), ALU.mult)
                v.tensor_tensor(usm, b[:, :, TP:T], twice(R[:, TP:T]), ALU.mult).then_inc(acc_free, 1)
                eng.drain()
                v.tensor_copy(ut[:, 2 * j:2 * j + 2, 0:NST], U[:, :, UP - NST:UP])
                v.tensor_copy(ut[:, 2 * j:2 * j + 2, NST:NST + TS], usm)
                src, step = U, 1
                for i in range(gi + 1):
                    dst, first = (Ta, Tb)[i % 2], 2 * step - 1
                    v.tensor_tensor(dst[:, :, first:UP], src[:, :, first:UP], src[:, :, first - step:UP - step], ALU.add)
                    eng.drain()
                    src, step = dst, 2 * step
                for m in range(2):
                    v.tensor_tensor(src[:, m, 16:32], src[:, m, 16:32], invc[:, gi, :], ALU.mult)
                v.tensor_tensor(us2, usm, wsum[:, 2 * j:2 * j + 2, :], ALU.add)
                eng.drain()
                pooled = (Tb if src is Ta else Ta)[:, :, 0:T]
                v.scalar_tensor_tensor(out=pooled[:, :, 0:TP], in0=src[:, :, 16:UP], scalar=1.0 / w, in1=U[:, :, 16:UP],
                                       op0=ALU.mult, op1=ALU.subtract)
                v.scalar_tensor_tensor(out=pooled[:, :, TP:T], in0=us2, scalar=1.0 / w, in1=usm, op0=ALU.mult, op1=ALU.subtract)
                eng.drain()
                split_h(hA if j < 4 else hB, slice(2 * j % 8, 2 * j % 8 + 2), pooled)
                eng.drain()
            for gi in range(4):
                upto(N0["grp"] + gi + 2)
                for j in range(2):
                    block_used(N0["grp"] + gi)
                    eng.wait_ge(acc_free, G0["grp"] + 2 * gi + j + 1)
                    h, t = (hA, 4 * gi + 2 * j) if gi < 2 else (hB, 4 * gi + 2 * j - 8)
                    split_h(h, slice(t, t + 2), zF[:, j])
            eng.drain()
            eng.wait_ge(stored[0], STORED[0])
            for j in range(2):
                eng.wait_ge(turned, TURN0["ut"] + j + 1)
                stage_item(G0["ut"] + j, 2 + j, 23)
            for j in range(8):
                n = N0["wout"] + 2 * j
                upto(n + 3)
                block_used(n + 1)
                add_x(G0["wout"] + j, 2 * j, GAIN["memq"][0])

            def maxima(parts):
                for in_, c, ax in parts:
                    v.tensor_reduce(small[:, c + 8:c + 9], in_, ax, ALU.max)
                eng.drain()
                for i, (_, c, _) in enumerate(parts):
                    last = v.tensor_scalar(small[:, c:c + 1], small[:, c + 8:c + 9], -SCALE, None, ALU.mult)
                    if i == len(parts) - 1:
                        last.then_inc(nb_ready, 1)

            def inverses(c, n=2):
                following(eng, e_ready)
                v.reciprocal(small[:, c + 12:c + 12 + n], small[:, c + 4:c + 4 + n])
                eng.drain()

            def head_out(h, ready):
                v.tensor_copy(hA[:, h, 0, 0:TP], ab[:, 3, 0:TP])
                eng.drain()
                v.tensor_tensor(hA[:, h, 1, 0:TP], ab[:, 3, 0:TP], hA[:, h, 0, 0:TP].bitcast(F32), ALU.subtract).then_inc(h_ready, 1)

            def samples_out(bank, heads, q):
                src = ab[:, bank, 0:P].rearrange("p (m r) -> p r m", r=32)[:, 0:heads, :]
                dst = [hA[:, 0:heads, part, TP + 4 * q:TP + 4 * q + 4] for part in range(2)]
                v.tensor_copy(dst[0], src)
                eng.drain()
                return v.tensor_tensor(dst[1], src, dst[0].bitcast(F32), ALU.subtract)

            def mem_attention(l):
                g = G0[f"mq{l}"]
                n = N0[f"mq{l}"]
                mo = N0[f"mo{l}"]

                def queries(j):
                    block_used(n + 2 * j + 1)
                    v.tensor_tensor(qm[:, 2 * j:2 * j + 2, :], banks(g + j), twice(R[:, :]), ALU.mult).then_inc(acc_free, 1)

                def head_max(h):
                    following(eng, s_ready)
                    maxima([(ab[:, h % 2, q * TP:(q + 1) * TP], 2 * (h % 2) + q, AX.X) for q in range(2)])

                def head_probabilities(h):
                    s = h % 2
                    inverses(2 * s)
                    for q in range(2):
                        last = v.tensor_scalar(Pm[:, s, q, :], Pm[:, s, q, :], small[:, 12 + 2 * s + q:13 + 2 * s + q], None, ALU.mult)
                    last.then_inc(p_ready, 1)

                def head_turned():
                    following(eng, t_ready)
                    v.tensor_copy(PTm[:, :, :].rearrange("p k t -> p (k t)"), ab[:, 2, :]).then_inc(pt_ready, 1)

                def head_finish(h):
                    following(eng, o_ready)
                    head_out(h, None)

                def samples_max(q):
                    eng.wait_ge(scored, SC0[f"m{l}"] + 4 * q + 4)
                    maxima([(ab[:, q, 0:TP], 16 + q, AX.X)])

                def samples_probabilities(q):
                    inverses(16 + q, 1)
                    v.tensor_scalar(PsM[:, q, :], PsM[:, q, :], small[:, 28 + q:29 + q], None, ALU.mult).then_inc(p_ready, 1)

                def samples_turned(q):
                    following(eng, t_ready)
                    cols = ab[:, 2, 0:2 * P].rearrange("p (k m r) -> p k m r", k=2, r=32)
                    dst = PTzM.rearrange("p k b h c -> p k b (h c)")
                    for k in range(2):
                        last = v.tensor_copy(dst[:, k, 4 * q:4 * q + 4, 0:16:NH_MEM + 1], cols[:, k, :, 0:NH_MEM])
                    last.then_inc(pt_ready, 1)

                def samples_rows(q):
                    eng.wait_ge(v_used, VU0[f"m{l}"] + 4 * q + 4)
                    v.tensor_copy(Os[:, q, :], ab[:, (3, 0)[q], 0:P]).then_inc(os_ready, 1)

                eng.wait_ge(stored[0], STORED[2 if l == 0 else 4])
                eng.wait_ge(stored[1], STORED[3 if l == 0 else 5])
                upto(n + 2)
                rms(STAT[f"memq{l}"])
                upto(n + 3)
                queries(0)
                v.memset(QzM, 0.0)
                v.memset(PTzM, 0.0)
                head_max(0)
                head_max(1)
                head_probabilities(0)
                head_probabilities(1)
                upto(mo + 1)
                head_turned()
                queries(1)
                eng.drain()
                v.tensor_copy(QzM.rearrange("p b h c -> p (h c) b")[:, 0:16:NH_MEM + 1, :], qm[:, :, TP:T])
                head_finish(0)
                head_turned()
                head_max(2)
                head_max(3)
                head_finish(1)
                head_probabilities(2)
                head_probabilities(3)
                upto(mo + 2)
                head_turned()
                head_finish(2)
                head_turned()
                head_finish(3)
                upto(mo + 3)
                samples_max(0)
                samples_probabilities(0)
                samples_turned(0)
                samples_max(1)
                samples_probabilities(1)
                samples_turned(1)
                samples_rows(0)
                following(eng, t_ready)
                samples_out(1, NH_MEM, 0)
                samples_rows(1)
                following(eng, t_ready)
                samples_out(2, NH_MEM, 1).then_inc(h_ready, 1)
                eng.drain()

            def mem_layer(l):
                mem_attention(l)
                for i in range(4):
                    upto(N0[f"mo{l}"] + i + 2)
                    for j in range(2):
                        block_used(N0[f"mo{l}"] + i, half=1 + j)
                        add_x(G0[f"mo{l}"] + 2 * i + j, 4 * i + 2 * j, GAIN["ffn"][l])

            def ffn(l, gain):
                for part in range(3):
                    n, g, turns = N0[f"f{l}g{part}"], G0[f"f{l}g{part}"], PARTS[part] // 2
                    e0 = 22 * l + sum(PARTS[:part]) // 2

                    def turn(i, h, t):
                        first = part == 0 and isinstance(i, int)
                        lo(n + 2, 4 * i)
                        if first:
                            rms(STAT[f"ffn{l}"])
                        lo(n + 3, 4 * i)
                        block_used(n + 1, 4 * i)
                        v.tensor_tensor(gateF, banks(g), twice(R[:, :]), ALU.mult).then_inc(acc_free, 1)
                        lo(n + 4, 4 * i)
                        lo(n + 5, 4 * i)
                        eng.wait_ge(silu_ready, 1 * i + (e0 + 1))
                        v.tensor_tensor(siluF, siluF, twice(R[:, :]), ALU.mult)
                        eng.drain()
                        block_used(n + 3, 4 * i)
                        v.tensor_tensor(upF, banks(g + 1), siluF, ALU.mult).then_inc(acc_free, 1)
                        eng.drain()
                        split_h(h, t, upF)
                        eng.drain()

                    upto(n + 1)
                    first = 0
                    if part == 0:
                        turn(0, hA, slice(0, 2))
                        first = 1
                    with eng.Fori(first, 4) as i:
                        turn(i, hA, bass.ds(2 * i, 2))
                    with eng.Fori(4, turns) as i:
                        turn(i, hB, bass.ds(2 * i - 8, 2))
                    if part < 2:
                        nd, gd = N0[f"f{l}d{part}"], G0[f"f{l}d{part}"]
                        with eng.Fori(0, 4) as i:
                            for j in range(2):
                                lo(nd + 2 * j + 2, 4 * i)
                                lo(nd + 2 * j + 3, 4 * i)
                                block_used(nd + 2 * j + 1, 4 * i)
                                dst = x[:, bass.ds(4 * i + 2 * j, 2), :]
                                v.tensor_tensor(dst, banks(gd + j), dst, ALU.add).then_inc(acc_free, 1)
                        eng.drain()
                        at[0] = nd + 18
                    else:
                        at[0] = n + 4 * turns + 2
                        nd = N0[f"f{l}d2"]
                        for q in range(4):
                            upto(nd + 3 * q + 4)
                            for j in range(2):
                                block_used(nd + 3 * q + 2, half=1 + j)
                                add_x(G0[f"f{l}d2"] + 2 * q + j, 4 * q + 2 * j, gain)

            mem_layer(0)
            ffn(0, GAIN["kv"][0])

            n = N0["ksh"]
            for j in range(2):
                upto(n + 2 * j + 2)
                if j == 0:
                    rms(STAT["kv"], T, 3)
                upto(n + 2 * j + 3)
                block_used(n + 2 * j + 1)
                v.tensor_tensor(KT[:, 2 * j:2 * j + 2, :], banks(G0["ksh"] + j), twice(R[:, :]), ALU.mult).then_inc(acc_free, 1)
            v.memset(Vrep, 0.0)
            upto(N0["dq"] + 1)
            block_used(N0["vsh"] + 3)
            g = G0["vsh"]
            for c in range(2):
                last = v.tensor_scalar(V[:, c, :], acc[:, 2 * (g % 2) + c, :], Rc[:, c:c + 1], None, ALU.mult)
            last.then_inc(acc_free, 1)
            v.tensor_scalar(Vsm, acc[0:TS, 2 * ((g + 1) % 2), :], Rc[0:TS, 2:3], None, ALU.mult).then_inc(acc_free, 1)
            for m in range(0, DC, 2):
                split_x(GAIN["mix"][1], m)
            eng.wait_ge(stored[0], STORED[4])
            eng.wait_ge(stored[1], STORED[5])
            eng.wait_ge(vs_done, 16)
            v.memset(QzD, 0.0)
            eng.drain()

            def dil_max(h):
                following(eng, s_ready)
                S1 = S[:, 0:768].rearrange("p (g j) -> p g j", g=NG)
                S0 = S[:, 768:1152].rearrange("p (g j) -> p g j", g=NG)
                v.tensor_tensor(S1, ab[:, 0:2, :].rearrange("p b (g j) -> p (b g) j", j=TP)[:, 0:NG, :], mask[:, :, :], ALU.add)
                v.tensor_tensor(S0, ab[:, 2, 0:384].rearrange("p (g j) -> p g j", g=NG), mask[:, :, P:2 * P], ALU.add).then_inc(s_free, 1)
                eng.drain()
                maxima([(S[:, 0:768], 0, AX.X), (S[:, 768:1152], 1, AX.X)])

            def dil_probabilities():
                inverses(0)
                for (c, w, o_) in ((0, TP, 0), (768, P, TP)):
                    v.tensor_tensor(Pn[:, o_:o_ + w], S[:, c:c + w], S[:, c + w:c + 2 * w], ALU.add)
                eng.drain()
                for (c, w, o_) in ((0, TP, 0), (768, P, TP)):
                    v.tensor_tensor(Pn[:, o_:o_ + w], Pn[:, o_:o_ + w], S[:, c + 2 * w:c + 3 * w], ALU.add)
                eng.drain()
                for i, (w, o_) in enumerate(((TP, 0), (P, TP))):
                    last = v.tensor_scalar(Pn[:, o_:o_ + w], Pn[:, o_:o_ + w], small[:, 12 + i:13 + i], None, ALU.mult)
                last.then_inc(p_ready, 1)

            def dil_turned():
                following(eng, t_ready)
                v.tensor_copy(PT[:, :], ab[:, 3, 0:384]).then_inc(pt_ready, 1)

            def dil_finish(h):
                following(eng, o_ready)
                head_out(h, None)

            steps = [lambda h: (dil_max(h), dil_probabilities()), lambda h: None,
                     lambda h: (dil_turned(), dil_max(h + 1), dil_probabilities()), lambda h: dil_finish(h), lambda h: dil_turned(), lambda h: dil_finish(h + 1)]
            for hp in range(4):
                for j in range(6):
                    n, g = N0["dq"] + 6 * hp + j, G0["dq"] + 3 * hp + j // 2
                    upto(n + 2)
                    if j % 2:
                        block_used(n)
                        dst = qd[:, hp % 2, j // 2]
                        v.tensor_tensor(dst, banks(g), twice(R[:, :]), ALU.mult).then_inc(acc_free, 1)
                        eng.drain()
                        v.tensor_copy(QzD[:, j // 2, :, hp, 2 * hp:2 * hp + 2], dst[:, :, TP:T].rearrange("p h b -> p b h"))
                    if hp:
                        steps[j](2 * hp - 2)
            def dil_samples_max(q):
                eng.wait_ge(scored, SC0["dil"] + 4 * q + 4)
                maxima([(ab[:, q, 0:387], 16 + q, AX.X)])

            def dil_samples_probabilities(q):
                inverses(16 + q, 1)
                v.tensor_scalar(PsDf[:, q, :], PsDf[:, q, :], small[:, 28 + q:29 + q], None, ALU.mult).then_inc(p_ready, 1)
                eng.drain()
                v.tensor_reduce(small[:, 8 + q:9 + q], PsD[:, q, :, P], AX.X, ALU.add)

            def dil_samples_turned(q):
                following(eng, t_ready)
                cols = ab[:, 2, 0:3 * P].rearrange("p (g m r) -> p g m r", g=NG, r=32)
                dst = PTzD.rearrange("p g b k h -> p g b (k h)")
                for c in range(2):
                    last = v.tensor_copy(dst[:, :, 4 * q:4 * q + 4, c::NH + 2], cols[:, :, :, c:NH:2])
                last.then_inc(pt_ready, 1)

            def dil_samples_rows(q):
                eng.wait_ge(v_used, VU0["dil"] + 4 * q + 4)
                v.scalar_tensor_tensor(out=Os[:, q, :], in0=Vrep[:, q, :], scalar=small[:, 8 + q:9 + q],
                                       in1=ab[:, (3, 0)[q], 0:P], op0=ALU.mult, op1=ALU.add).then_inc(os_ready, 1)

            dil_max(6)
            dil_probabilities()
            upto(N0["do"] + 2)
            dil_turned()
            dil_max(7)
            dil_finish(6)
            dil_probabilities()
            upto(N0["do"] + 3)
            dil_turned()
            dil_finish(7)
            v.memset(PTzD, 0.0)
            eng.drain()
            dil_samples_max(0)
            dil_samples_probabilities(0)
            dil_samples_turned(0)
            dil_samples_max(1)
            dil_samples_probabilities(1)
            dil_samples_turned(1)
            eng.wait_ge(vrep_in, 16 * TS)
            dil_samples_rows(0)
            following(eng, t_ready)
            samples_out(1, NH, 0)
            dil_samples_rows(1)
            following(eng, t_ready)
            samples_out(2, NH, 1).then_inc(h_ready, 1)
            eng.drain()
            for j in range(8):
                n = N0["do"] + j
                upto(n + 2)
                block_used(n)
                add_x(G0["do"] + j, 2 * j, GAIN["memq"][1])
            mem_layer(1)
            ffn(1, None)

            rms(STAT["final"], 0, 3, rms_ready)
            for k in range(0, 6, 2):
                eng.wait_ge(turned, TURN0["y"] + k + 1)
                rows, dst, src, r = output_item(k)
                v.tensor_scalar(dst, src, r, None, ALU.mult).then_inc(y_out[0], 1)

        @block.gpsimd
        def _(eng):
            gp = nc.gpsimd

            def squares(done, width=T):
                for j in range(8):
                    done(j)
                    src = x[:, 2 * j:2 * j + 2, 0:width]
                    gp.tensor_tensor((sq if j else ssq)[:, :, 0:width], src, src, ALU.mult)
                    eng.drain()
                    if j:
                        last = gp.tensor_tensor(ssq[:, :, 0:width], ssq[:, :, 0:width], sq[:, :, 0:width], ALU.add)
                        if j == 7:
                            last.then_inc(ssq_ready, 1)
                        eng.drain()

            def taken(g):
                eng.wait_ge(acc_free, g + 1)

            def by_item(g):
                return lambda j: taken(g + j)

            def load_memory_rows(l):
                eng.wait_ge(half_used, 2 * N0[f"mq{l}"])
                load_cached(eng, (f"mk{l}", 0))
                eng.wait_ge(half_used, 2 * (N0[f"mq{l}"] + 4))
                for i in range(1, 4):
                    load_cached(eng, (f"mk{l}", i))
                load_cached(eng, (f"mv{l}", 0))
                for i in range(1, 4):
                    eng.wait_ge(turned, TURN0[f"mk{l}"] + 2 * i)
                    load_cached(eng, (f"mv{l}", i))

            later = [(key, s) for key, s in CACHED if key[0][0] == "d" and key != ("dk", 0)]

            squares(lambda j: taken(G0["memload"] + 3), TP)
            taken(G0["xload"])
            for m in range(0, DC, 2):
                h, k, c = (hA, hB)[m // 8], m % 8, GAIN["memkv"][1] + m
                gain = gains[:, c:c + 2].rearrange("p (m o) -> p m o", o=1).to_broadcast([P, 2, TP])
                gp.tensor_tensor(sq[:, :, 0:TP], x[:, m:m + 2, 0:TP], gain, ALU.mult)
                eng.drain()
                eng.wait_ge(high_ready, m + 2)
                gp.tensor_tensor(h[:, k:k + 2, 1, 0:TP], sq[:, :, 0:TP], h[:, k:k + 2, 0, 0:TP].bitcast(F32),
                                 ALU.subtract).then_inc(low_ready, 1)
                eng.drain()
            load_cached(eng, ("x", 0))
            load_cached(eng, ("x", 1))
            eng.wait_ge(half_used, 2 * N0["memk1"])
            for key in (("x", 2), ("state", 0)):
                load_cached(eng, key)
            squares(lambda j: taken(G0["xt"] + 4))
            eng.dma_start(mem_v_p[0, 0].rearrange("(c p) h d -> p c (h d)", p=P), mV[:, 0, :, :]).then_inc(out_done, 16)
            eng.dma_start(mem_k_p[0, 0].rearrange("(c p) h d -> p c (h d)", p=P),
                          stage_u.rearrange("p (c k) -> p c k", c=2)).then_inc(stored[0], 16)
            taken(G0["memkt1"])
            eng.dma_start(mem_v_p[1, 0].rearrange("(c p) h d -> p c (h d)", p=P), mV[:, 1, :, :]).then_inc(out_done, 16)
            eng.dma_start(mem_k_p[1, 0].rearrange("(c p) h d -> p c (h d)", p=P),
                          stage2.rearrange("p (c k) -> p c k", c=2)).then_inc(stored[1], 16)
            for j in range(2):
                taken(G0["ut"] + j)
                src, cols = (stage_m, stage_u)[j], slice(1024 * j, 1024 * (j + 1))
                eng.dma_start(pool_p[0, 0, :, cols], src[0:NST, :]).then_inc(stored[j], 16)
                eng.dma_start(pool_s[0, :, NST - 1, cols], src[NST:NST + TS, :]).then_inc(stored[j], 16)
            eng.dma_start(pool_s[0, :, 0:NST - 1, :], a["state_pool"][0, :, 1:NST, :]).then_inc(out_done, 16)
            squares(by_item(G0["wout"]))
            load_memory_rows(0)
            squares(by_item(G0["mo0"]))
            squares(by_item(G0["f0d2"]))
            taken(G0["vsh"] + 1)
            eng.dma_start(v_s.rearrange("b t h d -> (b t) (h d)"), Vsm).then_inc(vs_done, 16)
            eng.dma_start(wv_p[0].rearrange("(c p) h d -> p c (h d)", p=P), V[:, :, :]).then_inc(out_done, 16)
            taken(G0["kt"])
            eng.dma_start(wk_p[0].rearrange("(c p) h d -> p c (h d)", p=P),
                          stage.rearrange("p (c k) -> p c k", c=2)).then_inc(stored[0], 16)
            taken(G0["kt"] + 1)
            eng.dma_start(k_s.rearrange("b t h d -> (b t) (h d)"), stage2[0:TS, 0:MEMD]).then_inc(stored[1], 16)
            load_cached(eng, ("dk", 0))
            eng.wait_ge(vs_done, 16)
            for b in range(TS):
                r = 32 * (b % 4)
                dst = Vrep[r:r + NH, b // 4, :]
                src = v_s[b, 0].rearrange("k (o d) -> k o d", o=1).to_broadcast([KVH, 2, P])
                eng.dma_start(dst, src).then_inc(vrep_in, 16)
            eng.wait_ge(half_used, 2 * N0["do"])
            for i, (key, _) in enumerate(later):
                if i >= 5:
                    kind, b = later[i - 5][0]
                    if kind == "dk":
                        eng.wait_ge(turned, TURN0["dk"] + 2 * (b + 1))
                    else:
                        eng.wait_ge(v_used, VU0["dil"] + b + 1)
                load_cached(eng, key)
            squares(by_item(G0["do"]))
            load_memory_rows(1)
            squares(by_item(G0["mo1"]))
            squares(by_item(G0["f1d2"]))
            eng.wait_ge(out_done, 16 * 4)
            eng.wait_ge(stored[0], STORED[4])
            eng.wait_ge(stored[1], STORED[5])
            eng.wait_ge(vs_done, 16)


_INS = ["x_prompt", "x_sample", "mem_prompt", "state_pool", "cache_win_k", "cache_win_v", "cache_mem_k", "cache_mem_v",
        "norm_mix", "norm_mem_q", "norm_mem_kv", "norm_ffn", "pool_w_in", "pool_w_group", "pool_scale", "pool_w_out",
        "norm_kv", "w_k_shared", "w_v_shared", "dil_w_q", "dil_w_o", "mem_w_q", "mem_w_k", "mem_w_v", "mem_w_o",
        "ffn_w_gate", "ffn_w_up", "ffn_w_down", "norm_final"]
_OUTS = [(1, TP, D), (TS, 1, D), (1, 1, NST, D), (1, TS, NST, D), (1, TP, KVH, P), (1, TP, KVH, P), (TS, 1, KVH, P),
         (TS, 1, KVH, P), (2, 1, TP, NH_MEM, P), (2, 1, TP, NH_MEM, P)]


def _shape_constants():
    q = np.arange(P)[:, None] + P
    j = np.arange(2 * P)[None, :]
    mask = np.stack([np.where((q - j >= 0) & ((q - j) % d == 0) & ((q - j) // d <= WIN_KEYS), 0.0, MASKED) for d in DILS], 1)
    t = np.arange(16)
    inv = np.stack([w / np.minimum(t + 1, w) for w in (2, 4, 8, 16)])
    return {"c_ident": np.eye(P, dtype=np.float32), "c_mask": mask.astype(np.float32),
            "c_inv": np.broadcast_to(inv[None], (P, 4, 16)).astype(np.float32)}


def kernel(**inputs):
    import concourse.bacc as bacc
    from concourse.bass_utils import run_bass_kernel_spmd

    nc = bacc.Bacc("TRN2", target_bir_lowering=False, num_devices=1)
    arrays, aps = {}, {}
    given = {n: np.ascontiguousarray(inputs[n]) for n in _INS}
    given.update(_shape_constants())
    for name, v in given.items():
        arrays[f"in_{name}"] = v
        aps[name] = nc.dram_tensor(f"in_{name}", v.shape, F32, kind="ExternalInput").ap()
    outs = [nc.dram_tensor(f"out_{i}", s, F32, kind="ExternalOutput").ap() for i, s in enumerate(_OUTS)]
    trunk(nc, aps, outs)
    r = run_bass_kernel_spmd(nc, [arrays], core_ids=[0])
    return tuple(r.results[0][f"out_{i}"] for i in range(len(_OUTS)))
```
